# Optimizing a Trainium2 kernel written in Bass

```python
import math
import jax, jax.numpy as jnp
from jax import lax
import numpy as np

D_MODEL = 1024
BATCH = 1
SEQ = 512
DEPTH = 1

CHUNK = 64
D_SSM = D_MODEL // 2
SSM_GROUP = 16
N_GROUPS = D_SSM // SSM_GROUP
STATE = 64
N_HEADS = 8
HEAD_DIM = 64
D_ATTN = N_HEADS * HEAD_DIM
D_IN = D_SSM + 3 * D_ATTN
D_FF = 4 * D_MODEL
Q_BLOCK = 128
EPS = 1e-6
DT_MIN = 1e-3
DT_MAX = 1e-1


def rmsnorm(x, g):
    xf = x.astype(jnp.float32)
    y = xf * lax.rsqrt(jnp.mean(xf * xf, axis=-1, keepdims=True) + EPS)
    return (y * g.astype(jnp.float32)).astype(x.dtype)

def s5_branch(u, A_re, A_im, log_dt, B_re, B_im, C_re, C_im, D_skip, w_glu, b_glu):
    f32 = jnp.float32
    bsz, seq, _ = u.shape
    uf = u.astype(f32)
    ug = uf.reshape(bsz, seq, N_GROUPS, SSM_GROUP)
    lam = lax.complex(A_re.astype(f32), A_im.astype(f32))
    dt = jnp.exp(log_dt.astype(f32))[:, None]
    a_bar = jnp.exp(lam * dt)
    b_bar = ((a_bar - 1.0) / lam)[..., None] * lax.complex(B_re.astype(f32), B_im.astype(f32))
    bu = lax.complex(jnp.einsum('bsgc,gpc->bsgp', ug, b_bar.real),
                     jnp.einsum('bsgc,gpc->bsgp', ug, b_bar.imag))
    a = jnp.broadcast_to(a_bar, (1, seq, N_GROUPS, STATE))

    def combine(left, right):
        a_l, b_l = left
        a_r, b_r = right
        return a_r * a_l, a_r * b_l + b_r

    _, states = lax.associative_scan(combine, (a, bu), axis=1)
    y = (jnp.einsum('bsgp,gcp->bsgc', states.real, C_re.astype(f32))
         - jnp.einsum('bsgp,gcp->bsgc', states.imag, C_im.astype(f32)))
    y = y.reshape(bsz, seq, D_SSM) + D_skip.astype(f32) * uf
    y = jax.nn.gelu(y)
    y = y * jax.nn.sigmoid(y @ w_glu.astype(f32) + b_glu.astype(f32))
    return y.astype(u.dtype)

def stick_breaking_attention(q, k, v):
    f32 = jnp.float32
    bsz, seq, nh, dh = q.shape
    nb = seq // Q_BLOCK
    qb = q.astype(f32).reshape(bsz, nb, Q_BLOCK, nh, dh).transpose(1, 0, 2, 3, 4)
    kf = k.astype(f32)
    vf = v.astype(f32)
    key_pos = jnp.arange(seq)
    scale = HEAD_DIM ** -0.5

    def one_block(args):
        blk, q_blk = args
        q_pos = blk * Q_BLOCK + jnp.arange(Q_BLOCK)
        z = jnp.einsum('bqhd,bkhd->bhqk', q_blk, kf) * scale
        mask = key_pos[None, :] < q_pos[:, None]
        log_fail = jnp.where(mask, jax.nn.log_sigmoid(-z), 0.0)
        after = lax.cumsum(log_fail, axis=3, reverse=True) - log_fail
        log_w = jax.nn.log_sigmoid(z) + after
        w = jnp.where(mask, jnp.exp(log_w), 0.0)
        return jnp.einsum('bhqk,bkhd->bqhd', w, vf)

    out = lax.map(one_block, (jnp.arange(nb), qb))
    return out.transpose(1, 0, 2, 3, 4).reshape(bsz, seq, nh * dh).astype(q.dtype)

def first_inputs(seed: int = 0) -> dict:
    key = jax.random.key(seed)
    ks = jax.random.split(key, 22)
    f32 = jnp.float32

    def nrm(k, shape, scale):
        return jax.random.normal(k, shape, f32) * scale

    x = nrm(ks[0], (BATCH, SEQ, D_MODEL), 1.0)
    norm_mix = 1.0 + nrm(ks[1], (DEPTH, D_MODEL), 0.02)
    w_in = nrm(ks[2], (DEPTH, D_MODEL, D_IN), D_MODEL ** -0.5)
    A_re = -0.5 + nrm(ks[3], (DEPTH, N_GROUPS, STATE), 0.01)
    A_im = jnp.pi * jnp.arange(STATE, dtype=f32) + nrm(ks[4], (DEPTH, N_GROUPS, STATE), 0.01)
    log_dt = jax.random.uniform(ks[5], (DEPTH, N_GROUPS), f32, math.log(DT_MIN), math.log(DT_MAX))
    B_re = nrm(ks[6], (DEPTH, N_GROUPS, STATE, SSM_GROUP), (2 * SSM_GROUP) ** -0.5)
    B_im = nrm(ks[7], (DEPTH, N_GROUPS, STATE, SSM_GROUP), (2 * SSM_GROUP) ** -0.5)
    C_re = nrm(ks[8], (DEPTH, N_GROUPS, SSM_GROUP, STATE), STATE ** -0.5)
    C_im = nrm(ks[9], (DEPTH, N_GROUPS, SSM_GROUP, STATE), STATE ** -0.5)
    D_skip = nrm(ks[10], (DEPTH, D_SSM), 1.0)
    w_glu = nrm(ks[11], (DEPTH, D_SSM, D_SSM), D_SSM ** -0.5)
    b_glu = nrm(ks[12], (DEPTH, D_SSM), 0.02)
    w_up_ssm = nrm(ks[13], (DEPTH, D_SSM, D_MODEL), D_SSM ** -0.5)
    w_up_attn = nrm(ks[14], (DEPTH, D_ATTN, D_MODEL), D_ATTN ** -0.5)
    w_gate = nrm(ks[15], (DEPTH, D_MODEL, 2 * D_MODEL), D_MODEL ** -0.5)
    b_gate = nrm(ks[16], (DEPTH, 2 * D_MODEL), 0.02)
    w_out = nrm(ks[17], (DEPTH, D_MODEL, D_MODEL), D_MODEL ** -0.5)
    norm_mlp = 1.0 + nrm(ks[18], (DEPTH, D_MODEL), 0.02)
    w_ff1 = nrm(ks[19], (DEPTH, D_MODEL, D_FF), D_MODEL ** -0.5)
    w_ff2 = nrm(ks[20], (DEPTH, D_FF, D_MODEL), D_FF ** -0.5)
    norm_final = 1.0 + nrm(ks[21], (D_MODEL,), 0.02)
    return {"x": x, "norm_mix": norm_mix, "w_in": w_in, "A_re": A_re, "A_im": A_im,
            "log_dt": log_dt, "B_re": B_re, "B_im": B_im, "C_re": C_re, "C_im": C_im,
            "D_skip": D_skip, "w_glu": w_glu, "b_glu": b_glu, "w_up_ssm": w_up_ssm,
            "w_up_attn": w_up_attn, "w_gate": w_gate, "b_gate": b_gate, "w_out": w_out,
            "norm_mlp": norm_mlp, "w_ff1": w_ff1, "w_ff2": w_ff2, "norm_final": norm_final}

def first_block(x, norm_mix, w_in, A_re, A_im, log_dt, B_re, B_im, C_re, C_im, D_skip, w_glu, b_glu,
              w_up_ssm, w_up_attn, w_gate, b_gate, w_out, norm_mlp, w_ff1, w_ff2, norm_final):
    h = x
    bsz, seq, _ = x.shape
    for l in range(DEPTH):
        u = rmsnorm(h, norm_mix[l])
        proj = u @ w_in[l]
        u_ssm, q, k, v = jnp.split(proj, [D_SSM, D_SSM + D_ATTN, D_SSM + 2 * D_ATTN], axis=-1)
        y_ssm = s5_branch(u_ssm, A_re[l], A_im[l], log_dt[l], B_re[l], B_im[l], C_re[l], C_im[l],
                          D_skip[l], w_glu[l], b_glu[l])
        y_attn = stick_breaking_attention(q.reshape(bsz, seq, N_HEADS, HEAD_DIM),
                                          k.reshape(bsz, seq, N_HEADS, HEAD_DIM),
                                          v.reshape(bsz, seq, N_HEADS, HEAD_DIM))
        gates = jax.nn.sigmoid((u @ w_gate[l] + b_gate[l]).astype(jnp.float32)).astype(u.dtype)
        g_ssm, g_attn = jnp.split(gates, 2, axis=-1)
        merged = g_ssm * (y_ssm @ w_up_ssm[l]) + g_attn * (y_attn @ w_up_attn[l])
        h = h + merged @ w_out[l]
        hid = jax.nn.relu(rmsnorm(h, norm_mlp[l]) @ w_ff1[l])
        h = h + (hid * hid) @ w_ff2[l]
    return rmsnorm(h, norm_final)


DEPTH_2 = 2

PLE_DIM = 256
N_MIXERS = 2

GLA_HEADS = 4
GLA_KEY_DIM = D_MODEL // 2
GLA_VAL_DIM = D_MODEL
GLA_DK = GLA_KEY_DIM // GLA_HEADS
GLA_DV = GLA_VAL_DIM // GLA_HEADS
GLA_GATE_RANK = 16
GLA_GATE_NORMALIZER = 16.0
GLA_CHUNK = 64
GLA_IN = 2 * GLA_KEY_DIM + 2 * GLA_VAL_DIM + GLA_GATE_RANK

FOX_HEADS = 16
FOX_WIDTH = D_MODEL
FOX_HD = FOX_WIDTH // FOX_HEADS
FOX_BLOCK = 128
FOX_IN = 4 * FOX_WIDTH + FOX_HEADS

N_GLA = (DEPTH_2 + 1) // 2
N_FOX = DEPTH_2 // 2


def rms_norm(x, g):
    xf = x.astype(jnp.float32)
    y = xf * lax.rsqrt(jnp.mean(xf * xf, axis=-1, keepdims=True) + EPS)
    return (y * g.astype(jnp.float32)).astype(x.dtype)

def to_heads(t, n_heads):
    b, s, w = t.shape
    return t.reshape(b, s, n_heads, w // n_heads).transpose(0, 2, 1, 3)

def gla_chunked(q, k, v, log_a):
    b_, h_, s_, dk = q.shape
    dv = v.shape[-1]
    n = s_ // GLA_CHUNK
    q = q.reshape(b_, h_, n, GLA_CHUNK, dk)
    k = k.reshape(b_, h_, n, GLA_CHUNK, dk)
    v = v.reshape(b_, h_, n, GLA_CHUNK, dv)
    cum = jnp.cumsum(log_a.reshape(b_, h_, n, GLA_CHUNK, dk), axis=3)
    q_in = q * jnp.exp(cum)
    k_in = k * jnp.exp(-cum)
    causal = jnp.tril(jnp.ones((GLA_CHUNK, GLA_CHUNK), dtype=bool))
    attn = jnp.where(causal, jnp.einsum('bhncd,bhnjd->bhncj', q_in, k_in), 0.0)
    o_intra = jnp.einsum('bhncj,bhnjv->bhncv', attn, v)
    cum_last = cum[:, :, :, -1:, :]
    k_dec = k * jnp.exp(cum_last - cum)
    decay_chunk = jnp.exp(cum_last[:, :, :, 0, :])

    def step(state, inp):
        k_n, v_n, d_n = inp
        new_state = state * d_n[..., None] + jnp.einsum('bhcd,bhcv->bhdv', k_n, v_n)
        return new_state, state

    xs = (jnp.moveaxis(k_dec, 2, 0), jnp.moveaxis(v, 2, 0), jnp.moveaxis(decay_chunk, 2, 0))
    init = jnp.zeros((b_, h_, dk, dv), jnp.float32)
    _, states = lax.scan(step, init, xs)
    o_inter = jnp.einsum('bhncd,nbhdv->bhncv', q_in, states)
    return (o_intra + o_inter).reshape(b_, h_, s_, dv)

def gla_mixer(h, w_in, w_a2, b_a, o_gain, w_out):
    b_, s_, _ = h.shape
    proj = h @ w_in
    q, k, v, g, a_lr = jnp.split(
        proj, [GLA_KEY_DIM, 2 * GLA_KEY_DIM, 2 * GLA_KEY_DIM + GLA_VAL_DIM, 2 * GLA_KEY_DIM + 2 * GLA_VAL_DIM], axis=-1)
    log_a = jax.nn.log_sigmoid((a_lr @ w_a2).astype(jnp.float32) + b_a.astype(jnp.float32)) / GLA_GATE_NORMALIZER
    qh = to_heads(q, GLA_HEADS).astype(jnp.float32) * (GLA_DK ** -0.5)
    kh = to_heads(k, GLA_HEADS).astype(jnp.float32)
    vh = to_heads(v, GLA_HEADS).astype(jnp.float32)
    ah = to_heads(log_a, GLA_HEADS)
    o = gla_chunked(qh, kh, vh, ah).astype(h.dtype)
    o = rms_norm(o.transpose(0, 2, 1, 3), o_gain).reshape(b_, s_, GLA_VAL_DIM)
    return (o * jax.nn.silu(g)) @ w_out

def fox_attention(q, k, v, log_f):
    b_, h_, s_, d = q.shape
    nq = s_ // FOX_BLOCK
    c = jnp.cumsum(log_f, axis=-1)
    q_blocks = jnp.moveaxis(q.reshape(b_, h_, nq, FOX_BLOCK, d), 2, 0)
    c_blocks = jnp.moveaxis(c.reshape(b_, h_, nq, FOX_BLOCK), 2, 0)
    starts = jnp.arange(nq, dtype=jnp.int32) * FOX_BLOCK
    key_pos = jnp.arange(s_, dtype=jnp.int32)
    scale = FOX_HD ** -0.5

    def block(args):
        qb, cb, start = args
        q_pos = start + jnp.arange(FOX_BLOCK, dtype=jnp.int32)
        logits = (jnp.einsum('bhqd,bhkd->bhqk', qb, k).astype(jnp.float32) * scale
                  + cb[..., :, None] - c[..., None, :])
        mask = key_pos[None, :] <= q_pos[:, None]
        probs = jax.nn.softmax(jnp.where(mask, logits, -jnp.inf), axis=-1)
        return jnp.einsum('bhqk,bhkd->bhqd', probs.astype(v.dtype), v)

    out = lax.map(block, (q_blocks, c_blocks, starts))
    return jnp.moveaxis(out, 0, 2).reshape(b_, h_, s_, d)

def fox_mixer(h, w_in, b_f, q_gain, k_gain, w_out):
    b_, s_, _ = h.shape
    proj = h @ w_in
    q, k, v, g, f_logit = jnp.split(proj, [FOX_WIDTH, 2 * FOX_WIDTH, 3 * FOX_WIDTH, 4 * FOX_WIDTH], axis=-1)
    log_f = jax.nn.log_sigmoid(f_logit.astype(jnp.float32) + b_f.astype(jnp.float32))
    qh = rms_norm(to_heads(q, FOX_HEADS), q_gain)
    kh = rms_norm(to_heads(k, FOX_HEADS), k_gain)
    vh = to_heads(v, FOX_HEADS)
    o = fox_attention(qh, kh, vh, log_f.transpose(0, 2, 1))
    o = o.transpose(0, 2, 1, 3).reshape(b_, s_, FOX_WIDTH)
    return (o * jax.nn.silu(g)) @ w_out

def second_inputs(seed: int = 0) -> dict:
    key = jax.random.key(seed)
    ks = jax.random.split(key, 20)
    f32 = jnp.float32
    nrm = lambda k, shape, fan_in: jax.random.normal(k, shape, f32) * (fan_in ** -0.5)
    gain = lambda k, shape: 1.0 + 0.02 * jax.random.normal(k, shape, f32)
    return {
        "x": jax.random.normal(ks[0], (BATCH, SEQ, D_MODEL), f32),
        "p": jax.random.normal(ks[1], (DEPTH_2, BATCH, SEQ, PLE_DIM), f32),
        "norm_mixer": gain(ks[2], (DEPTH_2, D_MODEL)),
        "gla_w_in": nrm(ks[3], (N_GLA, D_MODEL, GLA_IN), D_MODEL),
        "gla_w_a2": nrm(ks[4], (N_GLA, GLA_GATE_RANK, GLA_KEY_DIM), GLA_GATE_RANK),
        "gla_b_a": 0.1 * jax.random.normal(ks[5], (N_GLA, GLA_KEY_DIM), f32),
        "gla_o_norm": gain(ks[6], (N_GLA, GLA_DV)),
        "gla_w_out": nrm(ks[7], (N_GLA, GLA_VAL_DIM, D_MODEL), GLA_VAL_DIM),
        "fox_w_in": nrm(ks[8], (N_FOX, D_MODEL, FOX_IN), D_MODEL),
        "fox_b_f": 2.0 + 0.5 * jax.random.normal(ks[9], (N_FOX, FOX_HEADS), f32),
        "fox_q_norm": gain(ks[10], (N_FOX, FOX_HD)),
        "fox_k_norm": gain(ks[11], (N_FOX, FOX_HD)),
        "fox_w_out": nrm(ks[12], (N_FOX, FOX_WIDTH, D_MODEL), FOX_WIDTH),
        "ple_proj": nrm(ks[13], (DEPTH_2, PLE_DIM, D_MODEL), PLE_DIM),
        "ple_gate": nrm(ks[14], (DEPTH_2, D_MODEL, D_MODEL), D_MODEL),
        "ple_norm": gain(ks[15], (DEPTH_2, D_MODEL)),
        "final_norm": gain(ks[16], (D_MODEL,)),
    }

def second_block(x, p, norm_mixer, gla_w_in, gla_w_a2, gla_b_a, gla_o_norm, gla_w_out,
              fox_w_in, fox_b_f, fox_q_norm, fox_k_norm, fox_w_out,
              ple_proj, ple_gate, ple_norm, final_norm):
    h = x
    for i in range(DEPTH_2):
        hn = rms_norm(h, norm_mixer[i])
        j = i // N_MIXERS
        if i % N_MIXERS == 0:
            h = h + gla_mixer(hn, gla_w_in[j], gla_w_a2[j], gla_b_a[j], gla_o_norm[j], gla_w_out[j])
        else:
            h = h + fox_mixer(hn, fox_w_in[j], fox_b_f[j], fox_q_norm[j], fox_k_norm[j], fox_w_out[j])
        h = h + (p[i] @ ple_proj[i]) * jax.nn.sigmoid(rms_norm(h, ple_norm[i]) @ ple_gate[i])
    return rms_norm(h, final_norm)


def setup_inputs(seed=0):
    out = dict(first_inputs(seed))
    for name, value in second_inputs(seed + 1).items():
        if name != "x":
            out[name + "_2"] = value
    return out


def reference(
    x, norm_mix, w_in, A_re, A_im, log_dt, B_re, B_im, C_re, C_im, D_skip, w_glu, b_glu,
    w_up_ssm, w_up_attn, w_gate, b_gate, w_out, norm_mlp, w_ff1, w_ff2, norm_final, p_2,
    norm_mixer_2, gla_w_in_2, gla_w_a2_2, gla_b_a_2, gla_o_norm_2, gla_w_out_2, fox_w_in_2,
    fox_b_f_2, fox_q_norm_2, fox_k_norm_2, fox_w_out_2, ple_proj_2, ple_gate_2, ple_norm_2,
    final_norm_2,
):
    x = first_block(
        x, norm_mix, w_in, A_re, A_im, log_dt, B_re, B_im, C_re, C_im, D_skip, w_glu, b_glu,
        w_up_ssm, w_up_attn, w_gate, b_gate, w_out, norm_mlp, w_ff1, w_ff2, norm_final,
    )
    return second_block(
        x, p_2, norm_mixer_2, gla_w_in_2, gla_w_a2_2, gla_b_a_2, gla_o_norm_2, gla_w_out_2,
        fox_w_in_2, fox_b_f_2, fox_q_norm_2, fox_k_norm_2, fox_w_out_2, ple_proj_2, ple_gate_2,
        ple_norm_2, final_norm_2,
    )


_drawn_inputs = setup_inputs


def setup_inputs(seed=0):
    import zlib

    import numpy as np

    out = dict(_drawn_inputs(seed))
    spreads = {}
    factors = {'norm_mix': 4.43,
     'A_re': 200.0,
     'A_im': 2.676,
     'log_dt': 2.805,
     'B_re': 3.722,
     'B_im': 3.753,
     'C_re': 3.796,
     'C_im': 3.806,
     'b_glu': 8.0,
     'b_gate': 8.0,
     'norm_mlp': 2.819,
     'norm_mixer_2': 2.876,
     'gla_o_norm_2': 5.788,
     'fox_q_norm_2': 8.0,
     'fox_k_norm_2': 8.0,
     'ple_norm_2': 200.0,
     'final_norm_2': 20.519}
    for name, (base, spread) in spreads.items():
        noise = np.random.default_rng([zlib.crc32(name.encode()), seed]).standard_normal(out[name].shape)
        drawn = base * np.exp(spread * noise) if base else spread * noise
        out[name] = __import__('jax').numpy.asarray(drawn.astype(out[name].dtype))
    for name, factor in factors.items():
        out[name] = (out[name] * factor).astype(out[name].dtype)
    return out
```

```python
from contextlib import ExitStack

import concourse.bass as bass
import concourse.mybir as mybir
import numpy as np

F32 = mybir.dt.float32
F32R = mybir.dt.float32r
U32 = mybir.dt.uint32
ALU = mybir.AluOpType
ACT = mybir.ActivationFunctionType
AX = mybir.AxisListType

P = 128
T = 512
D = 1024
DC = D // P
TT = T // P
DH = 512
HC = DH // P
FFB = 8
S5_PAIRS = 16
GLA_H = 4
GLA_N = 8
GLA_C = 64
FOX_PAIRS = 8
EPS = 1e-6
NEG = -1e30
ROUND = 12582912.0
TWO_PI = float(np.nextafter(np.float32(2 * np.pi), np.float32(0)))
UW = 2048

U_MIX, N_MIX = 0, 8
U_MERGE = U_MIX + N_MIX
MERGE_BLOCKS = [2, 2, 2, 2, 4, 4, 4, 2, 2, 2, 2, 4, 4]
U_OUT = U_MERGE + len(MERGE_BLOCKS)
U_FF = U_OUT + 4
U_ALR = U_FF + 4 * FFB
U_GLA = U_ALR + 1
U_GLAG = U_GLA + 2 * GLA_H
U_GLAO = U_GLAG + 4
U_PLE0 = U_GLAO + 4
U_F = U_PLE0 + 5
U_FOX = U_F + 1
U_FOXO = U_FOX + 2 * FOX_PAIRS
U_PLE1 = U_FOXO + 4
NU = U_PLE1 + 5
BLOCKS = ([2] * N_MIX + MERGE_BLOCKS + [2] * 4 + [2, 2, 4, 4] * FFB + [1] + [2] * (2 * GLA_H + 8)
          + [8, 2, 2, 2, 2] + [1] + [2] * (2 * FOX_PAIRS + 4) + [8, 2, 2, 2, 2])
DONE = [0]
for _b in BLOCKS:
    DONE.append(DONE[-1] + _b)
assert len(BLOCKS) == NU

VEC = {}
_at = 0
for _name, _w in [("norm_mix", 8), ("norm_mlp", 8), ("norm_final", 8), ("norm_mixer0", 8), ("ple_norm0", 8),
                  ("norm_mixer1", 8), ("ple_norm1", 8), ("final_norm", 8), ("D_skip", 4), ("b_glu", 4),
                  ("b_gate", 16), ("gla_b_a", 4), ("gla_o_norm", 2), ("fox_q_norm", 1), ("fox_k_norm", 1),
                  ("fox_b_f", 1)]:
    VEC[_name] = _at
    _at += _w
NVEC = _at
CST = {}
_at = 0
for _name, _w in [("ident", P), ("ones", P), ("keymask", P), ("querymask", P), ("tri", P), ("negones", P),
                  ("headones", P), ("samechunk", P), ("reset", T), ("tvec", T)]:
    CST[_name] = (_at, _at + _w)
    _at += _w
NCST = _at

KB_AT = {0: 0, 1: 512, 3: 896, 2: 1024}
QB_AT = {3: 0, 2: 512, 0: 896, 1: 1024}
NZ = 1280


class Chain:

    def __init__(self, eng, sem):
        self.eng, self.sem, self.base, self.n = eng, sem, 0, 0

    def do(self, ins):
        ins.then_inc(self.sem, 1)
        self.n += 1

    def sync(self):
        self.eng.wait_ge(self.sem, self.base + self.n)

    def enter(self, i, per):
        self.start, self.per = self.base + self.n, per
        self.base, self.n = i * per + self.start, 0

    def leave(self, count):
        assert self.n == self.per, (self.sem.name, self.n)
        self.base, self.n = self.start + self.per * count, 0


def build(nc, wstream, xT, pT, vecs_d, cst_d, s5p_d, cpad_d, wa2_d, outT):
    ctx = ExitStack()
    with ctx:
        def sb(name, shape, dt=F32, stack=ctx):
            return stack.enter_context(nc.sbuf_tensor(name, shape, dt))

        def sem(name):
            return ctx.enter_context(nc.semaphore(name))

        h = sb("h", [P, DC, T])
        uhi = sb("uhi", [P, DC, T], F32R)
        ulo = sb("ulo", [P, DC, T], F32R)
        wraw = sb("wraw", [P, 2, UW])
        whi = sb("whi", [P, 2, UW], F32R)
        wlo = sb("wlo", [P, 2, UW], F32R)
        vecs = sb("vecs", [P, NVEC])
        ident = sb("ident", [P, P])
        ones = sb("ones", [P, P])
        headones = sb("headones", [P, P])
        identr = sb("identr", [P, P], F32R)
        onesr = sb("onesr", [P, P], F32R)
        keymaskr = sb("keymaskr", [P, P], F32R)
        querymaskr = sb("querymaskr", [P, P], F32R)
        trir = sb("trir", [P, P], F32R)
        negonesr = sb("negonesr", [P, P], F32R)
        samechunk = sb("samechunk", [P, P])
        reset = sb("reset", [P, T])
        biases = sb("biases", [P, 6])
        eps_b, one_b, halfpi_b, zero_b = (biases[:, k:k + 1] for k in range(4))

        def vec(name, c=0):
            return vecs[:, VEC[name] + c:VEC[name] + c + 1]

        def scope():
            return ExitStack()

        wa2 = sb("wa2", [16, T])
        s5r = sb("s5r", [P, 2, S5_PAIRS], F32R)

        with scope() as m:
            ys = sb("ys", [P, HC, T], F32, m)
            ya = sb("ya", [P, HC, T], F32, m)
            with scope() as e:
                tvec = sb("tvec", [P, T], F32, e)
                s5p = sb("s5p", [P, 24, S5_PAIRS], F32, e)
                BT = sb("BT", [P, HC, 2, P], F32, e)
                Bs = sb("Bs", [P, 2, P], F32, e)
                Cs = sb("Cs", [P, 4, 2, P], F32, e)
                Cn = sb("Cn", [P, 4, P], F32, e)
                uch = sb("uch", [P, T], F32, e)
                vT = sb("vT", [P, T], F32, e)
                qkhi = sb("qkhi", [P, 2, T], F32R, e)
                qklo = sb("qklo", [P, 2, T], F32R, e)
                with scope() as s:
                    sq = sb("sq", [P, 2, T], F32, s)
                    un = sb("un", [P, 2, T], F32, s)
                    rs_ln = sb("rs_ln", [P, T], F32, s)
                    rs_half = sb("rs_half", [P, T], F32, s)
                    rs_y = sb("rs_y", [P, T], F32, s)
                    rs_t = sb("rs_t", [P, T], F32, s)
                    rstd = sb("rstd", [P, T], F32, s)
                    with scope() as pl:
                        pe_in = sb("pe_in", [P, 2, T], F32, pl)
                        pehi = sb("pehi", [P, 2, T], F32R, pl)
                        pelo = sb("pelo", [P, 2, T], F32R, pl)
                        pp = sb("pp", [P, DC, T], F32, pl)
                        sg = sb("sg", [P, 2, T], F32, pl)
                    cst_in = sb("cst_in", [P, 5, P], F32, s)
                    s5b = sb("s5b", [P, 6, 512], F32, s)
                with scope() as s:
                    vhi = sb("vhi", [P, TT, P], F32R, s)
                    vlo = sb("vlo", [P, TT, P], F32R, s)
                    att = sb("att", [P, NZ], F32, s)
                    athi = sb("athi", [P, NZ], F32R, s)
                    atlo = sb("atlo", [P, NZ], F32R, s)
                    cosT = sb("cosT", [P, 4, T], F32, s)
                    sinT = sb("sinT", [P, 4, T], F32, s)
                    ph = sb("ph", [P, 2, T], F32, s)
                    rin = sb("rin", [P, 2, T], F32, s)
                    rin2 = sb("rin2", [P, 2, T], F32, s)
                    zst = sb("zst", [P, 2, T], F32, s)
                    rout1 = sb("rout1", [P, 2, T], F32, s)
                    rout2 = sb("rout2", [P, 2, T], F32, s)
            with scope() as s:
                yhi = sb("yhi", [P, HC, T], F32R, s)
                ylo = sb("ylo", [P, HC, T], F32R, s)
                ahi = sb("ahi", [P, HC, T], F32R, s)
                alo = sb("alo", [P, HC, T], F32R, s)
                gate = sb("gate", [P, 2, 4, T], F32, s)
                glu = sb("glu", [P, 2, T], F32, s)
                mg = glu
                mhi = sb("mhi", [P, DC, T], F32R, s)
                mlo = sb("mlo", [P, DC, T], F32R, s)
        with scope() as s:
            rl = sb("rl", [P, 2, T], F32, s)
            hd = sb("hd", [P, 2, T], F32, s)
            hdhi = sb("hdhi", [P, 4, T], F32R, s)
            hdlo = sb("hdlo", [P, 4, T], F32R, s)
        with scope() as m:
            og = sb("og", [P, DC, T], F32, m)
            gr = sb("gr", [P, DC, T], F32, m)
            with scope() as s:
                alr = sb("alr", [P, T], F32, s)
                cum = sb("cum", [P, GLA_H, T], F32, s)
                la = sb("la", [P, 2, T], F32, s)
                eq = sb("eq", [P, T], F32, s)
                ek = sb("ek", [P, T], F32, s)
                kd = sb("kd", [P, T], F32, s)
                qin = sb("qin", [P, T], F32, s)
                kin = sb("kin", [P, T], F32, s)
                kdec = sb("kdec", [P, T], F32, s)
                qihi = sb("qihi", [P, T], F32R, s)
                qilo = sb("qilo", [P, T], F32R, s)
                kihi = sb("kihi", [P, T], F32R, s)
                kilo = sb("kilo", [P, T], F32R, s)
                kdhi = sb("kdhi", [P, T], F32R, s)
                kdlo = sb("kdlo", [P, T], F32R, s)
                gvhi = sb("gvhi", [P, TT, 256], F32R, s)
                gvlo = sb("gvlo", [P, TT, 256], F32R, s)
                ai = sb("ai", [P, TT, P], F32, s)
                aihi = sb("aihi", [P, TT, P], F32R, s)
                ailo = sb("ailo", [P, TT, P], F32R, s)
                st = sb("st", [P, 2, 256], F32, s)
                sthi = sb("sthi", [P, GLA_N, 256], F32R, s)
                stlo = sb("stlo", [P, GLA_N, 256], F32R, s)
                gsq, g_ln, g_half, g_t, g_y = la, qin, kin, kdec, alr
            with scope() as s:
                fl = sb("fl", [16, 3, T], F32, s)
                nchi = sb("nchi", [16, T], F32R, s)
                nclo = sb("nclo", [16, T], F32R, s)
                cmhi = sb("cmhi", [16, T], F32R, s)
                cmlo = sb("cmlo", [16, T], F32R, s)
                gq8 = sb("gq8", [P, 1], F32, s)
                qk = sb("qk", [P, 2, T], F32, s)
                qksq = sb("qksq", [P, 2, T], F32, s)
                f_ln = sb("f_ln", [P, 2, T], F32, s)
                f_half = sb("f_half", [P, 2, T], F32, s)
                f_y = sb("f_y", [P, 2, T], F32, s)
                fqhi = sb("fqhi", [P, 2, T], F32R, s)
                fqlo = sb("fqlo", [P, 2, T], F32R, s)
                fvT = sb("fvT", [P, T], F32, s)
                fvhi = sb("fvhi", [P, TT, P], F32R, s)
                fvlo = sb("fvlo", [P, TT, P], F32R, s)
                pr = sb("pr", [P, NZ], F32, s)
                pthi = sb("pthi", [P, NZ], F32R, s)
                ptlo = sb("ptlo", [P, NZ], F32R, s)
                nmax = sb("nmax", [P, TT], F32, s)
                rsum = sb("rsum", [P, TT], F32, s)
                rinv = sb("rinv", [P, TT], F32, s)
        ps = ctx.enter_context(nc.psum_tensor("ps", [P, 8, 512], F32))
        flat = ps[:, :, :].rearrange("p b n -> p (b n)")
        SS_BANK = (7, 4, 0, 0, 7, 7, 7, 7)
        NORM_U = {0: 0, 1: 1, 3: 2, 4: 3, 5: 4, 6: 5}
        N_CST = 13


        KV_FIRST = (0, 1, 4)

        def kv_sums(c):
            return ps[:, (6, 7, 2, 3)[2 * (c // 4) + c % 2], (c // 2) % 2 * 256:(c // 2) % 2 * 256 + 256]

        x_in, cst_sem, par_in, pe_sem = sem("x_in"), sem("consts_in"), sem("params_in"), sem("ple_in")
        cs_in = sem("c_matrix_in")
        out_sem = sem("out_stored")
        landed = [sem("weights_landed0"), sem("weights_landed1")]
        hi_done, lo_done = sem("weights_hi_done"), sem("weights_lo_done")
        block_done = sem("block_done")
        act_own, dve_own, pool_own = sem("act_own_steps"), sem("dve_own_steps"), sem("pool_own_steps")
        consts_ready, bias_ready = sem("consts_ready"), sem("bias_ready")
        sq_done, ss_done = sem("norm_squares"), sem("norm_sums")
        y_done, un_done, u_hi, u_ready = sem("norm_guess"), sem("norm_scaled"), sem("norm_hi"), sem("u_ready")
        ln_done, gln_done, fln_done = sem("norm_log"), sem("gla_norm_log"), sem("fox_norm_log")
        h_added = sem("h_added")
        h_normed = sem("h_normed")
        s5_exp, s5_arg, s5_trig = sem("s5_exp"), sem("s5_arg"), sem("s5_trig")
        B_ready, BT_done = sem("s5_B_scaled"), sem("s5_B_transposed")
        bs_ready, nim_ready = sem("s5_B_staged"), sem("s5_C_ready")
        q_hi, qk_ready, vT_ready, uch_ready = sem("qk_hi"), sem("qk_ready"), sem("vT_ready"), sem("u_ssm_ready")
        v_tr, v_hi, v_ready = sem("v_transposed"), sem("v_hi"), sem("v_ready")
        phase_ready, table_ready = sem("s5_phase"), sem("s5_tables")
        bu_done, bu_used, z5_done, rot_out, y5_done, ys_done = (sem("s5_" + n) for n in (
            "bu", "bu_used", "state", "rotated", "y", "chunk"))
        z_done, l_done, sp_done, l_hi, l_ready, tri_done = (sem("att_" + n) for n in (
            "scores", "log1p", "softplus", "fail_hi", "fail_ready", "logw"))
        w_hi, w_ready, pv_done, ya_done = sem("att_w_hi"), sem("att_w_ready"), sem("att_out"), sem("att_stored")
        ye_hi, y_ready, sig_evac, y2_done, up_evac, mg_done, mg_hi, mg_ready = (sem("merge_" + n) for n in (
            "hi", "branch_ready", "sigmoid", "glu", "up", "sum", "sum_hi", "sum_ready"))
        rl_done, hd_done, hd_hi, hd_ready = sem("relu_done"), sem("hid_done"), sem("hid_hi"), sem("hid_ready")
        alr_ready, la_mm, la_abs, la_ln, cum_done = (sem("gla_" + n) for n in (
            "lowrank", "gate_logits", "gate_evac", "gate_log", "cum"))
        dec_in, dec_done, in_done, in_hi, in_ready = (sem("gla_" + n) for n in (
            "decay_in", "decays", "scaled", "scaled_hi", "scaled_ready"))
        kd_tr, kd_hi, kd_ready, gv_hi, gv_ready = (sem("gla_" + n) for n in (
            "k_transposed", "k_hi", "k_ready", "v_hi", "v_ready"))
        ai_mm, ai_done, ai_hi, ai_ready = (sem("gla_" + n) for n in ("attn", "attn_masked", "attn_hi", "attn_ready"))
        kv_mm, st_done, st_hi, st_ready = (sem("gla_" + n) for n in ("kv", "state", "state_hi", "state_ready"))
        go_mm, gsq_done, gss_mm, gy_done, go_done = (sem("gla_" + n) for n in ("out", "squares", "sums", "guess", "stored"))
        g_evac, silu_done, prod_done, gated, gated_hi = (sem("gate_" + n) for n in ("logits", "silu", "product", "u", "u_hi"))
        f_evac, f_ln_done, f_min, c_ready, f_exp = (sem("fox_" + n) for n in ("f_in", "f_log", "f_min", "c_ready", "f_one"))
        qk_copy, qk_sq, qk_ss, fy_done, qk_n, fq_hi, fq_ready = (sem("fox_" + n) for n in (
            "qk", "squares", "sums", "guess", "qk_normed", "qk_hi", "qk_ready"))
        fvT_ready, g_copy, fv_tr, fv_hi, fv_ready = (sem("fox_" + n) for n in ("vT", "g", "v_transposed", "v_hi", "v_ready"))
        cm_ready, fz_done, max_done, exp_done, p_done, pt_done, pt_hi, pt_ready, fpv_done, fo_done = (
            sem("fox_" + n) for n in ("bias", "scores", "max", "exp", "probs", "transposed", "probs_hi", "probs_ready",
                                      "pv", "stored"))
        pe_hi, pe_ready, pp_done, sg_done = sem("ple_hi"), sem("ple_ready"), sem("ple_proj"), sem("ple_sigmoid")
        sgp = sem("ple_gated")
        out_ready = sem("out_ready")

        block = ctx.enter_context(nc.Block())

        @block.sync
        def _(sp):
            sp.dma_start(h[:, :, :], xT).then_inc(x_in, 16)
            sp.dma_start(vecs[:, :], vecs_d).then_inc(cst_sem, 16)
            for name, dst in (("ident", ident), ("ones", ones), ("headones", headones), ("samechunk", samechunk),
                              ("reset", reset), ("tvec", tvec)):
                a, b = CST[name]
                sp.dma_start(dst[:, :], cst_d[:, a:b]).then_inc(cst_sem, 16)
            for k, name in enumerate(("ones", "keymask", "querymask", "tri", "negones")):
                a, b = CST[name]
                sp.dma_start(cst_in[:, k, :], cst_d[:, a:b]).then_inc(cst_sem, 16)
            sp.dma_start(wa2[:, :], wa2_d).then_inc(cst_sem, 16)
            for n in range(2):
                sp.dma_start(wraw[:, n, :], wstream[n]).then_inc(landed[n], 16)
            sp.dma_start(s5p[:, 0:3, :], s5p_d[:, 0:48].rearrange("p (a b) -> p a b", a=3)).then_inc(par_in, 16)
            sp.dma_start(s5b[:, 0:2, :], s5p_d[:, 48:].rearrange("p (a b) -> p a b", a=2)).then_inc(par_in, 16)
            with nc.sync.Fori(0, (NU - 3) // 2) as i:
                for n in range(2):
                    sp.wait_ge(lo_done, i * 2 + (n + 1))
                    sp.dma_start(wraw[:, n, :], wstream[i * 2 + (n + 2)]).then_inc(landed[n], 16)
            sp.wait_ge(lo_done, NU - 2)
            sp.dma_start(wraw[:, 0, :], wstream[NU - 1]).then_inc(landed[0], 16)
            for c in range(DC):
                sp.wait_ge(out_ready, c + 1)
                sp.dma_start(outT[:, c, :], pp[:, c, :]).then_inc(out_sem, 16)
            sp.wait_ge(out_sem, 16 * DC)

        assert NU % 2 == 1

        @block.gpsimd
        def _(pool):
            own = Chain(pool, pool_own)

            def load_c(i):
                pool.dma_start(Cs[:, :, :, :], cpad_d[i].rearrange("p (a b c) -> p a b c", a=4, b=2)).then_inc(cs_in, 16)

            def negate_c(i):
                pool.wait_ge(cs_in, i * 16 + 16)
                nc.gpsimd.tensor_tensor(Cn[:, :, :], Cs[:, :, 1, :], biases[:, 4:5].unsqueeze(2).to_broadcast([P, 4, P]),
                                        ALU.mult).then_inc(nim_ready, 1)

            def mixer(i, last=False):
                for p in range(4):
                    pool.wait_ge(z5_done, i * 4 + (p + 1))
                    pool.wait_ge(table_ready, i * 4 + (p + 1))
                    if p >= 1:
                        pool.wait_ge(y5_done, i * 4 + p)
                    own.do(nc.gpsimd.tensor_tensor(rout1[:, :, :], zst[:, :, :],
                                                   cosT[:, p, :].unsqueeze(1).to_broadcast([P, 2, T]), ALU.mult))
                    own.do(nc.gpsimd.tensor_tensor(rout2[:, :, :], zst[:, :, :],
                                                   sinT[:, p, :].unsqueeze(1).to_broadcast([P, 2, T]), ALU.mult))
                    own.sync()
                    nc.gpsimd.tensor_tensor(rout1[:, 0, :], rout1[:, 0, :], rout2[:, 1, :], ALU.add)
                    nc.gpsimd.tensor_tensor(rout1[:, 1, :], rout1[:, 1, :], rout2[:, 0, :], ALU.subtract).then_inc(rot_out, 1)
                if not last:
                    pool.wait_ge(y5_done, i * 4 + 4)
                    load_c(i + 1)
                    negate_c(i + 1)

            nc.gpsimd.memset(biases[:, 0:1], EPS)
            nc.gpsimd.memset(biases[:, 1:2], 1.0)
            nc.gpsimd.memset(biases[:, 2:3], float(np.pi / 2))
            nc.gpsimd.memset(biases[:, 3:4], 0.0)
            nc.gpsimd.memset(biases[:, 4:5], -1.0).then_inc(bias_ready, 1)
            pool.wait_ge(bias_ready, 1)
            load_c(0)
            negate_c(0)
            with nc.gpsimd.Fori(0, HC - 1) as i:
                own.enter(i, 8)
                mixer(i)
                own.leave(HC - 1)
            mixer(HC - 1, True)
            pool.wait_ge(go_done, 2 * GLA_H)
            pool.dma_start(pe_in[:, :, :], pT[0]).then_inc(pe_sem, 16)
            pool.wait_ge(fo_done, 2 * FOX_PAIRS)
            pool.dma_start(pe_in[:, :, :], pT[1]).then_inc(pe_sem, 16)

        @block.tensor
        def _(pe):
            def three(out, lh, ll, rh, rl_, start, stop=False, done=None):
                nc.tensor.matmul(out, lh, rh, start=start, stop=False, skip_group_check=True)
                nc.tensor.matmul(out, lh, rl_, start=False, stop=False, skip_group_check=True)
                mm = nc.tensor.matmul(out, ll, rh, start=False, stop=stop, skip_group_check=True)
                if done is not None:
                    mm.then_inc(done, 1)

            def gemm(n, slot, blocks, cols, hi, lo, by_k=False, k_wait=None):
                pe.wait_ge(lo_done, n + 1)
                wh = whi[:, slot, :].rearrange("p (k c) -> p k c", c=cols)
                wl = wlo[:, slot, :].rearrange("p (k c) -> p k c", c=cols)

                def step(b, k):
                    col, w0, kc, x0, bank = b
                    three(ps[:, bank, :], wh[:, w0 + k, col:col + P], wl[:, w0 + k, col:col + P],
                          hi[:, x0 + k, :], lo[:, x0 + k, :], k == 0, k == kc - 1,
                          block_done if k == kc - 1 else None)

                if by_k:
                    for k in range(blocks[0][2]):
                        if k_wait is not None:
                            k_wait(k)
                        for b in blocks:
                            step(b, k)
                else:
                    for b in blocks:
                        for k in range(b[2]):
                            step(b, k)

            def two(bank):
                return [(0, 0, DC, 0, bank), (P, 0, DC, 0, bank + 1)]

            def one(k):
                return [(k * P, 0, DC, 0, k)]

            def u_wait(j):
                return lambda k: pe.wait_ge(u_ready, 8 * NORM_U[j] + k + 1)

            def norm_sums(j):
                for c in range(DC):
                    pe.wait_ge(sq_done, 8 * j + c + 1)
                    nc.tensor.matmul(ps[:, SS_BANK[j], :], ones[:, :], sq[:, c % 2, :], start=(c == 0),
                                     stop=(c == DC - 1)).then_inc(ss_done, 1)

            def s5_prepare():
                pe.wait_ge(B_ready, 2)
                pe.wait_ge(cst_sem, 16 * N_CST)
                for r in range(2):
                    for c in range(HC):
                        mm = nc.tensor.transpose(ps[:, 5 + r, c * P:(c + 1) * P], s5b[:, 2 + r, c * P:(c + 1) * P],
                                                 ident[:, :])
                mm.then_inc(BT_done, 1)

            Z0, Z1, Z2, S0, YB = 2, 3, 4, 5, 7
            zf = flat[:, Z0 * 512:Z0 * 512 + NZ]

            def transpose_values(i):
                pe.wait_ge(vT_ready, i + 1)
                for t in range(TT):
                    mm = nc.tensor.transpose(ps[:, 0, t * P:(t + 1) * P], vT[:, t * P:(t + 1) * P], ident[:, :])
                mm.then_inc(v_tr, 1)

            def mixer(i, last=False):
                def bu(p):
                    if p >= 1:
                        pe.wait_ge(bu_used, i * 4 + p)
                    pe.wait_ge(bs_ready, i + 1)
                    pe.wait_ge(uch_ready, i + 1)
                    rows = slice(32 * p, 32 * p + 32)
                    nc.tensor.matmul(ps[:, S0, :], Bs[rows, 0, :], uch[rows, :], start=True, stop=True)
                    nc.tensor.matmul(ps[:, S0 + 1, :], Bs[rows, 1, :], uch[rows, :], start=True,
                                     stop=True).then_inc(bu_done, 1)

                def scores(hh):
                    if hh == 0:
                        pe.wait_ge(qk_ready, i * 2 + 2)
                    else:
                        pe.wait_ge(ya_done, i * 2 + 1)
                    rows = slice(64 * hh, 64 * hh + 64)
                    for kb in range(TT):
                        out = zf[:, KB_AT[kb]:KB_AT[kb] + T - kb * P]
                        keys = slice(kb * P, (kb + 1) * P)
                        three(out, qkhi[rows, 1, keys], qklo[rows, 1, keys], qkhi[rows, 0, kb * P:],
                              qklo[rows, 0, kb * P:], kb != 3)
                        mm = nc.tensor.matmul(out[:, 0:P], identr[:, :], keymaskr[:, :], start=False, stop=False,
                                              skip_group_check=True)
                    mm.then_inc(z_done, 1)

                def log_weights(hh):
                    pe.wait_ge(l_ready, i * 2 + (hh + 1))
                    for kb in range(TT):
                        for kc in range(kb, TT):
                            n = T - kc * P
                            at = KB_AT[kb] + (kc - kb) * P
                            lhs = trir if kc == kb else negonesr
                            for part in (athi, atlo):
                                mm = nc.tensor.matmul(zf[:, at:at + n], lhs[:, :], part[:, KB_AT[kc]:KB_AT[kc] + n],
                                                      start=False, stop=False, skip_group_check=True)
                    mm.then_inc(tri_done, 1)

                def weigh_values(hh):
                    pe.wait_ge(w_ready, i * 2 + (hh + 1))
                    for kb in range(TT):
                        n = T - kb * P
                        three(ps[:, Z0, kb * P:], vhi[:, kb, :], vlo[:, kb, :], athi[:, KB_AT[kb]:KB_AT[kb] + n],
                              atlo[:, KB_AT[kb]:KB_AT[kb] + n], kb == 0, kb == TT - 1,
                              pv_done if kb == TT - 1 else None)

                def y(p):
                    pe.wait_ge(rot_out, i * 4 + (p + 1))
                    pe.wait_ge(nim_ready, i + 1)
                    nc.tensor.matmul(ps[:, YB, :], Cs[:, p, 0, :], rout1[:, 0, :], start=(p == 0), stop=False)
                    mm = nc.tensor.matmul(ps[:, YB, :], Cn[:, p, :], rout1[:, 1, :], start=False, stop=(p == 3))
                    mm.then_inc(y5_done, 1)

                scores(0)
                bu(0)
                pe.wait_ge(v_ready, i + 1)
                if not last:
                    gemm(i * 2 + 2, 0, one(0), 256, uhi, ulo)
                bu(1)
                log_weights(0)
                y(0)
                bu(2)
                weigh_values(0)
                scores(1)
                y(1)
                bu(3)
                if not last:
                    gemm(i * 2 + 2, 0, one(1), 256, uhi, ulo)
                    pe.wait_ge(qk_ready, i * 2 + 3)
                    gemm(i * 2 + 3, 1, one(0), 256, uhi, ulo)
                log_weights(1)
                y(2)
                if not last:
                    pe.wait_ge(qk_ready, i * 2 + 4)
                    gemm(i * 2 + 3, 1, one(1), 256, uhi, ulo)
                    transpose_values(i + 1)
                weigh_values(1)
                y(3)
                pe.wait_ge(ya_done, i * 2 + 2)

            def merge():
                n = U_MERGE
                gemm(n, n % 2, two(0), 256, uhi, ulo)
                pe.wait_ge(ya_done, 2 * HC)
                gemm(n + 1, (n + 1) % 2, two(2), 256, uhi, ulo)
                pe.wait_ge(sig_evac, 2)
                gemm(n + 2, (n + 2) % 2, two(0), 256, uhi, ulo)
                pe.wait_ge(sig_evac, 4)
                gemm(n + 3, (n + 3) % 2, two(2), 256, uhi, ulo)
                pe.wait_ge(ys_done, HC)
                pe.wait_ge(y_ready, HC)
                gemm(n + 4, (n + 4) % 2, [(m * P, 0, HC, 0, 4 + m) for m in range(4)], 512, yhi, ylo)

                def up(k, bank):
                    blocks = [(0, 0, HC, 0, bank), (P, 0, HC, 0, bank + 1)]
                    pe.wait_ge(lo_done, k + 1)
                    gemm_up(k, blocks, bank)

                def gemm_up(k, blocks, bank):
                    slot = k % 2
                    wh = whi[:, slot, :].rearrange("p (k c) -> p k c", c=256)
                    wl = wlo[:, slot, :].rearrange("p (k c) -> p k c", c=256)
                    for m in range(2):
                        for b, (xh, xl) in enumerate(((yhi, ylo), (ahi, alo))):
                            for kk in range(HC):
                                w = b * HC + kk
                                three(ps[:, bank + 2 * m + b, :], wh[:, w, m * P:(m + 1) * P], wl[:, w, m * P:(m + 1) * P],
                                      xh[:, kk, :], xl[:, kk, :], kk == 0, kk == HC - 1,
                                      block_done if kk == HC - 1 else None)

                pe.wait_ge(y_ready, 3 * HC)
                pe.wait_ge(sig_evac, 8)
                up(n + 5, 0)
                pe.wait_ge(sig_evac, 12)
                up(n + 6, 4)
                pe.wait_ge(up_evac, 4)
                gemm(n + 7, (n + 7) % 2, two(0), 256, uhi, ulo)
                gemm(n + 8, (n + 8) % 2, two(2), 256, uhi, ulo)
                pe.wait_ge(sig_evac, 14)
                gemm(n + 9, (n + 9) % 2, two(0), 256, uhi, ulo)
                pe.wait_ge(sig_evac, 16)
                gemm(n + 10, (n + 10) % 2, two(2), 256, uhi, ulo)
                pe.wait_ge(up_evac, 8)
                up(n + 11, 4)
                pe.wait_ge(sig_evac, 20)
                up(n + 12, 0)
                n = U_OUT
                pe.wait_ge(up_evac, 12)
                gemm(n, n % 2, two(4), 256, mhi, mlo, True, lambda k: pe.wait_ge(mg_ready, k + 1))
                gemm(n + 1, (n + 1) % 2, two(6), 256, mhi, mlo)
                pe.wait_ge(up_evac, 16)
                gemm(n + 2, (n + 2) % 2, two(0), 256, mhi, mlo)
                gemm(n + 3, (n + 3) % 2, two(2), 256, mhi, mlo)

            ADDED_FF = DC

            def ff(i):
                for q in range(2):
                    n = i * 8 + (U_FF + 4 * q)
                    s = (U_FF + 4 * q) % 2
                    a, b = (0, 4) if q == 0 else (4, 0)
                    at = i * 16 + (ADDED_FF + 8 * q)
                    hid = i * 8 + 4 * q
                    first = u_wait(1)
                    pe.wait_ge(h_added, at - 4)
                    gemm(n, s, two(a), 256, uhi, ulo, True, first)
                    gemm(n + 1, 1 - s, two(a + 2), 256, uhi, ulo)
                    pe.wait_ge(h_added, at)
                    gemm(n + 2, s, [(m * P, 0, 4, 0, b + m) for m in range(4)], 512, hdhi, hdlo, True,
                         lambda k: pe.wait_ge(hd_ready, hid + (k + 1)))
                    gemm(n + 3, 1 - s, [(m * P, 0, 4, 0, a + m) for m in range(4)], 512, hdhi, hdlo, True)

            def gla_gate_logits():
                gemm(U_ALR, U_ALR % 2, [(0, 0, DC, 0, 0)], 256, uhi, ulo, True, u_wait(3))
                pe.wait_ge(alr_ready, 1)
                for hh in range(GLA_H):
                    nc.tensor.matmul(ps[:, 4 + hh, :], wa2[:, hh * P:(hh + 1) * P], alr[0:16, :], start=True,
                                     stop=True).then_inc(la_mm, 1)

            def gla_head(i, last=False):
                n = i * 2 + (U_GLA + 1)
                slot = (U_GLA + 1) % 2
                pe.wait_ge(lo_done, n + 1)
                wh = whi[:, slot, :].rearrange("p (k c) -> p k c", c=256)
                wl = wlo[:, slot, :].rearrange("p (k c) -> p k c", c=256)
                for t in range(TT):
                    tok = slice(t * P, (t + 1) * P)
                    for k in range(DC):
                        three(ps[:, 2 + t // 2, (t % 2) * 256:(t % 2) * 256 + 256], uhi[:, k, tok], ulo[:, k, tok],
                              wh[:, k, :], wl[:, k, :], k == 0, k == DC - 1,
                              block_done if k == DC - 1 and t % 2 else None)
                pe.wait_ge(in_done, i * 3 + 3)
                for t in range(TT):
                    mm = nc.tensor.transpose(ps[:, 4, t * P:(t + 1) * P], kdec[:, t * P:(t + 1) * P], ident[:, :])
                mm.then_inc(kd_tr, 1)
                pe.wait_ge(in_ready, i * 2 + 2)
                for t in range(TT):
                    tok = slice(t * P, (t + 1) * P)
                    three(ps[:, 5, tok], kihi[:, tok], kilo[:, tok], qihi[:, tok], qilo[:, tok], True, True,
                          ai_mm if t == TT - 1 else None)
                pe.wait_ge(kd_ready, i + 1)
                pe.wait_ge(gv_ready, i + 1)
                for c in range(GLA_N - 1):
                    rows = slice(64 * (c % 2), 64 * (c % 2) + 64)
                    keys = slice((c // 2) * P, (c // 2 + 1) * P)
                    three(kv_sums(c), kdhi[rows, keys], kdlo[rows, keys], gvhi[rows, c // 2, :], gvlo[rows, c // 2, :],
                          True, True, kv_mm)
                if not last:
                    gemm(i * 2 + (U_GLA + 2), U_GLA % 2, two(0), 256, uhi, ulo)
                pe.wait_ge(ai_ready, i + 1)
                pe.wait_ge(st_done, i * (GLA_N - 1) + (GLA_N - 1))
                for dv in range(2):
                    out = ps[:, 6 + dv, :]
                    cols = slice(dv * P, (dv + 1) * P)
                    for t in range(TT):
                        three(out[:, t * P:(t + 1) * P], gvhi[:, t, cols], gvlo[:, t, cols], aihi[:, t, :], ailo[:, t, :],
                              t == 0)
                    for c in range(1, GLA_N):
                        if dv == 0:
                            pe.wait_ge(st_ready, i * (GLA_N - 1) + c)
                        tok = slice(c * GLA_C, (c + 1) * GLA_C)
                        three(out[:, tok], sthi[:, c, cols], stlo[:, c, cols], qihi[:, tok], qilo[:, tok], False,
                              c == GLA_N - 1, go_mm if c == GLA_N - 1 else None)
                for dv in range(2):
                    pe.wait_ge(gsq_done, i * 2 + (dv + 1))
                    mm = nc.tensor.matmul(ps[:, 4, :], ones[:, :], gsq[:, dv, :], start=(dv == 0), stop=(dv == 1))
                mm.then_inc(gss_mm, 1)

            def residual_gemm(n, added, k_wait):
                for b in range(4):
                    if b >= 2:
                        pe.wait_ge(h_added, added + 2 * (b - 1))
                    gemm(n + b, (n + b) % 2, two(2 * (b % 2)), 256, uhi, ulo, b == 0, k_wait if b == 0 else None)

            def gate_gemm(n):
                for b in range(4):
                    if b >= 2:
                        pe.wait_ge(g_evac, 2 * (b - 1))
                    gemm(n + b, (n + b) % 2, two(2 * (b % 2)), 256, uhi, ulo)

            def ple_proj(layer, n):
                pe.wait_ge(pe_ready, 2 * layer + 2)
                pe.wait_ge(lo_done, n + 1)
                wh = whi[:, n % 2, :].rearrange("p (k c) -> p k c", c=1024)
                wl = wlo[:, n % 2, :].rearrange("p (k c) -> p k c", c=1024)
                for m in range(DC):
                    if m >= 3:
                        pe.wait_ge(pp_done, 8 * layer + m - 2)
                    for k in range(2):
                        three(ps[:, 4 + m % 3, :], wh[:, k, m * P:(m + 1) * P], wl[:, k, m * P:(m + 1) * P], pehi[:, k, :],
                              pelo[:, k, :], k == 0, k == 1, block_done if k == 1 else None)

            def ple_gate(layer, n, j):
                for b in range(4):
                    if b >= 2:
                        pe.wait_ge(sg_done, 8 * layer + 2 * (b - 1))
                    gemm(n + b, (n + b) % 2, two(2 * (b % 2)), 256, uhi, ulo, b == 0, u_wait(j) if b == 0 else None)

            TB = 5
            tf = flat[:, TB * 512:TB * 512 + NZ]

            def fox_qk_sums(i):
                pe.wait_ge(qk_sq, i + 1)
                for k in range(2):
                    mm = nc.tensor.matmul(ps[:, Z0 + k, :], headones[:, :], qksq[:, k, :], start=True, stop=True)
                mm.then_inc(qk_ss, 1)

            def fox_transpose_values(i):
                pe.wait_ge(fvT_ready, i + 1)
                for t in range(TT):
                    mm = nc.tensor.transpose(ps[:, TB + 2, t * P:(t + 1) * P], fvT[:, t * P:(t + 1) * P], ident[:, :])
                mm.then_inc(fv_tr, 1)

            def fox(i, last=False):
                def scores(hh):
                    if hh == 0:
                        pe.wait_ge(fq_ready, i + 1)
                    pe.wait_ge(cm_ready, i * 2 + (hh + 1))
                    rows = slice(64 * hh, 64 * hh + 64)
                    for qb in range(TT - 1, -1, -1):
                        n = (qb + 1) * P
                        out = zf[:, QB_AT[qb]:QB_AT[qb] + n]
                        toks = slice(qb * P, (qb + 1) * P)
                        three(out, fqhi[rows, 0, toks], fqlo[rows, 0, toks], fqhi[rows, 1, 0:n], fqlo[rows, 1, 0:n],
                              qb != 0)
                        for part in (cmhi, cmlo):
                            nc.tensor.matmul(out, onesr[0:16, :], part[:, 0:n], start=False, stop=False,
                                             skip_group_check=True)
                        mm = nc.tensor.matmul(out[:, n - P:n], identr[:, :], querymaskr[:, :], start=False, stop=False,
                                              skip_group_check=True)
                    mm.then_inc(fz_done, 1)

                def transpose_probs(hh):
                    pe.wait_ge(p_done, i * 2 + (hh + 1))
                    if hh == 0:
                        pe.wait_ge(fv_ready, i + 1)
                    else:
                        pe.wait_ge(fo_done, i * 2 + 1)
                    for qb in range(TT):
                        for kb in range(qb + 1):
                            at = KB_AT[kb] + (qb - kb) * P
                            mm = nc.tensor.transpose(tf[:, at:at + P], pr[:, QB_AT[qb] + kb * P:QB_AT[qb] + (kb + 1) * P],
                                                     ident[:, :])
                    mm.then_inc(pt_done, 1)

                def weigh_values(hh):
                    pe.wait_ge(pt_ready, i * 2 + (hh + 1))
                    for kb in range(TT):
                        n = T - kb * P
                        three(ps[:, TB, kb * P:], fvhi[:, kb, :], fvlo[:, kb, :], pthi[:, KB_AT[kb]:KB_AT[kb] + n],
                              ptlo[:, KB_AT[kb]:KB_AT[kb] + n], kb == 0, kb == TT - 1,
                              fpv_done if kb == TT - 1 else None)

                scores(0)
                if not last:
                    gemm(i * 2 + (U_FOX + 2), U_FOX % 2, one(0), 256, uhi, ulo)
                transpose_probs(0)
                scores(1)
                if not last:
                    pe.wait_ge(g_copy, i + 1)
                    gemm(i * 2 + (U_FOX + 2), U_FOX % 2, one(1), 256, uhi, ulo)
                weigh_values(0)
                transpose_probs(1)
                if not last:
                    fox_qk_sums(i + 1)
                    pe.wait_ge(qk_copy, i * 2 + 4)
                    gemm(i * 2 + (U_FOX + 3), (U_FOX + 1) % 2, one(0), 256, uhi, ulo)
                weigh_values(1)
                if not last:
                    fox_transpose_values(i + 1)
                    gemm(i * 2 + (U_FOX + 3), (U_FOX + 1) % 2, one(1), 256, uhi, ulo)

            pe.wait_ge(cst_sem, 16 * N_CST)
            norm_sums(0)
            gemm(0, 0, two(0), 256, uhi, ulo, True, u_wait(0))
            pe.wait_ge(qk_ready, 2)
            gemm(1, 1, two(0), 256, uhi, ulo)
            s5_prepare()
            transpose_values(0)
            pe.wait_ge(consts_ready, 6)
            with nc.tensor.Fori(0, HC - 1) as i:
                mixer(i)
            mixer(HC - 1, True)
            merge()
            norm_sums(1)
            with nc.tensor.Fori(0, FFB // 2) as i:
                ff(i)
            norm_sums(2)
            norm_sums(3)
            gla_gate_logits()
            gemm(U_GLA, U_GLA % 2, two(0), 256, uhi, ulo)
            with nc.tensor.Fori(0, GLA_H - 1) as i:
                gla_head(i)
            gla_head(GLA_H - 1, True)
            gate_gemm(U_GLAG)
            residual_gemm(U_GLAO, 72, lambda k: pe.wait_ge(gated, k + 1))
            ple_proj(0, U_PLE0)
            norm_sums(4)
            ple_gate(0, U_PLE0 + 1, 4)
            norm_sums(5)
            gemm(U_F, U_F % 2, [(0, 0, DC, 0, 0)], 256, uhi, ulo, True, u_wait(5))
            pe.wait_ge(f_evac, 1)
            gemm(U_FOX, U_FOX % 2, two(0), 256, uhi, ulo)
            fox_qk_sums(0)
            pe.wait_ge(qk_copy, 2)
            gemm(U_FOX + 1, (U_FOX + 1) % 2, two(0), 256, uhi, ulo)
            fox_transpose_values(0)
            with nc.tensor.Fori(0, FOX_PAIRS - 1) as i:
                fox(i)
            fox(FOX_PAIRS - 1, True)
            residual_gemm(U_FOXO, 88, lambda k: pe.wait_ge(gated, 8 + k + 1))
            ple_proj(1, U_PLE1)
            norm_sums(6)
            ple_gate(1, U_PLE1 + 1, 6)
            norm_sums(7)

        @block.scalar
        def _(act):
            own = Chain(act, act_own)
            A = nc.scalar.activation

            def copy(out, in_, scale=1.0):
                return A(out, in_, ACT.Copy, scale=scale)

            def split_hi(n, slot, parity_turn, done_before=None):
                act.wait_ge(landed[slot], parity_turn * 16 + 16)
                if done_before is not None:
                    act.wait_ge(block_done, done_before)
                copy(whi[:, slot, :], wraw[:, slot, :]).then_inc(hi_done, 1)

            def split_static(n):
                if n < NU:
                    split_hi(n, n % 2, n // 2, DONE[n - 1] if n >= 2 else None)

            def rsqrt_guess(out, tmp, sums, mean, ln_done, done, turn):
                A(tmp, sums, ACT.Ln, bias=eps_b, scale=mean).then_inc(ln_done, 1)
                act.wait_ge(ln_done, turn)
                A(out, tmp, ACT.Exp, scale=-0.5).then_inc(done, 1)

            def norm(j, h_wait, keep=False):
                for c in range(DC):
                    h_wait(act, c)
                    if c >= 2:
                        act.wait_ge(ss_done, 8 * j + c - 1)
                    A(sq[:, c % 2, :], h[:, c, :], ACT.Square).then_inc(sq_done, 1)
                act.wait_ge(ss_done, 8 * j + 8)
                rsqrt_guess(rs_y[:, :], rs_ln[:, :], ps[:, SS_BANK[j], :], 1.0 / D, ln_done, y_done, j + 1)
                if not keep:
                    u = NORM_U[j]
                    for c in range(DC):
                        act.wait_ge(un_done, 8 * u + c + 1)
                        copy(uhi[:, c, :], un[:, c % 2, :]).then_inc(u_hi, 1)

            def s5_prepare():
                act.wait_ge(par_in, 32)
                A(s5p[:, 3, :], s5p[:, 2, :], ACT.Exp).then_inc(s5_exp, 1)
                act.wait_ge(s5_arg, 1)
                A(s5p[:, 6, :], s5p[:, 4, :], ACT.Exp).then_inc(s5_exp, 1)
                act.wait_ge(s5_arg, 2)
                A(s5p[:, 14, :], s5p[:, 12, :], ACT.Sin, scale=TWO_PI).then_inc(s5_trig, 1)
                own.do(A(s5p[:, 13, :], s5p[:, 12, :], ACT.Abs))
                own.sync()
                A(s5p[:, 15, :], s5p[:, 13, :], ACT.Sin, scale=-TWO_PI, bias=halfpi_b).then_inc(s5_trig, 1)

            def s5_stage():
                act.wait_ge(BT_done, 1)
                own.do(copy(BT[:, :, 0, :], ps[:, 5, :].rearrange("p (c n) -> p c n", c=HC)))
                own.do(copy(BT[:, :, 1, :], ps[:, 6, :].rearrange("p (c n) -> p c n", c=HC)))
                own.sync()
                copy(Bs[:, :, :], BT[:, 0, :, :]).then_inc(bs_ready, 1)

            Z0 = 2
            zf = flat[:, Z0 * 512:Z0 * 512 + NZ]

            def evac_qk(i):
                act.wait_ge(block_done, i * 4 + 2)
                copy(qkhi[:, 0, :], ps[:, 0, :], 0.125).then_inc(q_hi, 1)
                copy(qkhi[:, 1, :], ps[:, 1, :]).then_inc(q_hi, 1)

            def evac_v(i):
                act.wait_ge(block_done, i * 4 + 3)
                copy(vT[:, :], ps[:, 0, :]).then_inc(vT_ready, 1)

            def values_hi(i):
                act.wait_ge(v_tr, i + 1)
                copy(vhi[:, :, :], ps[:, 0, :].rearrange("p (t c) -> p t c", t=TT)).then_inc(v_hi, 1)

            def evac_u(i):
                act.wait_ge(block_done, i * 4 + 4)
                copy(uch[:, :], ps[:, 1, :]).then_inc(uch_ready, 1)

            def table(i, p):
                act.wait_ge(phase_ready, i * 4 + (p + 1))
                own.do(A(sinT[:, p, :], cosT[:, p, :], ACT.Sin, scale=-TWO_PI))
                own.sync()
                own.do(A(cosT[:, p, :], cosT[:, p, :], ACT.Abs))
                own.sync()
                A(cosT[:, p, :], cosT[:, p, :], ACT.Sin, scale=-TWO_PI, bias=halfpi_b).then_inc(table_ready, 1)

            def mixer(i, last=False):
                def log1p(hh):
                    act.wait_ge(z_done, i * 2 + (hh + 1))
                    own.do(A(att[:, :], zf, ACT.Abs))
                    own.sync()
                    own.do(A(att[:, :], att[:, :], ACT.Exp, scale=-1.0))
                    own.sync()
                    A(att[:, :], att[:, :], ACT.Ln, bias=one_b).then_inc(l_done, 1)

                def fail_hi(hh):
                    act.wait_ge(sp_done, i * 2 + (hh + 1))
                    copy(athi[:, :], att[:, :]).then_inc(l_hi, 1)

                def weights(hh):
                    act.wait_ge(tri_done, i * 2 + (hh + 1))
                    own.do(A(att[:, :], zf, ACT.Exp))
                    own.sync()
                    copy(athi[:, :], att[:, :]).then_inc(w_hi, 1)

                def store(hh):
                    act.wait_ge(pv_done, i * 2 + (hh + 1))
                    rows = slice(64 * hh, 64 * hh + 64)
                    copy(ya[rows, i, :], ps[rows, Z0, :]).then_inc(ya_done, 1)

                log1p(0)
                split_hi(None, 1, i + 1, i * 4 + 4)
                fail_hi(0)
                weights(0)
                table(i, 2)
                table(i, 3)
                store(0)
                log1p(1)
                if not last:
                    evac_qk(i + 1)
                fail_hi(1)
                if not last:
                    split_hi(None, 0, i + 2, i * 4 + 6)
                weights(1)
                if not last:
                    evac_v(i + 1)
                    table(i + 1, 0)
                store(1)
                if not last:
                    values_hi(i + 1)
                    table(i + 1, 1)
                    act.wait_ge(ys_done, i + 1)
                    evac_u(i + 1)
                    act.wait_ge(bu_done, i * 4 + 4)
                    copy(Bs[:, :, :], BT[:, i + 1, :, :]).then_inc(bs_ready, 1)

            def merge():
                n = U_MERGE
                for c in range(HC):
                    act.wait_ge(ys_done, c + 1)
                    own.do(A(ys[:, c, :], ys[:, c, :], ACT.Gelu_apprx_tanh))
                own.sync()
                for c in range(HC):
                    copy(yhi[:, c, :], ys[:, c, :]).then_inc(ye_hi, 1)
                act.wait_ge(ya_done, 2 * HC)
                for c in range(HC):
                    copy(ahi[:, c, :], ya[:, c, :]).then_inc(ye_hi, 1)

                def gates(unit, branch, m):
                    for b in range(2):
                        act.wait_ge(block_done, DONE[unit] + b + 1)
                        A(gate[:, branch, m % 4 + b, :], ps[:, 2 * branch + b, :], ACT.Sigmoid,
                          bias=vec("b_gate", DC * branch + m + b)).then_inc(sig_evac, 1)
                    split_static(unit + 2)

                for k in range(4):
                    gates(n + k, k % 2, 2 * (k // 2))
                for m in range(4):
                    act.wait_ge(block_done, DONE[n + 4] + m + 1)
                    if m >= 2:
                        act.wait_ge(y2_done, m - 1)
                    A(glu[:, m % 2, :], ps[:, 4 + m, :], ACT.Sigmoid, bias=vec("b_glu", m)).then_inc(sig_evac, 1)
                split_static(n + 6)
                for m in range(HC):
                    act.wait_ge(y2_done, m + 1)
                    copy(yhi[:, m, :], ys[:, m, :]).then_inc(ye_hi, 1)

                def sums_hi(unit, m0):
                    for m in range(m0, m0 + 2):
                        act.wait_ge(mg_done, m + 1)
                        copy(mhi[:, m, :], mg[:, m % 2, :]).then_inc(mg_hi, 1)
                    split_static(unit + 2)

                sums_hi(n + 5, 0)
                sums_hi(n + 6, 2)
                for k in range(4):
                    gates(n + 7 + k, k % 2, 4 + 2 * (k // 2))
                sums_hi(n + 11, 4)
                sums_hi(n + 12, 6)
                for k in range(4):
                    split_static(U_OUT + 2 + k)

            def ff(i):
                for q in range(2):
                    n = U_FF + 4 * q
                    turn = i * 4
                    base = i * 24 + (DONE[U_FF] + 12 * q)
                    a = 4 * q
                    hid = i * 8 + 4 * q

                    def relu(m):
                        act.wait_ge(block_done, base + (m + 1))
                        A(rl[:, m % 2, :], ps[:, a + m, :], ACT.Relu).then_inc(rl_done, 1)

                    def hid_hi(m):
                        act.wait_ge(hd_done, hid + (m + 1))
                        copy(hdhi[:, m, :], hd[:, m % 2, :]).then_inc(hd_hi, 1)

                    relu(0)
                    relu(1)
                    split_hi(None, n % 2, turn + (n + 2) // 2, base + 2)
                    hid_hi(0)
                    hid_hi(1)
                    relu(2)
                    relu(3)
                    split_hi(None, (n + 1) % 2, turn + (n + 3) // 2, base + 4)
                    hid_hi(2)
                    hid_hi(3)
                    split_hi(None, n % 2, turn + (n + 4) // 2, base + 8)
                    split_hi(None, (n + 1) % 2, turn + (n + 5) // 2, base + 12)

            def gla_prepare():
                act.wait_ge(block_done, DONE[U_ALR + 1])
                copy(alr[0:16, :], ps[0:16, 0, :]).then_inc(alr_ready, 1)
                split_static(U_ALR + 2)
                for hh in range(GLA_H):
                    act.wait_ge(la_mm, hh + 1)
                    if hh >= 1:
                        act.wait_ge(cum_done, hh)
                    own.do(A(la[:, 0, :], ps[:, 4 + hh, :], ACT.Abs, bias=vec("gla_b_a", hh)))
                    own.sync()
                    own.do(A(la[:, 0, :], la[:, 0, :], ACT.Exp, scale=-1.0))
                    own.sync()
                    A(la[:, 0, :], la[:, 0, :], ACT.Ln, bias=one_b).then_inc(la_ln, 1)

            def gla_decays(i):
                act.wait_ge(cum_done, GLA_H)
                act.wait_ge(dec_in, i + 1)
                own.do(A(eq[:, :], cum[:, i, :], ACT.Exp, scale=1.0 / 16))
                own.do(A(ek[:, :], cum[:, i, :], ACT.Exp, scale=-1.0 / 16))
                A(kd[:, :], kd[:, :], ACT.Exp, scale=1.0 / 16).then_inc(dec_done, 1)

            def gla_in_hi(i):
                for k, (dst, src) in enumerate(((qihi, qin), (kihi, kin))):
                    act.wait_ge(in_done, i * 3 + (k + 1))
                    copy(dst[:, :], src[:, :]).then_inc(in_hi, 1)

            def gla_head(i, last=False):
                act.wait_ge(kd_tr, i + 1)
                copy(kdhi[:, :], ps[:, 4, :]).then_inc(kd_hi, 1)
                act.wait_ge(block_done, i * 4 + (DONE[U_GLA] + 4))
                copy(gvhi[:, :, :], flat[:, 1024:2048].rearrange("p (t c) -> p t c", t=TT)).then_inc(gv_hi, 1)
                split_hi(None, (U_GLA + 3) % 2, i + (U_GLA + 3) // 2)
                act.wait_ge(ai_done, i + 1)
                copy(aihi[:, :, :], ai[:, :, :]).then_inc(ai_hi, 1)
                for c in range(GLA_N - 1):
                    act.wait_ge(st_done, i * (GLA_N - 1) + (c + 1))
                    copy(sthi[:, c + 1, :], st[:, c % 2, :]).then_inc(st_hi, 1)
                if not last:
                    split_hi(None, U_GLA % 2, i + (U_GLA + 4) // 2, i * 4 + (DONE[U_GLA] + 6))
                for dv in range(2):
                    act.wait_ge(go_mm, i * 2 + (dv + 1))
                    A(gsq[:, dv, :], ps[:, 6 + dv, :], ACT.Square).then_inc(gsq_done, 1)
                act.wait_ge(gss_mm, i + 1)
                rsqrt_guess(g_y[:, :], g_ln[:, :], ps[:, 4, :], 1.0 / 256, gln_done, gy_done, i + 1)
                if not last:
                    gla_decays(i + 1)
                    gla_in_hi(i + 1)

            def gate_evac(n):
                for b in range(4):
                    for k in range(2):
                        act.wait_ge(block_done, DONE[n + b] + k + 1)
                        copy(gr[:, 2 * b + k, :], ps[:, 2 * (b % 2) + k, :]).then_inc(g_evac, 1)
                    split_static(n + b + 2)

            def gated_out(turn):
                act.wait_ge(g_evac, 8) if turn == 0 else act.wait_ge(g_copy, FOX_PAIRS)
                for c in range(DC):
                    A(gr[:, c, :], gr[:, c, :], ACT.Silu).then_inc(silu_done, 1)
                for c in range(DC):
                    act.wait_ge(prod_done, 8 * turn + c + 1)
                    copy(uhi[:, c, :], og[:, c, :]).then_inc(gated_hi, 1)

            def split_next(n, count):
                for k in range(count):
                    split_static(n + k)

            def ple_split(layer):
                act.wait_ge(pe_sem, 16 * layer + 16)
                for k in range(2):
                    copy(pehi[:, k, :], pe_in[:, k, :]).then_inc(pe_hi, 1)

            def ple_evac(layer, n):
                for m in range(DC):
                    act.wait_ge(block_done, DONE[n] + m + 1)
                    copy(pp[:, m, :], ps[:, 4 + m % 3, :]).then_inc(pp_done, 1)
                split_static(n + 2)

            def ple_gate(layer, n):
                for b in range(4):
                    for k in range(2):
                        m = 2 * b + k
                        act.wait_ge(block_done, DONE[n + b] + k + 1)
                        if m >= 2:
                            act.wait_ge(h_added, 80 + 16 * layer + m - 1)
                        A(sg[:, m % 2, :], ps[:, 2 * (b % 2) + k, :], ACT.Sigmoid).then_inc(sg_done, 1)
                    split_static(n + b + 2)

            tf = flat[:, 5 * 512:5 * 512 + NZ]

            def fox_prepare():
                act.wait_ge(block_done, DONE[U_F + 1])
                own.do(A(fl[:, 0, :], ps[0:16, 0, :], ACT.Identity, bias=vecs[0:16, VEC["fox_b_f"]:VEC["fox_b_f"] + 1]))
                own.sync()
                A(fl[:, 1, :], fl[:, 0, :], ACT.Abs).then_inc(f_evac, 1)
                act.wait_ge(f_evac, 1)
                own.do(A(fl[:, 1, :], fl[:, 1, :], ACT.Exp, scale=-1.0))
                own.sync()
                A(fl[:, 1, :], fl[:, 1, :], ACT.Ln, bias=biases[0:16, 1:2]).then_inc(f_ln_done, 1)
                act.wait_ge(c_ready, 1)
                copy(nchi[:, :], fl[:, 2, :]).then_inc(f_exp, 1)

            def fox_evac(i, k):
                act.wait_ge(block_done, i * 4 + (DONE[U_FOX] + 1 + k))
                copy(qk[:, k, :], ps[:, k, :]).then_inc(qk_copy, 1)

            def fox_squares(i):
                act.wait_ge(qk_copy, i * 2 + 2)
                A(qksq[:, :, :], qk[:, :, :], ACT.Square).then_inc(qk_sq, 1)

            def fox_qk_norm(i):
                act.wait_ge(qk_ss, i + 1)
                rsqrt_guess(f_y[:, :, :], f_ln[:, :, :], ps[:, Z0:Z0 + 2, :], 1.0 / 64, fln_done, fy_done, i + 1)

            def fox_qk_hi(i):
                act.wait_ge(qk_n, i + 1)
                copy(fqhi[:, :, :], qk[:, :, :]).then_inc(fq_hi, 1)

            def fox_v_evac(i):
                act.wait_ge(block_done, i * 4 + (DONE[U_FOX] + 3))
                copy(fvT[:, :], ps[:, 0, :]).then_inc(fvT_ready, 1)

            def fox_values_hi(i):
                act.wait_ge(fv_tr, i + 1)
                copy(fvhi[:, :, :], ps[:, 7, :].rearrange("p (t c) -> p t c", t=TT)).then_inc(fv_hi, 1)

            def fox_g_evac(i):
                act.wait_ge(block_done, i * 4 + (DONE[U_FOX] + 4))
                copy(gr[:, i, :], ps[:, 1, :]).then_inc(g_copy, 1)

            def fox(i, last=False):
                def exps(hh):
                    act.wait_ge(max_done, i * 2 + (hh + 1))
                    for qb in range(TT):
                        n = (qb + 1) * P
                        e = A(pr[:, QB_AT[qb]:QB_AT[qb] + n], zf[:, QB_AT[qb]:QB_AT[qb] + n], ACT.Exp,
                              bias=nmax[:, qb:qb + 1], accum_out=rsum[:, qb:qb + 1])
                        if qb == TT - 1:
                            e.then_inc(exp_done, 1)
                        else:
                            own.do(e)

                def probs_hi(hh):
                    act.wait_ge(pt_done, i * 2 + (hh + 1))
                    copy(pthi[:, :], tf).then_inc(pt_hi, 1)

                def store(hh):
                    act.wait_ge(fpv_done, i * 2 + (hh + 1))
                    rows = slice(64 * hh, 64 * hh + 64)
                    copy(og[rows, i, :], ps[rows, 5, :]).then_inc(fo_done, 1)

                exps(0)
                if not last:
                    fox_evac(i + 1, 0)
                probs_hi(0)
                exps(1)
                if not last:
                    fox_evac(i + 1, 1)
                    fox_squares(i + 1)
                store(0)
                probs_hi(1)
                if not last:
                    fox_qk_norm(i + 1)
                    split_hi(None, U_FOX % 2, i + (U_FOX + 4) // 2, i * 4 + (DONE[U_FOX] + 6))
                    fox_v_evac(i + 1)
                store(1)
                if not last:
                    fox_qk_hi(i + 1)
                    fox_values_hi(i + 1)
                    fox_g_evac(i + 1)
                    split_hi(None, (U_FOX + 1) % 2, i + (U_FOX + 5) // 2, i * 4 + (DONE[U_FOX] + 8))

            def h_from_adds(base):
                return lambda eng, c: eng.wait_ge(h_added, base + c + 1)

            act.wait_ge(x_in, 16)
            act.wait_ge(bias_ready, 1)
            act.wait_ge(cst_sem, 16 * N_CST)
            norm(0, lambda eng, c: None)
            split_static(0)
            split_static(1)
            s5_prepare()
            evac_qk(0)
            split_static(2)
            evac_v(0)
            evac_u(0)
            s5_stage()
            values_hi(0)
            table(0, 0)
            table(0, 1)
            with nc.scalar.Fori(0, HC - 1) as i:
                own.enter(i, 14)
                mixer(i)
                own.leave(HC - 1)
            mixer(HC - 1, True)
            merge()
            norm(1, h_from_adds(0))
            with nc.scalar.Fori(0, FFB // 2) as i:
                ff(i)
            norm(2, h_from_adds(64), keep=True)
            norm(3, lambda eng, c: eng.wait_ge(h_normed, c + 1))
            gla_prepare()
            gla_decays(0)
            act.wait_ge(block_done, DONE[U_GLA + 1])
            split_static(U_GLA + 2)
            gla_in_hi(0)
            with nc.scalar.Fori(0, GLA_H - 1) as i:
                own.enter(i, 2)
                gla_head(i)
                own.leave(GLA_H - 1)
            gla_head(GLA_H - 1, True)
            gate_evac(U_GLAG)
            ple_split(0)
            gated_out(0)
            split_next(U_GLAO + 2, 4)
            ple_evac(0, U_PLE0)
            norm(4, h_from_adds(72))
            ple_gate(0, U_PLE0 + 1)
            norm(5, h_from_adds(80))
            fox_prepare()
            split_static(U_F + 2)
            fox_evac(0, 0)
            fox_evac(0, 1)
            fox_squares(0)
            split_static(U_FOX + 2)
            fox_qk_norm(0)
            fox_qk_hi(0)
            fox_v_evac(0)
            fox_values_hi(0)
            fox_g_evac(0)
            split_static(U_FOX + 3)
            with nc.scalar.Fori(0, FOX_PAIRS - 1) as i:
                own.enter(i, 6)
                fox(i)
                own.leave(FOX_PAIRS - 1)
            fox(FOX_PAIRS - 1, True)
            gated_out(1)
            split_next(U_FOXO + 2, 2)
            ple_split(1)
            split_next(U_FOXO + 4, 2)
            ple_evac(1, U_PLE1)
            norm(6, h_from_adds(88))
            ple_gate(1, U_PLE1 + 1)
            norm(7, h_from_adds(96), keep=True)

        @block.vector
        def _(dve):
            own = Chain(dve, dve_own)
            V = nc.vector

            def split_lo(n, slot):
                dve.wait_ge(hi_done, n + 1)
                V.tensor_tensor(wlo[:, slot, :], wraw[:, slot, :], whi[:, slot, :], ALU.subtract).then_inc(lo_done, 1)

            def split_static(n):
                if n < NU:
                    split_lo(n, n % 2)

            def newton(y, half, tmp, out):
                own.do(V.tensor_tensor(tmp, y, y, ALU.mult))
                own.sync()
                own.do(V.scalar_tensor_tensor(tmp, tmp, -1.0, half, ALU.mult, ALU.mult))
                own.sync()
                own.do(V.scalar_tensor_tensor(out, tmp, 1.5, y, ALU.add, ALU.mult))
                own.sync()

            def norm_scale(j):
                dve.wait_ge(ln_done, j + 1)
                own.do(V.tensor_scalar(rs_half[:, :], ps[:, SS_BANK[j], :], 0.5 / D, 0.5 * EPS, ALU.mult, ALU.add))
                dve.wait_ge(y_done, j + 1)
                newton(rs_y[:, :], rs_half[:, :], rs_t[:, :], rstd[:, :])

            def norm(j, gain):
                norm_scale(j)
                u = NORM_U[j]

                def lo(c):
                    dve.wait_ge(u_hi, 8 * u + c + 1)
                    V.tensor_tensor(ulo[:, c, :], un[:, c % 2, :], uhi[:, c, :], ALU.subtract).then_inc(u_ready, 1)

                for c in range(DC):
                    if c >= 2:
                        lo(c - 2)
                        dve.wait_ge(u_ready, 8 * u + c - 1)
                    V.scalar_tensor_tensor(un[:, c % 2, :], h[:, c, :], vec(gain, c), rstd[:, :], ALU.mult,
                                           ALU.mult).then_inc(un_done, 1)
                lo(DC - 2)
                lo(DC - 1)

            def norm_keep(j, gain, dst, done):
                norm_scale(j)
                for c in range(DC):
                    V.scalar_tensor_tensor(dst[:, c, :], h[:, c, :], vec(gain, c), rstd[:, :], ALU.mult,
                                           ALU.mult).then_inc(done, 1)

            def step(ins):
                own.do(ins)
                own.sync()

            c_all = 1 / (2 * np.pi)
            c_hi = float(np.float32(np.round(c_all * 2 ** 14) / 2 ** 14))
            c_lo = float(np.float32(c_all - c_hi))

            def s5_prepare():
                r = [s5p[:, k, :] for k in range(24)]
                TTp, TS, STT = V.tensor_tensor, V.tensor_scalar, V.scalar_tensor_tensor
                dve.wait_ge(s5_exp, 1)
                own.do(TTp(r[5], r[1], r[3], ALU.mult))
                TTp(r[4], r[0], r[3], ALU.mult).then_inc(s5_arg, 1)
                dve.wait_ge(s5_arg, 1)
                step(V.tensor_copy(s5r[:, 0, :], r[5]))
                step(TTp(r[16], r[5], s5r[:, 0, :], ALU.subtract))
                step(TS(r[9], r[5], c_all, None, ALU.mult))
                step(V.tensor_copy(s5r[:, 1, :], r[9]))
                own.do(V.tensor_copy(r[7], s5r[:, 1, :]))
                own.sync()
                step(STT(r[17], s5r[:, 0, :], c_hi, r[7], ALU.mult, ALU.subtract))
                step(STT(r[17], r[16], c_hi, r[17], ALU.mult, ALU.add))
                step(STT(r[8], r[5], c_lo, r[17], ALU.mult, ALU.add))
                step(TS(r[18], r[7], ROUND, ROUND, ALU.add, ALU.subtract))
                step(TTp(r[18], r[7], r[18], ALU.subtract))
                step(TTp(r[18], r[18], r[8], ALU.add))
                step(TS(r[19], r[18], ROUND, ROUND, ALU.add, ALU.subtract))
                TTp(r[12], r[18], r[19], ALU.subtract).then_inc(s5_arg, 1)
                dve.wait_ge(s5_exp, 2)
                dve.wait_ge(s5_trig, 2)
                own.do(TTp(r[16], r[6], r[15], ALU.mult))
                own.do(TTp(r[17], r[6], r[14], ALU.mult))
                own.do(TTp(r[18], r[0], r[0], ALU.mult))
                own.do(TTp(r[19], r[1], r[1], ALU.mult))
                own.sync()
                own.do(TS(r[16], r[16], 1.0, None, ALU.subtract))
                own.do(TTp(r[18], r[18], r[19], ALU.add))
                own.sync()
                own.do(V.reciprocal(r[19], r[18]))
                own.do(TTp(r[20], r[16], r[0], ALU.mult))
                own.do(TTp(r[21], r[17], r[1], ALU.mult))
                own.do(TTp(r[22], r[17], r[0], ALU.mult))
                own.do(TTp(r[23], r[16], r[1], ALU.mult))
                own.sync()
                own.do(TTp(r[20], r[20], r[21], ALU.add))
                own.do(TTp(r[22], r[22], r[23], ALU.subtract))
                own.sync()
                own.do(TTp(r[20], r[20], r[19], ALU.mult))
                own.do(TTp(r[22], r[22], r[19], ALU.mult))
                own.sync()

                def b(k):
                    return s5b[:, k, :].rearrange("p (a c) -> p a c", a=S5_PAIRS)

                def coef(k):
                    return s5p[:, k, :].unsqueeze(2).to_broadcast([P, S5_PAIRS, 32])

                own.do(TTp(b(2), b(0), coef(20), ALU.mult))
                own.do(TTp(b(4), b(1), coef(22), ALU.mult))
                own.do(TTp(b(3), b(1), coef(20), ALU.mult))
                own.do(TTp(b(5), b(0), coef(22), ALU.mult))
                own.sync()
                TTp(b(2), b(2), b(4), ALU.subtract).then_inc(B_ready, 1)
                TTp(b(3), b(3), b(5), ALU.add).then_inc(B_ready, 1)

            def phase(i, p):
                hi_s, lo_s = s5p[:, 7, bass.ds(i * 4 + p, 1)], s5p[:, 8, bass.ds(i * 4 + p, 1)]
                a, b = ph[:, 0, :], ph[:, 1, :]
                if not (isinstance(i, int) and i == 0 and p == 0):
                    dve.wait_ge(phase_ready, i * 4 + p)
                step(V.tensor_scalar(a, tvec[:, :], hi_s, None, ALU.mult))
                step(V.tensor_scalar(b, a, ROUND, ROUND, ALU.add, ALU.subtract))
                step(V.tensor_tensor(a, a, b, ALU.subtract))
                step(V.scalar_tensor_tensor(a, tvec[:, :], lo_s, a, ALU.mult, ALU.add))
                step(V.tensor_scalar(b, a, ROUND, ROUND, ALU.add, ALU.subtract))
                V.tensor_tensor(cosT[:, p, :], a, b, ALU.subtract).then_inc(phase_ready, 1)

            Z0, S0 = 2, 5
            zf = flat[:, Z0 * 512:Z0 * 512 + NZ]

            def evac_qk(i):
                dve.wait_ge(q_hi, i * 2 + 1)
                V.scalar_tensor_tensor(qklo[:, 0, :], ps[:, 0, :], 0.125, qkhi[:, 0, :], ALU.mult,
                                       ALU.subtract).then_inc(qk_ready, 1)
                dve.wait_ge(q_hi, i * 2 + 2)
                V.tensor_tensor(qklo[:, 1, :], ps[:, 1, :], qkhi[:, 1, :], ALU.subtract).then_inc(qk_ready, 1)

            def values_lo(i):
                dve.wait_ge(v_hi, i + 1)
                V.tensor_tensor(vlo[:, :, :], ps[:, 0, :].rearrange("p (t c) -> p t c", t=TT), vhi[:, :, :],
                                ALU.subtract).then_inc(v_ready, 1)

            def mixer(i, last=False):
                def pair(p):
                    cos2 = cosT[:, p, :].unsqueeze(1).to_broadcast([P, 2, T])
                    sin2 = sinT[:, p, :].unsqueeze(1).to_broadcast([P, 2, T])
                    dve.wait_ge(bu_done, i * 4 + (p + 1))
                    dve.wait_ge(table_ready, i * 4 + (p + 1))
                    own.do(V.tensor_tensor(rin[:, :, :], ps[:, S0:S0 + 2, :], cos2, ALU.mult))
                    V.tensor_tensor(rin2[:, :, :], ps[:, S0:S0 + 2, :], sin2, ALU.mult).then_inc(bu_used, 1)
                    dve.wait_ge(bu_used, i * 4 + (p + 1))
                    own.do(V.tensor_tensor(rin[:, 0, :], rin[:, 0, :], rin2[:, 1, :], ALU.subtract))
                    own.do(V.tensor_tensor(rin[:, 1, :], rin[:, 1, :], rin2[:, 0, :], ALU.add))
                    own.sync()
                    if p >= 1:
                        dve.wait_ge(rot_out, i * 4 + p)
                    decay = s5p[:, 6, bass.ds(i * 4 + p, 1)].to_broadcast([P, T])
                    own.do(V.tensor_tensor_scan(zst[:, 0, :], decay, rin[:, 0, :], 0.0, ALU.mult, ALU.add))
                    V.tensor_tensor_scan(zst[:, 1, :], decay, rin[:, 1, :], 0.0, ALU.mult, ALU.add).then_inc(z5_done, 1)

                def softplus(hh):
                    dve.wait_ge(l_done, i * 2 + (hh + 1))
                    V.scalar_tensor_tensor(att[:, :], zf, 0.0, att[:, :], ALU.max, ALU.add).then_inc(sp_done, 1)

                def fail_lo(hh):
                    dve.wait_ge(l_hi, i * 2 + (hh + 1))
                    V.tensor_tensor(atlo[:, :], att[:, :], athi[:, :], ALU.subtract).then_inc(l_ready, 1)

                def w_lo(hh):
                    dve.wait_ge(w_hi, i * 2 + (hh + 1))
                    V.tensor_tensor(atlo[:, :], att[:, :], athi[:, :], ALU.subtract).then_inc(w_ready, 1)

                pair(0)
                softplus(0)
                fail_lo(0)
                pair(1)
                phase(i, 3)
                w_lo(0)
                split_lo(i * 2 + 3, 1)
                pair(2)
                if not last:
                    phase(i + 1, 0)
                softplus(1)
                if not last:
                    evac_qk(i + 1)
                fail_lo(1)
                pair(3)
                if not last:
                    phase(i + 1, 1)
                w_lo(1)
                if not last:
                    split_lo(i * 2 + 4, 0)
                    values_lo(i + 1)
                dve.wait_ge(y5_done, i * 4 + 4)
                V.scalar_tensor_tensor(ys[:, i, :], uch[:, :], vecs[:, bass.ds(i + VEC["D_skip"], 1)],
                                       ps[:, 7, :], ALU.mult, ALU.add).then_inc(ys_done, 1)
                if not last:
                    phase(i + 1, 2)

            def merge():
                n = U_MERGE
                for c in range(2 * HC):
                    dve.wait_ge(ye_hi, c + 1)
                    dst, src, hi = ((ylo, ys, yhi), (alo, ya, ahi))[c // HC]
                    V.tensor_tensor(dst[:, c % HC, :], src[:, c % HC, :], hi[:, c % HC, :], ALU.subtract).then_inc(y_ready, 1)
                for k in range(4):
                    split_static(n + 2 + k)
                for m in range(HC):
                    dve.wait_ge(sig_evac, 8 + m + 1)
                    V.tensor_tensor(ys[:, m, :], ys[:, m, :], glu[:, m % 2, :], ALU.mult).then_inc(y2_done, 1)
                split_static(n + 6)
                for m in range(HC):
                    dve.wait_ge(ye_hi, 2 * HC + m + 1)
                    V.tensor_tensor(ylo[:, m, :], ys[:, m, :], yhi[:, m, :], ALU.subtract).then_inc(y_ready, 1)

                def up(unit, m0, bank):
                    for m in range(m0, m0 + 2):
                        b = bank + 2 * (m - m0)
                        for br in range(2):
                            dve.wait_ge(block_done, DONE[unit] + 2 * (m - m0) + br + 1)
                            g = gate[:, br, m % 4, :]
                            V.tensor_tensor(g, ps[:, b + br, :], g, ALU.mult).then_inc(up_evac, 1)
                        dve.wait_ge(up_evac, 2 * m + 2)
                        if m >= 2:
                            dve.wait_ge(mg_ready, m - 1)
                        V.tensor_tensor(mg[:, m % 2, :], gate[:, 0, m % 4, :], gate[:, 1, m % 4, :],
                                        ALU.add).then_inc(mg_done, 1)
                        if m > m0:
                            for mm in (m - 1, m):
                                dve.wait_ge(mg_hi, mm + 1)
                                V.tensor_tensor(mlo[:, mm, :], mg[:, mm % 2, :], mhi[:, mm, :],
                                                ALU.subtract).then_inc(mg_ready, 1)
                    split_static(unit + 2)

                up(n + 5, 0, 0)
                up(n + 6, 2, 4)
                for k in range(4):
                    split_static(n + 9 + k)
                up(n + 11, 4, 4)
                up(n + 12, 6, 0)
                residual(U_OUT, (4, 6, 0, 2))

            def residual(n, banks):
                for b in range(4):
                    for k in range(2):
                        dve.wait_ge(block_done, DONE[n + b] + k + 1)
                        m = 2 * b + k
                        V.tensor_tensor(h[:, m, :], ps[:, banks[b] + k, :], h[:, m, :], ALU.add).then_inc(h_added, 1)
                    split_static(n + b + 2)

            def ff(i):
                for q in range(2):
                    n = i * 8 + (U_FF + 4 * q)
                    s = (U_FF + 4 * q) % 2
                    base = i * 24 + (DONE[U_FF] + 12 * q)
                    a, b = (0, 4) if q == 0 else (4, 0)
                    hid = i * 8 + 4 * q

                    def square(m):
                        dve.wait_ge(rl_done, hid + (m + 1))
                        if m >= 2:
                            dve.wait_ge(hd_ready, hid + (m - 1))
                        V.tensor_tensor(hd[:, m % 2, :], rl[:, m % 2, :], rl[:, m % 2, :], ALU.mult).then_inc(hd_done, 1)

                    def lo(m):
                        dve.wait_ge(hd_hi, hid + (m + 1))
                        V.tensor_tensor(hdlo[:, m, :], hd[:, m % 2, :], hdhi[:, m, :], ALU.subtract).then_inc(hd_ready, 1)

                    def add(m, bank):
                        dve.wait_ge(block_done, base + (5 + m))
                        V.tensor_tensor(h[:, m, :], ps[:, bank, :], h[:, m, :], ALU.add).then_inc(h_added, 1)

                    square(0)
                    square(1)
                    lo(0)
                    lo(1)
                    split_lo(n + 2, s)
                    square(2)
                    square(3)
                    lo(2)
                    lo(3)
                    dve.wait_ge(hd_ready, hid + 4)
                    split_lo(n + 3, 1 - s)
                    for m in range(4):
                        add(m, b + m)
                    split_lo(n + 4, s)
                    for m in range(4):
                        add(4 + m, a + m)
                    split_lo(n + 5, 1 - s)

            def gla_prepare():
                split_static(U_ALR + 2)
                for hh in range(GLA_H):
                    dve.wait_ge(la_mm, hh + 1)
                    dve.wait_ge(la_ln, hh + 1)
                    step(V.tensor_scalar(la[:, 1, :], ps[:, 4 + hh, :], vec("gla_b_a", hh), 0.0, ALU.add, ALU.min))
                    step(V.tensor_tensor(la[:, 1, :], la[:, 1, :], la[:, 0, :], ALU.subtract))
                    V.tensor_tensor_scan(cum[:, hh, :], reset[:, :], la[:, 1, :], 0.0, ALU.mult,
                                         ALU.add).then_inc(cum_done, 1)
                    dve.wait_ge(cum_done, hh + 1)

            def gla_decay_in(i):
                c3 = cum[:, i, :].rearrange("p (n c) -> p n c", c=GLA_C)
                V.tensor_tensor(kd[:, :].rearrange("p (n c) -> p n c", c=GLA_C),
                                c3[:, :, GLA_C - 1:GLA_C].to_broadcast([P, GLA_N, GLA_C]), c3,
                                ALU.subtract).then_inc(dec_in, 1)

            def gla_scale(i):
                dve.wait_ge(dec_done, i + 1)
                dve.wait_ge(block_done, i * 4 + (DONE[U_GLA] + 2))
                V.scalar_tensor_tensor(qin[:, :], ps[:, 0, :], float(P) ** -0.5, eq[:, :], ALU.mult,
                                       ALU.mult).then_inc(in_done, 1)
                V.tensor_tensor(kin[:, :], ps[:, 1, :], ek[:, :], ALU.mult).then_inc(in_done, 1)
                V.tensor_tensor(kdec[:, :], ps[:, 1, :], kd[:, :], ALU.mult).then_inc(in_done, 1)
                for k, (dst, src, hi) in enumerate(((qilo, qin, qihi), (kilo, kin, kihi))):
                    dve.wait_ge(in_hi, i * 2 + (k + 1))
                    V.tensor_tensor(dst[:, :], src[:, :], hi[:, :], ALU.subtract).then_inc(in_ready, 1)

            def gla_head(i, last=False):
                dve.wait_ge(kd_hi, i + 1)
                V.tensor_tensor(kdlo[:, :], ps[:, 4, :], kdhi[:, :], ALU.subtract).then_inc(kd_ready, 1)
                dve.wait_ge(gv_hi, i + 1)
                V.tensor_tensor(gvlo[:, :, :], flat[:, 1024:2048].rearrange("p (t c) -> p t c", t=TT), gvhi[:, :, :],
                                ALU.subtract).then_inc(gv_ready, 1)
                split_lo(i * 2 + (U_GLA + 3), (U_GLA + 3) % 2)
                dve.wait_ge(ai_mm, i + 1)
                V.tensor_copy(biases[:, 5:6], ones[:, 0:1])
                V.copy_predicated(ai[:, :, :], samechunk[:, :].bitcast(U32).unsqueeze(1).to_broadcast([P, TT, P]),
                                  ps[:, 5, :].rearrange("p (t c) -> p t c", t=TT)).then_inc(ai_done, 1)
                dve.wait_ge(ai_hi, i + 1)
                V.tensor_tensor(ailo[:, :, :], ai[:, :, :], aihi[:, :, :], ALU.subtract).then_inc(ai_ready, 1)
                NS = GLA_N - 1
                for c in range(NS):
                    dve.wait_ge(kv_mm, i * NS + min(c + 3 if c in KV_FIRST else c + 1, NS))
                    kv = kv_sums(c)
                    if c == 0:
                        V.tensor_copy(st[:, 0, :], kv).then_inc(st_done, 1)
                    else:
                        at = c * GLA_C + GLA_C - 1
                        V.scalar_tensor_tensor(st[:, c % 2, :], st[:, (c - 1) % 2, :], eq[:, at:at + 1], kv, ALU.mult,
                                               ALU.add).then_inc(st_done, 1)
                    dve.wait_ge(st_hi, i * NS + (c + 1))
                    V.tensor_tensor(stlo[:, c + 1, :], st[:, c % 2, :], sthi[:, c + 1, :], ALU.subtract).then_inc(st_ready, 1)
                    dve.wait_ge(st_ready, i * NS + (c + 1))
                if not last:
                    split_lo(i * 2 + (U_GLA + 4), U_GLA % 2)
                    gla_decay_in(i + 1)
                dve.wait_ge(gln_done, i + 1)
                own.do(V.tensor_scalar(g_half[:, :], ps[:, 4, :], 0.5 / 256, 0.5 * EPS, ALU.mult, ALU.add))
                dve.wait_ge(gy_done, i + 1)
                newton(g_y[:, :], g_half[:, :], g_t[:, :], g_y[:, :])
                for dv in range(2):
                    V.scalar_tensor_tensor(og[:, i * 2 + dv, :], ps[:, 6 + dv, :], vec("gla_o_norm", dv), g_y[:, :],
                                           ALU.mult, ALU.mult).then_inc(go_done, 1)
                if not last:
                    gla_scale(i + 1)

            def gated_out(turn):
                for c in range(DC):
                    dve.wait_ge(silu_done, 8 * turn + c + 1)
                    V.tensor_tensor(og[:, c, :], og[:, c, :], gr[:, c, :], ALU.mult).then_inc(prod_done, 1)
                for c in range(DC):
                    dve.wait_ge(gated_hi, 8 * turn + c + 1)
                    V.tensor_tensor(ulo[:, c, :], og[:, c, :], uhi[:, c, :], ALU.subtract).then_inc(gated, 1)

            def ple_split(layer):
                for k in range(2):
                    dve.wait_ge(pe_hi, 2 * layer + k + 1)
                    V.tensor_tensor(pelo[:, k, :], pe_in[:, k, :], pehi[:, k, :], ALU.subtract).then_inc(pe_ready, 1)

            def ple_gate(layer, n):
                for b in range(4):
                    for k in range(2):
                        m = 2 * b + k
                        dve.wait_ge(sg_done, 8 * layer + m + 1)
                        V.tensor_tensor(sg[:, m % 2, :], sg[:, m % 2, :], pp[:, m, :], ALU.mult).then_inc(sgp, 1)
                        dve.wait_ge(sgp, 8 * layer + m + 1)
                        V.tensor_tensor(h[:, m, :], h[:, m, :], sg[:, m % 2, :], ALU.add).then_inc(h_added, 1)
                    split_static(n + b + 2)

            tf = flat[:, 5 * 512:5 * 512 + NZ]

            def fox_prepare():
                own.do(V.tensor_scalar(gq8[:, :], vec("fox_q_norm"), 0.125, None, ALU.mult))
                dve.wait_ge(f_evac, 1)
                step(V.tensor_scalar(fl[:, 2, :], fl[:, 0, :], 0.0, None, ALU.min))
                dve.wait_ge(f_ln_done, 1)
                step(V.tensor_tensor(fl[:, 0, :], fl[:, 1, :], fl[:, 2, :], ALU.subtract))
                V.tensor_tensor_scan(fl[:, 2, :], biases[0:16, 1:2].to_broadcast([16, T]), fl[:, 0, :], 0.0, ALU.mult,
                                     ALU.add).then_inc(c_ready, 1)
                dve.wait_ge(f_exp, 1)
                step(V.tensor_tensor(nclo[:, :], fl[:, 2, :], nchi[:, :], ALU.subtract))

            def fox_qk_norm(i):
                dve.wait_ge(fln_done, i + 1)
                own.do(V.tensor_scalar(f_half[:, :, :], ps[:, Z0:Z0 + 2, :], 0.5 / 64, 0.5 * EPS, ALU.mult, ALU.add))
                dve.wait_ge(fy_done, i + 1)
                newton(f_y[:, :, :], f_half[:, :, :], f_ln[:, :, :], f_y[:, :, :])
                own.do(V.scalar_tensor_tensor(qk[:, 0, :], qk[:, 0, :], gq8[:, :], f_y[:, 0, :], ALU.mult, ALU.mult))
                V.scalar_tensor_tensor(qk[:, 1, :], qk[:, 1, :], vec("fox_k_norm"), f_y[:, 1, :], ALU.mult,
                                       ALU.mult).then_inc(qk_n, 1)

            def fox_qk_lo(i):
                dve.wait_ge(fq_hi, i + 1)
                V.tensor_tensor(fqlo[:, :, :], qk[:, :, :], fqhi[:, :, :], ALU.subtract).then_inc(fq_ready, 1)

            def fox_bias(i, hh):
                row = ident[0:16, bass.ds(i * 2 + hh, 1)]
                own.do(V.tensor_scalar(cmhi[:, :], nchi[:, :], row, None, ALU.mult))
                V.tensor_scalar(cmlo[:, :], nclo[:, :], row, None, ALU.mult).then_inc(cm_ready, 1)

            def fox_values_lo(i):
                dve.wait_ge(fv_hi, i + 1)
                V.tensor_tensor(fvlo[:, :, :], ps[:, 7, :].rearrange("p (t c) -> p t c", t=TT), fvhi[:, :, :],
                                ALU.subtract).then_inc(fv_ready, 1)

            def fox(i, last=False):
                def row_max(hh):
                    dve.wait_ge(fz_done, i * 2 + (hh + 1))
                    for qb in range(TT):
                        n = (qb + 1) * P
                        r = V.tensor_reduce(nmax[:, qb:qb + 1], zf[:, QB_AT[qb]:QB_AT[qb] + n], AX.X, ALU.max, negate=True)
                        if qb == TT - 1:
                            r.then_inc(max_done, 1)
                        else:
                            own.do(r)

                def normalise(hh):
                    dve.wait_ge(exp_done, i * 2 + (hh + 1))
                    step(V.reciprocal(rinv[:, :], rsum[:, :]))
                    for qb in range(TT):
                        at = slice(QB_AT[qb], QB_AT[qb] + (qb + 1) * P)
                        r = V.tensor_scalar(pr[:, at], pr[:, at], rinv[:, qb:qb + 1], None, ALU.mult)
                        if qb == TT - 1:
                            r.then_inc(p_done, 1)
                        else:
                            own.do(r)

                def probs_lo(hh):
                    dve.wait_ge(pt_hi, i * 2 + (hh + 1))
                    V.tensor_tensor(ptlo[:, :], tf, pthi[:, :], ALU.subtract).then_inc(pt_ready, 1)

                row_max(0)
                fox_bias(i, 1)
                normalise(0)
                probs_lo(0)
                row_max(1)
                normalise(1)
                probs_lo(1)
                if not last:
                    fox_bias(i + 1, 0)
                    fox_qk_norm(i + 1)
                    split_lo(i * 2 + (U_FOX + 4), U_FOX % 2)
                    fox_qk_lo(i + 1)
                    fox_values_lo(i + 1)
                    split_lo(i * 2 + (U_FOX + 5), (U_FOX + 1) % 2)

            dve.wait_ge(cst_sem, 16 * N_CST)
            for k, dst in enumerate((onesr, keymaskr, querymaskr, trir, negonesr)):
                V.tensor_copy(dst[:, :], cst_in[:, k, :]).then_inc(consts_ready, 1)
            V.tensor_copy(identr[:, :], ident[:, :]).then_inc(consts_ready, 1)
            dve.wait_ge(bias_ready, 1)
            norm(0, "norm_mix")
            split_static(0)
            split_static(1)
            s5_prepare()
            evac_qk(0)
            split_static(2)
            dve.wait_ge(BT_done, 1)
            for p in range(3):
                phase(0, p)
            values_lo(0)
            with nc.vector.Fori(0, HC - 1) as i:
                own.enter(i, 36)
                mixer(i)
                own.leave(HC - 1)
            mixer(HC - 1, True)
            merge()
            norm(1, "norm_mlp")
            with nc.vector.Fori(0, FFB // 2) as i:
                ff(i)
            norm_keep(2, "norm_final", h, h_normed)
            norm(3, "norm_mixer0")
            V.memset(ai[:, :, :], 0.0)
            gla_prepare()
            gla_decay_in(0)
            split_static(U_GLA + 2)
            gla_scale(0)
            with nc.vector.Fori(0, GLA_H - 1) as i:
                own.enter(i, 4)
                gla_head(i)
                own.leave(GLA_H - 1)
            gla_head(GLA_H - 1, True)
            for k in range(4):
                split_static(U_GLAG + 2 + k)
            gated_out(0)
            residual(U_GLAO, (0, 2, 0, 2))
            ple_split(0)
            split_static(U_PLE0 + 2)
            norm(4, "ple_norm0")
            ple_gate(0, U_PLE0 + 1)
            norm(5, "norm_mixer1")
            fox_prepare()
            split_static(U_F + 2)
            split_static(U_FOX + 2)
            fox_bias(0, 0)
            fox_qk_norm(0)
            fox_qk_lo(0)
            fox_values_lo(0)
            split_static(U_FOX + 3)
            with nc.vector.Fori(0, FOX_PAIRS - 1) as i:
                own.enter(i, 21)
                fox(i)
                own.leave(FOX_PAIRS - 1)
            fox(FOX_PAIRS - 1, True)
            gated_out(1)
            residual(U_FOXO, (0, 2, 0, 2))
            ple_split(1)
            split_static(U_PLE1 + 2)
            norm(6, "ple_norm1")
            ple_gate(1, U_PLE1 + 1)
            norm_keep(7, "final_norm", pp, out_ready)


def pack_unit(w):
    k = w.shape[0] // P
    return w.reshape(k, P, w.shape[1]).transpose(1, 0, 2).reshape(P, UW)


def weight_units(a):
    def cols(w, c, n=256):
        return pack_unit(w[:, c:c + n])

    def pairs(w, *starts):
        return pack_unit(np.concatenate([w[:, c:c + P] for c in starts], axis=1))

    def padded(w):
        return pack_unit(np.concatenate([w, np.zeros((D, 256 - w.shape[1]), w.dtype)], axis=1))

    w_in, w_gate = a["w_in"][0], a["w_gate"][0]
    up = np.concatenate([a["w_up_ssm"][0], a["w_up_attn"][0]], axis=0)
    ff1, ff2 = a["w_ff1"][0], a["w_ff2"][0]
    gla, fox = a["gla_w_in_2"][0], a["fox_w_in_2"][0]
    for c in range(HC):
        yield pairs(w_in, DH + c * P, 2 * DH + c * P)
        yield pairs(w_in, 3 * DH + c * P, c * P)
    for half in range(2):
        for c in (512 * half, 512 * half + 256):
            yield cols(w_gate, c)
            yield cols(w_gate, D + c)
        if half == 0:
            yield pack_unit(a["w_glu"][0])
        for c in (512 * half, 512 * half + 256):
            yield cols(up, c)
    for c in range(4):
        yield cols(a["w_out"][0], 256 * c)
    for b in range(FFB):
        yield cols(ff1, 512 * b)
        yield cols(ff1, 512 * b + 256)
        yield cols(ff2[512 * b:512 * b + 512], 0, 512)
        yield cols(ff2[512 * b:512 * b + 512], 512, 512)
    yield padded(gla[:, 3072:3088])
    for hh in range(GLA_H):
        yield pairs(gla, hh * P, 512 + hh * P)
        yield cols(gla, 1024 + 256 * hh)
    for c in range(4):
        yield cols(gla, 2048 + 256 * c)
    for c in range(4):
        yield cols(a["gla_w_out_2"][0], 256 * c)
    for layer in range(2):
        if layer == 1:
            yield padded(fox[:, 4096:4112])
            for c in range(FOX_PAIRS):
                yield pairs(fox, c * P, D + c * P)
                yield pairs(fox, 2 * D + c * P, 3 * D + c * P)
            for c in range(4):
                yield cols(a["fox_w_out_2"][0], 256 * c)
        yield pack_unit(a["ple_proj_2"][layer])
        for c in range(4):
            yield cols(a["ple_gate_2"][layer], 256 * c)


def constants():
    p, f = np.arange(P)[:, None], np.arange(P)[None, :]
    t = np.arange(T)[None, :].repeat(P, 0)
    parts = {
        "ident": p == f, "ones": np.ones((P, P)), "keymask": np.where(p >= f, NEG, 0.0),
        "querymask": np.where(f > p, NEG, 0.0), "tri": np.where(p >= f, -1.0, 0.0), "negones": -np.ones((P, P)),
        "headones": p // 64 == f // 64, "samechunk": (p // GLA_C == f // GLA_C) & (f >= p),
        "reset": t % GLA_C != 0, "tvec": t,
    }
    return np.concatenate([np.asarray(parts[n], np.float32) for n in CST], axis=1)


def fm(x):
    return np.ascontiguousarray(x.T.reshape(-1, P, x.shape[0]).transpose(1, 0, 2))


def packed_vectors(a):
    out = np.zeros((P, NVEC), np.float32)

    def put(name, v):
        v = v.reshape(-1, P).T
        out[:, VEC[name]:VEC[name] + v.shape[1]] = v

    put("norm_mix", a["norm_mix"][0])
    put("norm_mlp", a["norm_mlp"][0])
    put("norm_final", a["norm_final"])
    put("norm_mixer0", a["norm_mixer_2"][0])
    put("norm_mixer1", a["norm_mixer_2"][1])
    put("ple_norm0", a["ple_norm_2"][0])
    put("ple_norm1", a["ple_norm_2"][1])
    put("final_norm", a["final_norm_2"])
    put("D_skip", a["D_skip"][0])
    put("b_glu", a["b_glu"][0])
    put("b_gate", a["b_gate"][0])
    put("gla_b_a", a["gla_b_a_2"][0])
    put("gla_o_norm", a["gla_o_norm_2"][0])
    put("fox_q_norm", np.concatenate([a["fox_q_norm_2"][0]] * 2))
    put("fox_k_norm", np.concatenate([a["fox_k_norm_2"][0]] * 2))
    out[0:16, VEC["fox_b_f"]] = a["fox_b_f_2"][0]
    return out


def s5_layout(a):
    def states(x):
        return x.reshape(S5_PAIRS, P).T

    params = [states(a["A_re"][0]), states(a["A_im"][0]), states(np.repeat(a["log_dt"][0], 64))]
    for b in (a["B_re"][0], a["B_im"][0]):
        tile = np.zeros((P, S5_PAIRS, 32), np.float32)
        for g in range(2):
            tile[64 * g:64 * g + 64, :, 16 * g:16 * g + 16] = b[g::2].transpose(1, 0, 2)
        params.append(tile.reshape(P, -1))
    c_tiles = np.zeros((HC, P, 4, 2, P), np.float32)
    for r, c in enumerate((a["C_re"][0], a["C_im"][0])):
        for g in range(32):
            chunk, pair, half = g // 8, (g // 2) % 4, g % 2
            at = 32 * pair + 16 * half
            c_tiles[chunk, 64 * half:64 * half + 64, pair, r, at:at + 16] = c[g].T
    return np.concatenate(params, axis=1), c_tiles.reshape(HC, P, -1)


def kernel(**inputs):
    import concourse.bacc as bacc
    from concourse.bass_utils import run_bass_kernel_spmd

    a = {k: np.asarray(v) for k, v in inputs.items()}
    s5p, cpad = s5_layout(a)
    arrays = {
        "wstream": np.stack(list(weight_units(a))), "xT": fm(a["x"][0]),
        "pT": np.stack([fm(a["p_2"][layer, 0]) for layer in range(2)]), "vecs_d": packed_vectors(a), "cst_d": constants(),
        "s5p_d": s5p, "cpad_d": cpad, "wa2_d": np.ascontiguousarray(a["gla_w_a2_2"][0]),
    }
    nc = bacc.Bacc("TRN2", target_bir_lowering=False, num_devices=1)
    args = [nc.dram_tensor(n, v.shape, mybir.dt.from_np(v.dtype), kind="ExternalInput").ap() for n, v in arrays.items()]
    args.append(nc.dram_tensor("outT", (P, DC, T), F32, kind="ExternalOutput").ap())
    build(nc, *args)
    r = run_bass_kernel_spmd(nc, [arrays], core_ids=[0])
    out = np.asarray(r.results[0]["outT"])
    return np.ascontiguousarray(out.transpose(2, 1, 0).reshape(1, T, D))
```

```python
from contextlib import ExitStack

import concourse.bass as bass
import concourse.mybir as mybir
import numpy as np

F32 = mybir.dt.float32
F32R = mybir.dt.float32r
U32 = mybir.dt.uint32
I32 = mybir.dt.int32
ALU = mybir.AluOpType
ACT = mybir.ActivationFunctionType
AX = mybir.AxisListType

P = 128
T = 512
D = 1024
DC = D // P
TT = T // P
DH = 512
HC = DH // P
FFB = 8
S5_PAIRS = 16
GLA_H = 4
GLA_N = 8
GLA_C = 64
FOX_PAIRS = 8
EPS = 1e-6
NEG = -1e30
ROUND = 12582912.0
TWO_PI = float(np.nextafter(np.float32(2 * np.pi), np.float32(0)))
UW = 2048

U_MIX, N_MIX = 0, 8
U_MERGE = U_MIX + N_MIX
MERGE_BLOCKS = [2, 2, 4, 2, 2, 4, 4, 2, 2, 2, 2, 4, 4]
U_OUT = U_MERGE + len(MERGE_BLOCKS)
U_FF = U_OUT + 4
U_ALR = U_FF + 4 * FFB
U_GLA = U_ALR + 1
U_GLAG = U_GLA + 2 * GLA_H
U_GLAO = U_GLAG + 4
U_PLE0 = U_GLAO + 4
U_F = U_PLE0 + 5
U_FOX = U_F + 1
U_FOXO = U_FOX + 2 * FOX_PAIRS
U_PLE1 = U_FOXO + 4
NU = U_PLE1 + 5
BLOCKS = ([2] * N_MIX + MERGE_BLOCKS + [2] * 4 + [2, 2, 4, 4] * FFB + [1] + [2] * (2 * GLA_H + 8)
          + [8, 2, 2, 2, 2] + [1] + [2] * (2 * FOX_PAIRS + 4) + [8, 2, 2, 2, 2])
DONE = [0]
for _b in BLOCKS:
    DONE.append(DONE[-1] + _b)
assert len(BLOCKS) == NU

VEC = {}
_at = 0
for _name, _w in [("norm_mix", 8), ("norm_mlp", 8), ("norm_final", 8), ("norm_mixer0", 8), ("ple_norm0", 8),
                  ("norm_mixer1", 8), ("ple_norm1", 8), ("final_norm", 8), ("D_skip", 4), ("b_glu", 4),
                  ("b_gate", 16), ("gla_b_a", 4), ("gla_o_norm", 2), ("fox_q_norm", 1), ("fox_k_norm", 1),
                  ("fox_b_f", 1)]:
    VEC[_name] = _at
    _at += _w
NVEC = _at
CST = {}
_at = 0
for _name, _w in [("ident", P), ("ones", P), ("keymask", P), ("querymask", P), ("tri", P), ("negones", P),
                  ("headones", P), ("samechunk", P), ("reset", T), ("tvec", T)]:
    CST[_name] = (_at, _at + _w)
    _at += _w
NCST = _at

KB_AT = {0: 0, 1: 512, 3: 896, 2: 1024}
QB_AT = {3: 0, 2: 512, 0: 896, 1: 1024}
NZ = 1280
QB_GROUPS = ((3,), (2, 0), (1,))
QB_COL = {3: 0, 2: 1, 0: 2, 1: 3}


class Chain:

    def __init__(self, eng, sem):
        self.eng, self.sem, self.base, self.n = eng, sem, 0, 0

    def do(self, ins):
        ins.then_inc(self.sem, 1)
        self.n += 1

    def sync(self):
        self.eng.wait_ge(self.sem, self.base + self.n)

    def enter(self, i, per):
        self.start, self.per = self.base + self.n, per
        self.base, self.n = i * per + self.start, 0

    def leave(self, count):
        assert self.n == self.per, (self.sem.name, self.n)
        self.base, self.n = self.start + self.per * count, 0


def build(nc, wstream, xT, pT, vecs_d, cst_d, s5p_d, cpad_d, wa2_d, outT):
    ctx = ExitStack()
    with ctx:
        def sb(name, shape, dt=F32, stack=ctx):
            return stack.enter_context(nc.sbuf_tensor(name, shape, dt))

        def sem(name):
            return ctx.enter_context(nc.semaphore(name))

        h = sb("h", [P, DC, T])
        uhi = sb("uhi", [P, DC, T], F32R)
        ulo = sb("ulo", [P, DC, T], F32R)
        wraw = sb("wraw", [P, 2, UW])
        whi = sb("whi", [P, 2, UW], F32R)
        wlo = sb("wlo", [P, 2, UW], F32R)
        vecs = sb("vecs", [P, NVEC])
        ident = sb("ident", [P, P])
        ones = sb("ones", [P, P])
        headones = sb("headones", [P, P])
        identr = sb("identr", [P, P], F32R)
        onesr = sb("onesr", [P, P], F32R)
        keymaskr = sb("keymaskr", [P, P], F32R)
        querymaskr = sb("querymaskr", [P, P], F32R)
        trir = sb("trir", [P, P], F32R)
        negonesr = sb("negonesr", [P, P], F32R)
        samechunk = sb("samechunk", [P, P])
        reset = sb("reset", [P, T])
        rs_half, rs_y, rs_t, rstd = (sb(n, [P, 2, TT]) for n in ("rs_half", "rs_y", "rs_t", "rstd"))
        g12 = sb("g12", [P, DC])
        biases = sb("biases", [P, 7])
        eps_b, one_b, halfpi_b, zero_b = (biases[:, k:k + 1] for k in range(4))

        def vec(name, c=0):
            return vecs[:, VEC[name] + c:VEC[name] + c + 1]

        def scope():
            return ExitStack()

        wa2 = sb("wa2", [16, T])
        s5r = sb("s5r", [P, 2, S5_PAIRS], F32R)

        with scope() as m:
            ys = sb("ys", [P, HC, T], F32, m)
            ya = sb("ya", [P, HC, T], F32, m)
            with scope() as e:
                tvec = sb("tvec", [P, T], F32, e)
                s5p = sb("s5p", [P, 24, S5_PAIRS], F32, e)
                BT = sb("BT", [P, HC, 2, P], F32, e)
                Bs = sb("Bs", [P, 2, P], F32, e)
                Cs = sb("Cs", [P, 4, 2, P], F32, e)
                Cn = sb("Cn", [P, 4, P], F32, e)
                uch = sb("uch", [P, T], F32, e)
                vT = sb("vT", [P, T], F32, e)
                qkhi = sb("qkhi", [P, 2, T], F32R, e)
                qklo = sb("qklo", [P, 2, T], F32R, e)
                with scope() as s:
                    sq = sb("sq", [P, 2, T], F32, s)
                    un = sb("un", [P, 2, T], F32, s)
                    acc = sb("acc", [P, T], F32, s)
                    with scope() as pl:
                        pe_in = sb("pe_in", [P, 2, T], F32, pl)
                        pehi = sb("pehi", [P, 2, T], F32R, pl)
                        pelo = sb("pelo", [P, 2, T], F32R, pl)
                        pp = sb("pp", [P, DC, T], F32, pl)
                        sg = sb("sg", [P, 2, T], F32, pl)
                    sq2, acc2 = un, pp[:, 6, :]
                    cst_in = sb("cst_in", [P, 5, P], F32, s)
                    s5b = sb("s5b", [P, 6, 512], F32, s)
                with scope() as s:
                    vhi = sb("vhi", [P, TT, P], F32R, s)
                    vlo = sb("vlo", [P, TT, P], F32R, s)
                    att = sb("att", [P, NZ], F32, s)
                    athi = sb("athi", [P, NZ], F32R, s)
                    atlo = sb("atlo", [P, NZ], F32R, s)
                    cosT = sb("cosT", [P, 4, T], F32, s)
                    sinT = sb("sinT", [P, 4, T], F32, s)
                    ph = sb("ph", [P, 2, T], F32, s)
                    rin = sb("rin", [P, 2, T], F32, s)
                    rin2 = sb("rin2", [P, 2, T], F32, s)
                    zst = sb("zst", [P, 2, T], F32, s)
                    rout1 = sb("rout1", [P, 2, T], F32, s)
                    rout2 = sb("rout2", [P, 2, T], F32, s)
            with scope() as s:
                yhi = sb("yhi", [P, HC, T], F32R, s)
                ylo = sb("ylo", [P, HC, T], F32R, s)
                ahi = sb("ahi", [P, HC, T], F32R, s)
                alo = sb("alo", [P, HC, T], F32R, s)
                gate = sb("gate", [P, 2, 4, T], F32, s)
                glu = sb("glu", [P, 2, T], F32, s)
                mg = glu
                mhi = sb("mhi", [P, DC, T], F32R, s)
                mlo = sb("mlo", [P, DC, T], F32R, s)
        with scope() as s:
            rl = sb("rl", [P, 2, T], F32, s)
            hd = sb("hd", [P, 2, T], F32, s)
            hdhi = sb("hdhi", [P, 4, T], F32R, s)
            hdlo = sb("hdlo", [P, 4, T], F32R, s)
        with scope() as m:
            og = sb("og", [P, DC, T], F32, m)
            gr = sb("gr", [P, DC, T], F32, m)
            with scope() as s:
                alr = sb("alr", [P, T], F32, s)
                cum = sb("cum", [P, GLA_H, T], F32, s)
                eq = sb("eq", [P, T], F32, s)
                ek = sb("ek", [P, T], F32, s)
                kd = sb("kd", [P, T], F32, s)
                qin = sb("qin", [P, T], F32, s)
                kin = sb("kin", [P, T], F32, s)
                kdec = sb("kdec", [P, T], F32, s)
                qzhi = sb("qzhi", [P, TT, 4, GLA_C], F32R, s)
                qzlo = sb("qzlo", [P, TT, 4, GLA_C], F32R, s)
                kihi = sb("kihi", [P, T], F32R, s)
                kilo = sb("kilo", [P, T], F32R, s)
                kdhi = sb("kdhi", [P, T], F32R, s)
                kdlo = sb("kdlo", [P, T], F32R, s)
                gvhi = sb("gvhi", [P, TT, 256], F32R, s)
                gvlo = sb("gvlo", [P, TT, 256], F32R, s)
                ai = sb("ai", [P, TT, P], F32, s)
                aihi = sb("aihi", [P, TT, P], F32R, s)
                ailo = sb("ailo", [P, TT, P], F32R, s)
                st = sb("st", [P, 2, 256], F32, s)
                sthi = sb("sthi", [P, GLA_N, 256], F32R, s)
                stlo = sb("stlo", [P, GLA_N, 256], F32R, s)
                otm = gr[:, 4:6, :].rearrange("p a t -> p (a t)").rearrange("p (t c) -> p t c", c=256)
                gsq = gr[:, 6, 0:256]
                gss, g_half, g_t, g_y = (sb(n, [P, TT], F32, s) for n in ("gss", "g_half", "g_t", "g_y"))
            with scope() as s:
                fl = sb("fl", [16, 3, T], F32, s)
                nchi = sb("nchi", [16, T], F32R, s)
                nclo = sb("nclo", [16, T], F32R, s)
                cmhi = sb("cmhi", [16, T], F32R, s)
                cmlo = sb("cmlo", [16, T], F32R, s)
                gq8 = sb("gq8", [P, 1], F32, s)
                qk = sb("qk", [P, 2, T], F32, s)
                qksq = sb("qksq", [P, 2, T], F32, s)
                f_t = sb("f_t", [P, 2, T], F32, s)
                f_half = sb("f_half", [P, 2, T], F32, s)
                f_y = sb("f_y", [P, 2, T], F32, s)
                fqhi = sb("fqhi", [P, 2, T], F32R, s)
                fqlo = sb("fqlo", [P, 2, T], F32R, s)
                fvT = sb("fvT", [P, T], F32, s)
                fvhi = sb("fvhi", [P, TT, P], F32R, s)
                fvlo = sb("fvlo", [P, TT, P], F32R, s)
                pr = sb("pr", [P, NZ], F32, s)
                pthi = sb("pthi", [P, NZ], F32R, s)
                ptlo = sb("ptlo", [P, NZ], F32R, s)
                nmax = sb("nmax", [P, TT], F32, s)
                rsum = sb("rsum", [P, TT], F32, s)
                rinv = sb("rinv", [P, TT], F32, s)
        ps = ctx.enter_context(nc.psum_tensor("ps", [P, 8, 512], F32))
        flat = ps[:, :, :].rearrange("p b n -> p (b n)")
        SS_BANK = (7, 4, 7, 7, 7, 7, 7)
        RMS_BANK2 = 3
        H_BASE = (None, 0, 64, 72, 80, 88, 96)
        BOTH = 2
        N_CST = 10
        X_PARTS = 4


        KV_FIRST = (0, 1, 4)

        def kv_sums(c):
            return ps[:, (6, 7, 2, 3)[2 * (c // 4) + c % 2], (c // 2) % 2 * 256:(c // 2) % 2 * 256 + 256]

        x_in = [sem(f"x_in{k}") for k in range(X_PARTS)]
        first_in, cst_sem, par_in, pe_sem = sem("vectors_in"), sem("consts_in"), sem("params_in"), sem("ple_in")
        B_in = sem("b_matrix_in")
        cs_in = sem("c_matrix_in")
        out_sem = sem("out_stored")
        landed = [sem("weights_landed0"), sem("weights_landed1")]
        hi_done, lo_done = sem("weights_hi_done"), sem("weights_lo_done")
        block_done = sem("block_done")
        act_own, dve_own, pool_own = sem("act_own_steps"), sem("dve_own_steps"), sem("pool_own_steps")
        consts_ready, bias_ready = sem("consts_ready"), sem("bias_ready")
        sq_done, acc_done, ss_done = sem("norm_squares"), sem("norm_chunk_sums"), sem("norm_sums")
        sq2_done, acc2_done = sem("norm2_squares"), sem("norm2_chunk_sums")
        rs_done, bc_done = sem("norm_rms"), sem("norm_rms_spread")
        un_done, u_hi, u_ready = sem("norm_scaled"), sem("norm_hi"), sem("u_ready")
        gss_done, fln_done, fy_done = sem("gla_sums"), sem("fox_norm_log"), sem("fox_norm_guess")
        h_added = sem("h_added")
        h_normed = sem("h_normed")
        s5_exp, s5_arg, s5_trig = sem("s5_exp"), sem("s5_arg"), sem("s5_trig")
        B_ready, BT_done = sem("s5_B_scaled"), sem("s5_B_transposed")
        bs_ready, nim_ready = sem("s5_B_staged"), sem("s5_C_ready")
        q_hi, qk_ready, vT_ready, uch_ready = sem("qk_hi"), sem("qk_ready"), sem("vT_ready"), sem("u_ssm_ready")
        v_tr, v_hi, v_ready = sem("v_transposed"), sem("v_hi"), sem("v_ready")
        phase_ready, table_ready = sem("s5_phase"), sem("s5_tables")
        bu_done, bu_used, z5_done, z5_used, rot_out, y5_done, ys_done = (sem("s5_" + n) for n in (
            "bu", "bu_used", "state", "state_used", "rotated", "y", "chunk"))
        z_done, l_done, sp_done, l_hi, l_ready, tri_done = (sem("att_" + n) for n in (
            "scores", "log1p", "softplus", "fail_hi", "fail_ready", "logw"))
        w_hi, w_ready, pv_done, ya_done = sem("att_w_hi"), sem("att_w_ready"), sem("att_out"), sem("att_stored")
        ye_hi, y_ready, sig_evac, y2_mult, up_evac, mg_done, mg_hi, mg_ready = (sem("merge_" + n) for n in (
            "hi", "branch_ready", "sigmoid", "glu", "up", "sum", "sum_hi", "sum_ready"))
        rl_done, hd_done, hd_hi, hd_ready = sem("relu_done"), sem("hid_done"), sem("hid_hi"), sem("hid_ready")
        alr_ready, la_mm, la_abs, la_ln, cum_done = (sem("gla_" + n) for n in (
            "lowrank", "gate_logits", "gate_evac", "gate_log", "cum"))
        dec_in, dec_done, in_done, in_hi, in_ready = (sem("gla_" + n) for n in (
            "decay_in", "decays", "scaled", "scaled_hi", "scaled_ready"))
        kd_tr, kd_hi, kd_ready, gv_hi, gv_ready = (sem("gla_" + n) for n in (
            "k_transposed", "k_hi", "k_ready", "v_hi", "v_ready"))
        ai_mm, ai_done, ai_hi, ai_ready = (sem("gla_" + n) for n in ("attn", "attn_masked", "attn_hi", "attn_ready"))
        kv_mm, st_done, st_hi, st_ready = (sem("gla_" + n) for n in ("kv", "state", "state_hi", "state_ready"))
        go_mm, otm_done, ot_done, go_done = (sem("gla_" + n) for n in (
            "out", "out_normed", "out_transposed", "stored"))
        g_evac, prod_done, gated, gated_hi = (sem("gate_" + n) for n in ("silu", "product", "u", "u_hi"))
        fox_silu, gate_copied = sem("fox_silu"), sem("gate_logits_copied")
        f_evac, f_ln_done, c_ready, f_exp = (sem("fox_" + n) for n in ("f_in", "f_log", "c_ready", "bias_hi"))
        qk_copy, qk_sq, qk_ss, qk_n, fq_hi, fq_ready = (sem("fox_" + n) for n in (
            "qk", "squares", "sums", "qk_normed", "qk_hi", "qk_ready"))
        fvT_ready, g_copy, fv_tr, fv_hi, fv_ready = (sem("fox_" + n) for n in ("vT", "g", "v_transposed", "v_hi", "v_ready"))
        cm_ready, fz_done, max_done, exp_done, p_done, pt_done, pt_hi, pt_ready, fpv_done, fo_done = (
            sem("fox_" + n) for n in ("bias", "scores", "max", "exp", "probs", "transposed", "probs_hi", "probs_ready",
                                      "pv", "stored"))
        pe_hi, pe_ready, pp_done, sg_done = sem("ple_hi"), sem("ple_ready"), sem("ple_proj"), sem("ple_sigmoid")
        sgp = sem("ple_gated")
        out_ready = sem("out_ready")

        def norm_chunk_sum(waits, eng, j, c):
            waits.wait_ge(sq_done, DC * j + c + 1)
            if c >= 2:
                waits.wait_ge(acc_done, (DC - 1) * j + c - 1)
            eng.tensor_tensor(acc[:, :], sq[:, 0, :] if c == 1 else acc[:, :], sq[:, c % 2, :], ALU.add).then_inc(acc_done, 1)

        def norm_chunk_sums(waits, eng, j):
            for c in range(1, DC - 1):
                norm_chunk_sum(waits, eng, j, c)

        block = ctx.enter_context(nc.Block())

        @block.sync
        def _(sp):
            sp.dma_start(s5p[:, 0:3, :], s5p_d[:, 0:48].rearrange("p (a b) -> p a b", a=3)).then_inc(par_in, 16)
            a, b = CST["ones"]
            sp.dma_start(ones[:, :], cst_d[:, a:b]).then_inc(first_in, 16)
            for k in range(X_PARTS):
                c = slice(k * DC // X_PARTS, (k + 1) * DC // X_PARTS)
                sp.dma_start(h[:, c, :], xT[:, c, :]).then_inc(x_in[k], 16)
            sp.dma_start(vecs[:, :], vecs_d).then_inc(first_in, 16)
            a, b = CST["ident"]
            sp.dma_start(ident[:, :], cst_d[:, a:b]).then_inc(first_in, 16)
            for n in range(2):
                sp.dma_start(wraw[:, n, :], wstream[n]).then_inc(landed[n], 16)
            sp.dma_start(s5b[:, 0:2, :], s5p_d[:, 48:].rearrange("p (a b) -> p a b", a=2)).then_inc(B_in, 16)
            for name, dst in (("headones", headones), ("samechunk", samechunk), ("reset", reset),
                              ("tvec", tvec)):
                a, b = CST[name]
                sp.dma_start(dst[:, :], cst_d[:, a:b]).then_inc(cst_sem, 16)
            for k, name in enumerate(("ones", "keymask", "querymask", "tri", "negones")):
                a, b = CST[name]
                sp.dma_start(cst_in[:, k, :], cst_d[:, a:b]).then_inc(cst_sem, 16)
            sp.dma_start(wa2[:, :], wa2_d).then_inc(cst_sem, 16)
            with nc.sync.Fori(0, (NU - 3) // 2) as i:
                for n in range(2):
                    sp.wait_ge(lo_done, i * 2 + (n + 1))
                    sp.dma_start(wraw[:, n, :], wstream[i * 2 + (n + 2)]).then_inc(landed[n], 16)
            sp.wait_ge(lo_done, NU - 2)
            sp.dma_start(wraw[:, 0, :], wstream[NU - 1]).then_inc(landed[0], 16)
            for c in range(DC):
                sp.wait_ge(out_ready, c + 1)
                sp.dma_start(outT[:, c, :], pp[:, c, :]).then_inc(out_sem, 16)
            sp.wait_ge(out_sem, 16 * DC)

        assert NU % 2 == 1

        @block.gpsimd
        def _(pool):
            own = Chain(pool, pool_own)

            def load_c(i):
                pool.dma_start(Cs[:, :, :, :], cpad_d[i].rearrange("p (a b c) -> p a b c", a=4, b=2)).then_inc(cs_in, 16)

            def negate_c(i):
                pool.wait_ge(cs_in, i * 16 + 16)
                nc.gpsimd.tensor_tensor(Cn[:, :, :], Cs[:, :, 1, :], biases[:, 4:5].unsqueeze(2).to_broadcast([P, 4, P]),
                                        ALU.mult).then_inc(nim_ready, 1)

            def split_lo(n, slot):
                pool.wait_ge(hi_done, n + 1)
                nc.gpsimd.tensor_tensor(wlo[:, slot, :], wraw[:, slot, :], whi[:, slot, :], ALU.subtract).then_inc(lo_done, 1)

            def mixer(i, last=False):
                for p in range(4):
                    pool.wait_ge(z5_done, i * 4 + (p + 1))
                    pool.wait_ge(table_ready, i * 4 + (p + 1))
                    if p >= 1:
                        pool.wait_ge(y5_done, i * 4 + p)
                    own.do(nc.gpsimd.tensor_tensor(rout1[:, :, :], zst[:, :, :],
                                                   cosT[:, p, :].unsqueeze(1).to_broadcast([P, 2, T]), ALU.mult))
                    nc.gpsimd.tensor_tensor(rout2[:, :, :], zst[:, :, :],
                                            sinT[:, p, :].unsqueeze(1).to_broadcast([P, 2, T]), ALU.mult).then_inc(z5_used, 1)
                    pool.wait_ge(z5_used, i * 4 + (p + 1))
                    nc.gpsimd.tensor_tensor(rout1[:, 0, :], rout1[:, 0, :], rout2[:, 1, :], ALU.add)
                    nc.gpsimd.tensor_tensor(rout1[:, 1, :], rout1[:, 1, :], rout2[:, 0, :], ALU.subtract).then_inc(rot_out, 1)
                    if p == 0:
                        split_lo(i * 2 + 3, 1)
                    if p == 2:
                        split_lo(i * 2 + 4, 0)
                if not last:
                    pool.wait_ge(y5_done, i * 4 + 4)
                    load_c(i + 1)
                    negate_c(i + 1)

            nc.gpsimd.memset(biases[:, 0:1], EPS)
            nc.gpsimd.memset(biases[:, 1:2], 1.0)
            nc.gpsimd.memset(biases[:, 2:3], float(np.pi / 2))
            nc.gpsimd.memset(biases[:, 3:4], 0.0)
            nc.gpsimd.memset(biases[:, 4:5], -1.0).then_inc(bias_ready, 1)
            pool.wait_ge(bias_ready, 1)
            load_c(0)
            negate_c(0)
            with nc.gpsimd.Fori(0, HC - 1) as i:
                own.enter(i, 4)
                mixer(i)
                own.leave(HC - 1)
            mixer(HC - 1, True)
            norm_chunk_sums(pool, nc.gpsimd, 1)
            for c in range(1, DC):
                pool.wait_ge(sq2_done, c + 1)
                if c >= 2:
                    pool.wait_ge(acc2_done, c - 1)
                nc.gpsimd.tensor_tensor(acc2, sq2[:, 0, :] if c == 1 else acc2, sq2[:, c % 2, :],
                                        ALU.add).then_inc(acc2_done, 1)
            pool.wait_ge(go_done, 2 * GLA_H)
            pool.dma_start(pe_in[:, :, :], pT[0]).then_inc(pe_sem, 16)
            norm_chunk_sums(pool, nc.gpsimd, 3)
            norm_chunk_sums(pool, nc.gpsimd, 4)
            pool.wait_ge(fo_done, 2 * FOX_PAIRS)
            pool.dma_start(pe_in[:, :, :], pT[1]).then_inc(pe_sem, 16)
            norm_chunk_sums(pool, nc.gpsimd, 5)
            norm_chunk_sums(pool, nc.gpsimd, 6)

        @block.tensor
        def _(pe):
            def three(out, lh, ll, rh, rl_, start, stop=False, done=None):
                nc.tensor.matmul(out, lh, rh, start=start, stop=False, skip_group_check=True)
                nc.tensor.matmul(out, lh, rl_, start=False, stop=False, skip_group_check=True)
                mm = nc.tensor.matmul(out, ll, rh, start=False, stop=stop, skip_group_check=True)
                if done is not None:
                    mm.then_inc(done, 1)

            def gemm(n, slot, blocks, cols, hi, lo, by_k=False, k_wait=None, part=None):
                pe.wait_ge(lo_done, n + 1)
                wh = whi[:, slot, :].rearrange("p (k c) -> p k c", c=cols)
                wl = wlo[:, slot, :].rearrange("p (k c) -> p k c", c=cols)

                def step(b, k):
                    col, w0, kc, x0, bank = b
                    three(ps[:, bank, :], wh[:, w0 + k, col:col + P], wl[:, w0 + k, col:col + P],
                          hi[:, x0 + k, :], lo[:, x0 + k, :], k == 0, k == kc - 1,
                          block_done if k == kc - 1 else None)

                if by_k:
                    for k in range(blocks[0][2]):
                        if k_wait is not None:
                            k_wait(k)
                        for b in blocks:
                            step(b, k)
                else:
                    for b in blocks:
                        for k in part or range(b[2]):
                            step(b, k)

            def narrow_and_next(n, j):
                pe.wait_ge(lo_done, n + 2)
                for k in range(DC):
                    u_wait(j)(k)
                    gemm(n, n % 2, [(0, 0, DC, 0, 2)], 256, uhi, ulo, part=[k])
                    gemm_part(n + 1, k // 2, k % 2)

            def gemm_part(n, k, b):
                wh = whi[:, n % 2, :].rearrange("p (k c) -> p k c", c=256)
                wl = wlo[:, n % 2, :].rearrange("p (k c) -> p k c", c=256)
                cols = slice(b * P, (b + 1) * P)
                three(ps[:, b, :], wh[:, k, cols], wl[:, k, cols], uhi[:, k, :], ulo[:, k, :], k == 0, k == DC - 1,
                      block_done if k == DC - 1 else None)

            def two(bank):
                return [(0, 0, DC, 0, bank), (P, 0, DC, 0, bank + 1)]

            def one(k):
                return [(k * P, 0, DC, 0, k)]

            def u_wait(j):
                return lambda k: pe.wait_ge(u_ready, 8 * j + k + 1)

            def norm_sums(j):
                pe.wait_ge(acc_done, (DC - 1) * (j + 1))
                for k, a in enumerate((acc[:, :], acc2) if j == BOTH else (acc[:, :],)):
                    if k:
                        pe.wait_ge(acc2_done, DC - 1)
                    for t in range(TT):
                        mm = nc.tensor.matmul(ps[:, SS_BANK[j], k * TT + t:k * TT + t + 1], a[:, t * P:(t + 1) * P],
                                              ones[:, 0:1], start=True, stop=True)
                mm.then_inc(ss_done, 1)

            def norm_spread(j):
                pe.wait_ge(rs_done, j + 1)
                for k in ((1, 0) if j == BOTH else (0,)):
                    bank = RMS_BANK2 if j == BOTH and k == 0 else SS_BANK[j]
                    for t in range(TT):
                        mm = nc.tensor.matmul(ps[:, bank, t * P:(t + 1) * P], rstd[:, k, t:t + 1].to_broadcast([P, P]),
                                              ident[:, :], start=True, stop=True)
                    mm.then_inc(bc_done, 1)

            def s5_prepare():
                pe.wait_ge(B_ready, 2)
                pe.wait_ge(cst_sem, 16 * N_CST)
                for r in range(2):
                    for c in range(HC):
                        mm = nc.tensor.transpose(ps[:, 5 + r, c * P:(c + 1) * P], s5b[:, 2 + r, c * P:(c + 1) * P],
                                                 ident[:, :])
                mm.then_inc(BT_done, 1)

            Z0, Z1, Z2, S0, YB = 2, 3, 4, 5, 7
            zf = flat[:, Z0 * 512:Z0 * 512 + NZ]

            def transpose_values(i):
                pe.wait_ge(vT_ready, i + 1)
                for t in range(TT):
                    mm = nc.tensor.transpose(ps[:, 0, t * P:(t + 1) * P], vT[:, t * P:(t + 1) * P], ident[:, :])
                mm.then_inc(v_tr, 1)

            def mixer(i, last=False):
                def bu(p):
                    if p >= 1:
                        pe.wait_ge(bu_used, i * 4 + p)
                    pe.wait_ge(bs_ready, i + 1)
                    pe.wait_ge(uch_ready, i + 1)
                    rows = slice(32 * p, 32 * p + 32)
                    nc.tensor.matmul(ps[:, S0, :], Bs[rows, 0, :], uch[rows, :], start=True, stop=True)
                    nc.tensor.matmul(ps[:, S0 + 1, :], Bs[rows, 1, :], uch[rows, :], start=True,
                                     stop=True).then_inc(bu_done, 1)

                def scores(hh):
                    if hh == 0:
                        pe.wait_ge(qk_ready, i * 2 + 2)
                    else:
                        pe.wait_ge(ya_done, i * 2 + 1)
                    rows = slice(64 * hh, 64 * hh + 64)
                    for kb in range(TT):
                        out = zf[:, KB_AT[kb]:KB_AT[kb] + T - kb * P]
                        keys = slice(kb * P, (kb + 1) * P)
                        three(out, qkhi[rows, 1, keys], qklo[rows, 1, keys], qkhi[rows, 0, kb * P:],
                              qklo[rows, 0, kb * P:], kb != 3)
                        mm = nc.tensor.matmul(out[:, 0:P], identr[:, :], keymaskr[:, :], start=False, stop=False,
                                              skip_group_check=True)
                    mm.then_inc(z_done, 1)

                def log_weights(hh):
                    pe.wait_ge(l_ready, i * 2 + (hh + 1))
                    for kb in range(TT):
                        for kc in range(kb, TT):
                            n = T - kc * P
                            at = KB_AT[kb] + (kc - kb) * P
                            lhs = trir if kc == kb else negonesr
                            for part in (athi, atlo):
                                mm = nc.tensor.matmul(zf[:, at:at + n], lhs[:, :], part[:, KB_AT[kc]:KB_AT[kc] + n],
                                                      start=False, stop=False, skip_group_check=True)
                    mm.then_inc(tri_done, 1)

                def weigh_values(hh):
                    pe.wait_ge(w_ready, i * 2 + (hh + 1))
                    for kb in range(TT):
                        n = T - kb * P
                        three(ps[:, Z0, kb * P:], vhi[:, kb, :], vlo[:, kb, :], athi[:, KB_AT[kb]:KB_AT[kb] + n],
                              atlo[:, KB_AT[kb]:KB_AT[kb] + n], kb == 0, kb == TT - 1,
                              pv_done if kb == TT - 1 else None)

                def y(p):
                    pe.wait_ge(rot_out, i * 4 + (p + 1))
                    pe.wait_ge(nim_ready, i + 1)
                    nc.tensor.matmul(ps[:, YB, :], Cs[:, p, 0, :], rout1[:, 0, :], start=(p == 0), stop=False)
                    mm = nc.tensor.matmul(ps[:, YB, :], Cn[:, p, :], rout1[:, 1, :], start=False, stop=(p == 3))
                    mm.then_inc(y5_done, 1)

                scores(0)
                bu(0)
                pe.wait_ge(v_ready, i + 1)
                gemm(i * 2 + 2, 0, one(0), 256, uhi, ulo)
                bu(1)
                gemm(i * 2 + 2, 0, one(1), 256, uhi, ulo, part=range(DC // 2))
                log_weights(0)
                y(0)
                bu(2)
                weigh_values(0)
                scores(1)
                gemm(i * 2 + 2, 0, one(1), 256, uhi, ulo, part=range(DC // 2, DC // 2 + 2))
                y(1)
                bu(3)
                gemm(i * 2 + 2, 0, one(1), 256, uhi, ulo, part=range(DC // 2 + 2, DC))
                if not last:
                    pe.wait_ge(qk_ready, i * 2 + 3)
                else:
                    pe.wait_ge(gate_copied, 1)
                gemm(i * 2 + 3, 1, one(0), 256, uhi, ulo)
                log_weights(1)
                y(2)
                if not last:
                    pe.wait_ge(qk_ready, i * 2 + 4)
                else:
                    pe.wait_ge(gate_copied, 2)
                gemm(i * 2 + 3, 1, one(1), 256, uhi, ulo)
                if not last:
                    transpose_values(i + 1)
                weigh_values(1)
                y(3)
                pe.wait_ge(ya_done, i * 2 + 2)

            def merge():
                n = U_MERGE
                pe.wait_ge(ya_done, 2 * HC)
                pe.wait_ge(ys_done, HC)
                pe.wait_ge(y_ready, HC)
                gemm(n + 2, (n + 2) % 2, [(m * P, 0, HC, 0, 4 + m) for m in range(4)], 512, yhi, ylo)
                pe.wait_ge(sig_evac, 4)
                gemm(n + 3, (n + 3) % 2, two(0), 256, uhi, ulo)
                gemm(n + 4, (n + 4) % 2, two(2), 256, uhi, ulo)

                def up(k, bank):
                    blocks = [(0, 0, HC, 0, bank), (P, 0, HC, 0, bank + 1)]
                    pe.wait_ge(lo_done, k + 1)
                    gemm_up(k, blocks, bank)

                def gemm_up(k, blocks, bank):
                    slot = k % 2
                    wh = whi[:, slot, :].rearrange("p (k c) -> p k c", c=256)
                    wl = wlo[:, slot, :].rearrange("p (k c) -> p k c", c=256)
                    for m in range(2):
                        for b, (xh, xl) in enumerate(((yhi, ylo), (ahi, alo))):
                            for kk in range(HC):
                                w = b * HC + kk
                                three(ps[:, bank + 2 * m + b, :], wh[:, w, m * P:(m + 1) * P], wl[:, w, m * P:(m + 1) * P],
                                      xh[:, kk, :], xl[:, kk, :], kk == 0, kk == HC - 1,
                                      block_done if kk == HC - 1 else None)

                pe.wait_ge(y_ready, 3 * HC)
                pe.wait_ge(sig_evac, 12)
                up(n + 5, 0)
                up(n + 6, 4)
                pe.wait_ge(up_evac, 4)
                gemm(n + 7, (n + 7) % 2, two(0), 256, uhi, ulo)
                gemm(n + 8, (n + 8) % 2, two(2), 256, uhi, ulo)
                pe.wait_ge(sig_evac, 14)
                gemm(n + 9, (n + 9) % 2, two(0), 256, uhi, ulo)
                pe.wait_ge(sig_evac, 16)
                gemm(n + 10, (n + 10) % 2, two(2), 256, uhi, ulo)
                pe.wait_ge(up_evac, 8)
                up(n + 11, 4)
                pe.wait_ge(sig_evac, 20)
                up(n + 12, 0)
                n = U_OUT
                pe.wait_ge(up_evac, 12)
                gemm(n, n % 2, two(4), 256, mhi, mlo, True, lambda k: pe.wait_ge(mg_ready, k + 1))
                gemm(n + 1, (n + 1) % 2, two(6), 256, mhi, mlo)
                pe.wait_ge(up_evac, 16)
                gemm(n + 2, (n + 2) % 2, two(0), 256, mhi, mlo)
                gemm(n + 3, (n + 3) % 2, two(2), 256, mhi, mlo)

            ADDED_FF = DC

            def ff(i):
                for q in range(2):
                    n = i * 8 + (U_FF + 4 * q)
                    s = (U_FF + 4 * q) % 2
                    a, b = (0, 4) if q == 0 else (4, 0)
                    at = i * 16 + (ADDED_FF + 8 * q)
                    hid = i * 8 + 4 * q
                    first = u_wait(1)
                    pe.wait_ge(h_added, at - 4)
                    gemm(n, s, two(a), 256, uhi, ulo, True, first)
                    gemm(n + 1, 1 - s, two(a + 2), 256, uhi, ulo)
                    pe.wait_ge(h_added, at)
                    gemm(n + 2, s, [(m * P, 0, 4, 0, b + m) for m in range(4)], 512, hdhi, hdlo, True,
                         lambda k: pe.wait_ge(hd_ready, hid + (k + 1)))
                    gemm(n + 3, 1 - s, [(m * P, 0, 4, 0, a + m) for m in range(4)], 512, hdhi, hdlo)

            def gla_gate_logits():
                narrow_and_next(U_ALR, BOTH)
                for b in range(2):
                    gemm_part(U_GLA, DC // 2, b)
                pe.wait_ge(alr_ready, 1)
                for hh in range(GLA_H):
                    nc.tensor.matmul(ps[:, 4 + hh, :], wa2[:, hh * P:(hh + 1) * P], alr[0:16, :], start=True,
                                     stop=True).then_inc(la_mm, 1)

            def gla_values(i):
                n = i * 2 + (U_GLA + 1)
                slot = (U_GLA + 1) % 2
                pe.wait_ge(lo_done, n + 1)
                wh = whi[:, slot, :].rearrange("p (k c) -> p k c", c=256)
                wl = wlo[:, slot, :].rearrange("p (k c) -> p k c", c=256)
                for t in range(TT):
                    tok = slice(t * P, (t + 1) * P)
                    for k in range(DC):
                        three(ps[:, 2 + t // 2, (t % 2) * 256:(t % 2) * 256 + 256], uhi[:, k, tok], ulo[:, k, tok],
                              wh[:, k, :], wl[:, k, :], k == 0, k == DC - 1,
                              block_done if k == DC - 1 and t % 2 else None)

            def gla_head(i, last=False):
                pe.wait_ge(in_done, i * 3 + 3)
                for t in range(TT):
                    mm = nc.tensor.transpose(ps[:, 4, t * P:(t + 1) * P], kdec[:, t * P:(t + 1) * P], ident[:, :])
                mm.then_inc(kd_tr, 1)
                pe.wait_ge(in_ready, i * 2 + 2)
                for t in range(TT):
                    tok = slice(t * P, (t + 1) * P)
                    three(ps[:, 5, tok], kihi[:, tok], kilo[:, tok], qzhi[:, t, 0:4:3, :], qzlo[:, t, 0:4:3, :], True, True,
                          ai_mm if t == TT - 1 else None)
                n = i * 2 + (U_GLA + 2)
                gemm(n, U_GLA % 2, one(0), 256, uhi, ulo, part=range(3))
                pe.wait_ge(kd_ready, i + 1)
                pe.wait_ge(gv_ready, i + 1)
                for c in range(GLA_N - 1):
                    rows = slice(64 * (c % 2), 64 * (c % 2) + 64)
                    keys = slice((c // 2) * P, (c // 2 + 1) * P)
                    three(kv_sums(c), kdhi[rows, keys], kdlo[rows, keys], gvhi[rows, c // 2, :], gvlo[rows, c // 2, :],
                          True, True, kv_mm)
                gemm(n, U_GLA % 2, one(0), 256, uhi, ulo, part=range(3, DC))
                gemm(n, U_GLA % 2, one(1), 256, uhi, ulo)
                pe.wait_ge(ai_ready, i + 1)
                pe.wait_ge(st_done, i * (GLA_N - 1) + (GLA_N - 1))
                for t in range(TT):
                    out = ps[:, 6 + t // 2, (t % 2) * 256:(t % 2) * 256 + 256]
                    three(out, aihi[:, t, :], ailo[:, t, :], gvhi[:, t, :], gvlo[:, t, :], True)
                    for v in range(2):
                        c = 2 * t + v
                        if c == 0:
                            continue
                        pe.wait_ge(st_ready, i * (GLA_N - 1) + c)
                        half = [q[:, t, 2 * v:2 * v + 2, :].rearrange("p a b -> p (a b)") for q in (qzhi, qzlo)]
                        three(out, *half, sthi[:, c, :], stlo[:, c, :], False, v == 1, go_mm if v == 1 and t % 2 else None)
                if not last:
                    gla_values(i + 1)
                else:
                    gemm(U_GLAG + 1, (U_GLAG + 1) % 2, two(2), 256, uhi, ulo)
                pe.wait_ge(otm_done, i + 1)
                for dv in range(2):
                    for t in range(TT):
                        mm = nc.tensor.transpose(ps[:, 6 + dv, t * P:(t + 1) * P], otm[:, t, dv * P:(dv + 1) * P], ident[:, :])
                mm.then_inc(ot_done, 1)

            def residual_gemm(n, added, k_wait):
                for b in range(4):
                    if b >= 2:
                        pe.wait_ge(h_added, added + 2 * (b - 1))
                    gemm(n + b, (n + b) % 2, two(2 * (b % 2)), 256, uhi, ulo, b == 0, k_wait if b == 0 else None)

            def gate_gemm(n):
                for b in range(2, 4):
                    pe.wait_ge(g_evac, 2 * (b - 1))
                    gemm(n + b, (n + b) % 2, two(2 * (b % 2)), 256, uhi, ulo)

            def ple_proj(layer, n, j):
                pe.wait_ge(pe_ready, 2 * layer + 2)
                pe.wait_ge(lo_done, n + 1)
                wh = whi[:, n % 2, :].rearrange("p (k c) -> p k c", c=1024)
                wl = wlo[:, n % 2, :].rearrange("p (k c) -> p k c", c=1024)
                for m in range(DC):
                    if m >= 3:
                        pe.wait_ge(pp_done, 8 * layer + m - 2)
                    if m == 3:
                        norm_sums(j)
                    if m == 6:
                        norm_spread(j)
                    for k in range(2):
                        three(ps[:, 4 + m % 3, :], wh[:, k, m * P:(m + 1) * P], wl[:, k, m * P:(m + 1) * P], pehi[:, k, :],
                              pelo[:, k, :], k == 0, k == 1, block_done if k == 1 else None)

            def ple_gate(layer, n, j):
                for b in range(4):
                    if b >= 2:
                        pe.wait_ge(sg_done, 8 * layer + 2 * (b - 1))
                    gemm(n + b, (n + b) % 2, two(2 * (b % 2)), 256, uhi, ulo, b == 0, u_wait(j) if b == 0 else None)

            TB = 5
            tf = flat[:, TB * 512:TB * 512 + NZ]

            def fox_qk_sums(i):
                pe.wait_ge(qk_sq, i + 1)
                for k in range(2):
                    mm = nc.tensor.matmul(ps[:, Z0 + k, :], headones[:, :], qksq[:, k, :], start=True, stop=True)
                mm.then_inc(qk_ss, 1)

            def fox_transpose_values(i):
                pe.wait_ge(fvT_ready, i + 1)
                for t in range(TT):
                    mm = nc.tensor.transpose(ps[:, TB + 2, t * P:(t + 1) * P], fvT[:, t * P:(t + 1) * P], ident[:, :])
                mm.then_inc(fv_tr, 1)

            def fox(i, last=False):
                def scores(hh):
                    if hh == 0:
                        pe.wait_ge(fq_ready, i + 1)
                    pe.wait_ge(cm_ready, i * 2 + (hh + 1))
                    rows = slice(64 * hh, 64 * hh + 64)
                    for qb in range(TT - 1, -1, -1):
                        n = (qb + 1) * P
                        out = zf[:, QB_AT[qb]:QB_AT[qb] + n]
                        toks = slice(qb * P, (qb + 1) * P)
                        three(out, fqhi[rows, 0, toks], fqlo[rows, 0, toks], fqhi[rows, 1, 0:n], fqlo[rows, 1, 0:n],
                              qb != 0)
                        for part in (cmhi, cmlo):
                            nc.tensor.matmul(out, onesr[0:16, :], part[:, 0:n], start=False, stop=False,
                                             skip_group_check=True)
                        mm = nc.tensor.matmul(out[:, n - P:n], identr[:, :], querymaskr[:, :], start=False, stop=False,
                                              skip_group_check=True)
                    mm.then_inc(fz_done, 1)

                def transpose_probs(hh):
                    if hh == 0:
                        pe.wait_ge(fv_ready, i + 1)
                    else:
                        pe.wait_ge(fo_done, i * 2 + 1)
                    for g, group in enumerate(QB_GROUPS):
                        pe.wait_ge(p_done, i * 6 + (hh * 3 + g + 1))
                        for qb in group:
                            for kb in range(qb + 1):
                                at = KB_AT[kb] + (qb - kb) * P
                                mm = nc.tensor.transpose(tf[:, at:at + P],
                                                         pr[:, QB_AT[qb] + kb * P:QB_AT[qb] + (kb + 1) * P], ident[:, :])
                    mm.then_inc(pt_done, 1)

                def weigh_values(hh):
                    pe.wait_ge(pt_ready, i * 2 + (hh + 1))
                    for kb in range(TT):
                        n = T - kb * P
                        three(ps[:, TB, kb * P:], fvhi[:, kb, :], fvlo[:, kb, :], pthi[:, KB_AT[kb]:KB_AT[kb] + n],
                              ptlo[:, KB_AT[kb]:KB_AT[kb] + n], kb == 0, kb == TT - 1,
                              fpv_done if kb == TT - 1 else None)

                scores(0)
                if not last:
                    gemm(i * 2 + (U_FOX + 2), U_FOX % 2, one(0), 256, uhi, ulo)
                transpose_probs(0)
                scores(1)
                if not last:
                    pe.wait_ge(g_copy, i + 1)
                    gemm(i * 2 + (U_FOX + 2), U_FOX % 2, one(1), 256, uhi, ulo)
                weigh_values(0)
                transpose_probs(1)
                if not last:
                    fox_qk_sums(i + 1)
                    pe.wait_ge(qk_copy, i * 2 + 4)
                    gemm(i * 2 + (U_FOX + 3), (U_FOX + 1) % 2, one(0), 256, uhi, ulo)
                weigh_values(1)
                if not last:
                    fox_transpose_values(i + 1)
                    gemm(i * 2 + (U_FOX + 3), (U_FOX + 1) % 2, one(1), 256, uhi, ulo)

            pe.wait_ge(first_in, 48)
            norm_sums(0)
            norm_spread(0)
            gemm(0, 0, two(0), 256, uhi, ulo, True, u_wait(0))
            pe.wait_ge(qk_ready, 2)
            gemm(1, 1, one(0), 256, uhi, ulo)
            s5_prepare()
            gemm(1, 1, one(1), 256, uhi, ulo)
            transpose_values(0)
            pe.wait_ge(consts_ready, 6)
            with nc.tensor.Fori(0, HC - 1) as i:
                mixer(i)
            mixer(HC - 1, True)
            merge()
            norm_sums(1)
            norm_spread(1)
            with nc.tensor.Fori(0, FFB // 2 - 1) as i:
                ff(i)
            ff(FFB // 2 - 1)
            norm_sums(BOTH)
            norm_spread(BOTH)
            gla_gate_logits()
            pe.wait_ge(h_normed, DC)
            for k in range(DC // 2 + 1, DC):
                for b in range(2):
                    gemm_part(U_GLA, k, b)
            gla_values(0)
            with nc.tensor.Fori(0, GLA_H - 1) as i:
                gla_head(i)
            gla_head(GLA_H - 1, True)
            gate_gemm(U_GLAG)
            residual_gemm(U_GLAO, 72, lambda k: pe.wait_ge(gated, k + 1))
            ple_proj(0, U_PLE0, 3)
            ple_gate(0, U_PLE0 + 1, 3)
            norm_sums(4)
            norm_spread(4)
            narrow_and_next(U_F, 4)
            for k in range(DC // 2, DC):
                for b in range(2):
                    gemm_part(U_FOX, k, b)
            fox_qk_sums(0)
            pe.wait_ge(qk_copy, 2)
            gemm(U_FOX + 1, (U_FOX + 1) % 2, two(0), 256, uhi, ulo)
            fox_transpose_values(0)
            with nc.tensor.Fori(0, FOX_PAIRS - 1) as i:
                fox(i)
            fox(FOX_PAIRS - 1, True)
            residual_gemm(U_FOXO, 88, lambda k: pe.wait_ge(gated, 8 + k + 1))
            ple_proj(1, U_PLE1, 5)
            ple_gate(1, U_PLE1 + 1, 5)
            norm_sums(6)
            norm_spread(6)

        @block.scalar
        def _(act):
            own = Chain(act, act_own)
            A = nc.scalar.activation

            def copy(out, in_, scale=1.0):
                return A(out, in_, ACT.Copy, scale=scale)

            def split_hi(n, slot, parity_turn, done_before=None):
                act.wait_ge(landed[slot], parity_turn * 16 + 16)
                if done_before is not None:
                    act.wait_ge(block_done, done_before)
                copy(whi[:, slot, :], wraw[:, slot, :]).then_inc(hi_done, 1)

            def split_static(n):
                if n < NU:
                    split_hi(n, n % 2, n // 2, DONE[n - 1] if n >= 2 else None)

            def square(j, c):
                if j == 0:
                    act.wait_ge(x_in[c * X_PARTS // DC], 16)
                else:
                    act.wait_ge(h_added, H_BASE[j] + c + 1)
                if c >= 2:
                    act.wait_ge(acc_done, (DC - 1) * j + max(c - 2, 1))
                A(sq[:, c % 2, :], h[:, c, :], ACT.Square).then_inc(sq_done, 1)
                if j == BOTH:
                    if c >= 2:
                        act.wait_ge(acc2_done, max(c - 2, 1))
                    A(sq2[:, c % 2, :], h[:, c, :], ACT.Square, scale=vec("norm_final", c)).then_inc(sq2_done, 1)

            def norm(j):
                if j == 0:
                    split_static(0)
                for c in range(DC):
                    act.wait_ge(un_done, 8 * j + c + 1)
                    copy(uhi[:, c, :], un[:, c % 2, :]).then_inc(u_hi, 1)

            def s5_prepare():
                act.wait_ge(par_in, 16)
                A(s5p[:, 3, :], s5p[:, 2, :], ACT.Exp).then_inc(s5_exp, 1)
                act.wait_ge(s5_arg, 1)
                A(s5p[:, 6, :], s5p[:, 4, :], ACT.Exp).then_inc(s5_exp, 1)

            def s5_turn():
                act.wait_ge(s5_arg, 2)
                A(s5p[:, 14, :], s5p[:, 12, :], ACT.Sin, scale=TWO_PI).then_inc(s5_trig, 1)
                own.do(A(s5p[:, 13, :], s5p[:, 12, :], ACT.Abs))
                own.sync()
                A(s5p[:, 15, :], s5p[:, 13, :], ACT.Sin, scale=-TWO_PI, bias=halfpi_b).then_inc(s5_trig, 1)

            def s5_stage():
                act.wait_ge(BT_done, 1)
                own.do(copy(BT[:, :, 0, :], ps[:, 5, :].rearrange("p (c n) -> p c n", c=HC)))
                own.do(copy(BT[:, :, 1, :], ps[:, 6, :].rearrange("p (c n) -> p c n", c=HC)))
                own.sync()
                copy(Bs[:, :, :], BT[:, 0, :, :]).then_inc(bs_ready, 1)

            Z0 = 2
            zf = flat[:, Z0 * 512:Z0 * 512 + NZ]

            def evac_qk(i):
                act.wait_ge(block_done, i * 4 + 2)
                copy(qkhi[:, 0, :], ps[:, 0, :], 0.125).then_inc(q_hi, 1)
                copy(qkhi[:, 1, :], ps[:, 1, :]).then_inc(q_hi, 1)

            def evac_v(i):
                act.wait_ge(block_done, i * 4 + 3)
                copy(vT[:, :], ps[:, 0, :]).then_inc(vT_ready, 1)

            def values_hi(i):
                act.wait_ge(v_tr, i + 1)
                copy(vhi[:, :, :], ps[:, 0, :].rearrange("p (t c) -> p t c", t=TT)).then_inc(v_hi, 1)

            def evac_u(i):
                act.wait_ge(block_done, i * 4 + 4)
                copy(uch[:, :], ps[:, 1, :]).then_inc(uch_ready, 1)

            def table(i, p):
                act.wait_ge(phase_ready, i * 4 + (p + 1))
                own.do(A(sinT[:, p, :], cosT[:, p, :], ACT.Sin, scale=-TWO_PI))
                own.sync()
                own.do(A(cosT[:, p, :], cosT[:, p, :], ACT.Abs))
                own.sync()
                A(cosT[:, p, :], cosT[:, p, :], ACT.Sin, scale=-TWO_PI, bias=halfpi_b).then_inc(table_ready, 1)

            def mixer(i, last=False):
                def log1p(hh):
                    act.wait_ge(z_done, i * 2 + (hh + 1))
                    own.do(A(att[:, :], zf, ACT.Abs))
                    own.sync()
                    own.do(A(att[:, :], att[:, :], ACT.Exp, scale=-1.0))
                    own.sync()
                    A(att[:, :], att[:, :], ACT.Ln, bias=one_b).then_inc(l_done, 1)

                def fail_hi(hh):
                    act.wait_ge(sp_done, i * 2 + (hh + 1))
                    copy(athi[:, :], att[:, :]).then_inc(l_hi, 1)

                def weights(hh):
                    act.wait_ge(tri_done, i * 2 + (hh + 1))
                    own.do(A(att[:, :], zf, ACT.Exp))
                    own.sync()
                    copy(athi[:, :], att[:, :]).then_inc(w_hi, 1)

                def load_exp():
                    own.sync()
                    own.do(A(biases[:, 6:7], zero_b, ACT.Exp))

                def store(hh):
                    act.wait_ge(pv_done, i * 2 + (hh + 1))
                    rows = slice(64 * hh, 64 * hh + 64)
                    copy(ya[rows, i, :], ps[rows, Z0, :]).then_inc(ya_done, 1)

                log1p(0)
                split_hi(None, 1, i + 1, i * 4 + 4)
                fail_hi(0)
                weights(0)
                table(i, 2)
                store(0)
                table(i, 3)
                load_exp()
                log1p(1)
                if not last:
                    evac_qk(i + 1)
                else:
                    for b in range(2):
                        act.wait_ge(block_done, DONE[U_MERGE] + b + 1)
                        copy(ph[:, b, :], ps[:, b, :]).then_inc(gate_copied, 1)
                fail_hi(1)
                split_hi(None, 0, i + 2, i * 4 + 6)
                weights(1)
                if not last:
                    evac_v(i + 1)
                    table(i + 1, 0)
                store(1)
                if not last:
                    values_hi(i + 1)
                    table(i + 1, 1)
                    act.wait_ge(ys_done, i + 1)
                    evac_u(i + 1)
                    act.wait_ge(bu_done, i * 4 + 4)
                    copy(Bs[:, :, :], BT[:, i + 1, :, :]).then_inc(bs_ready, 1)

            def merge():
                n = U_MERGE
                for c in range(HC):
                    act.wait_ge(ys_done, c + 1)
                    own.do(A(ys[:, c, :], ys[:, c, :], ACT.Gelu_apprx_tanh))
                own.sync()
                for c in range(HC):
                    copy(yhi[:, c, :], ys[:, c, :]).then_inc(ye_hi, 1)
                act.wait_ge(ya_done, 2 * HC)
                for c in range(HC):
                    copy(ahi[:, c, :], ya[:, c, :]).then_inc(ye_hi, 1)

                def gates(unit, branch, m):
                    for b in range(2):
                        act.wait_ge(block_done, DONE[unit] + b + 1)
                        logits = ps[:, 2 * branch + b, :]
                        if unit == n:
                            act.wait_ge(gate_copied, b + 1)
                            logits = ph[:, b, :]
                        elif unit == n + 1:
                            logits = ps[:, b, :]
                        A(gate[:, branch, m % 4 + b, :], logits, ACT.Sigmoid,
                          bias=vec("b_gate", DC * branch + m + b)).then_inc(sig_evac, 1)
                    if unit > n:
                        split_static(unit + 2)

                gates(n, 0, 0)
                gates(n + 1, 1, 0)
                for m in range(4):
                    act.wait_ge(block_done, DONE[n + 2] + m + 1)
                    if m >= 2:
                        act.wait_ge(y2_mult, m - 1)
                    A(glu[:, m % 2, :], ps[:, 4 + m, :], ACT.Sigmoid, bias=vec("b_glu", m)).then_inc(sig_evac, 1)
                split_static(n + 4)
                for m in range(HC):
                    act.wait_ge(y2_mult, m + 1)
                    copy(yhi[:, m, :], ys[:, m, :]).then_inc(ye_hi, 1)
                gates(n + 3, 0, 2)
                gates(n + 4, 1, 2)

                def sums_hi(unit, m0):
                    for m in range(m0, m0 + 2):
                        act.wait_ge(mg_done, m + 1)
                        copy(mhi[:, m, :], mg[:, m % 2, :]).then_inc(mg_hi, 1)
                    split_static(unit + 2)

                sums_hi(n + 5, 0)
                sums_hi(n + 6, 2)
                for k in range(4):
                    gates(n + 7 + k, k % 2, 4 + 2 * (k // 2))
                sums_hi(n + 11, 4)
                sums_hi(n + 12, 6)
                split_squares(U_OUT, 1)

            def split_squares(n, j, between=None):
                for k in range(4):
                    if k < 3:
                        split_static(n + 2 + k)
                    if k == 1 and between is not None:
                        between()
                    square(j, 2 * k)
                    square(j, 2 * k + 1)
                split_static(n + 5)

            def ff(i, last=False):
                for q in range(2):
                    n = U_FF + 4 * q
                    turn = i * 4
                    base = i * 24 + (DONE[U_FF] + 12 * q)
                    a = 4 * q
                    hid = i * 8 + 4 * q

                    def relu(m):
                        act.wait_ge(block_done, base + (m + 1))
                        A(rl[:, m % 2, :], ps[:, a + m, :], ACT.Relu).then_inc(rl_done, 1)

                    def hid_hi(m):
                        act.wait_ge(hd_done, hid + (m + 1))
                        copy(hdhi[:, m, :], hd[:, m % 2, :]).then_inc(hd_hi, 1)

                    relu(0)
                    relu(1)
                    split_hi(None, n % 2, turn + (n + 2) // 2, base + 2)
                    hid_hi(0)
                    hid_hi(1)
                    relu(2)
                    relu(3)
                    split_hi(None, (n + 1) % 2, turn + (n + 3) // 2, base + 4)
                    hid_hi(2)
                    hid_hi(3)
                    if last and q == 1:
                        for c in range(DC // 2):
                            square(BOTH, c)
                    split_hi(None, n % 2, turn + (n + 4) // 2, base + 8)
                    if last and q == 1:
                        for c in range(DC // 2, DC):
                            square(BOTH, c)
                    split_hi(None, (n + 1) % 2, turn + (n + 5) // 2, base + 12)

            def gla_prepare():
                act.wait_ge(block_done, DONE[U_ALR + 1])
                copy(alr[0:16, :], ps[0:16, 2, :]).then_inc(alr_ready, 1)
                split_static(U_ALR + 2)
                for hh in range(GLA_H):
                    act.wait_ge(la_mm, hh + 1)
                    A(cum[:, hh, :], ps[:, 4 + hh, :], ACT.Abs, bias=vec("gla_b_a", hh)).then_inc(la_abs, 1)
                act.wait_ge(la_abs, GLA_H)
                own.do(A(cum[:, :, :], cum[:, :, :], ACT.Exp, scale=-1.0))
                own.sync()
                for hh in (slice(0, 1), slice(1, GLA_H)):
                    A(cum[:, hh, :], cum[:, hh, :], ACT.Ln, bias=one_b).then_inc(la_ln, 1)

            def gla_decays(i):
                act.wait_ge(dec_in, i + 1)
                own.do(A(eq[:, :], cum[:, i, :], ACT.Exp, scale=1.0 / 16))
                own.do(A(ek[:, :], cum[:, i, :], ACT.Exp, scale=-1.0 / 16))
                A(kd[:, :], kd[:, :], ACT.Exp, scale=1.0 / 16).then_inc(dec_done, 1)

            def gla_in_hi(i):
                act.wait_ge(in_done, i * 3 + 1)
                copy(qzhi[:, :, 0:4:3, :], qin[:, :].rearrange("p (t a b) -> p t a b", t=TT, a=2)).then_inc(in_hi, 1)
                act.wait_ge(in_done, i * 3 + 2)
                copy(kihi[:, :], kin[:, :]).then_inc(in_hi, 1)

            def gla_head(i, last=False):
                act.wait_ge(kd_tr, i + 1)
                copy(kdhi[:, :], ps[:, 4, :]).then_inc(kd_hi, 1)
                act.wait_ge(block_done, i * 4 + (DONE[U_GLA] + 4))
                copy(gvhi[:, :, :], flat[:, 1024:2048].rearrange("p (t c) -> p t c", t=TT)).then_inc(gv_hi, 1)
                split_hi(None, (U_GLA + 3) % 2, i + (U_GLA + 3) // 2)
                act.wait_ge(ai_done, i + 1)
                copy(aihi[:, :, :], ai[:, :, :]).then_inc(ai_hi, 1)
                for c in range(GLA_N - 1):
                    act.wait_ge(st_done, i * (GLA_N - 1) + (c + 1))
                    copy(sthi[:, c + 1, :], st[:, c % 2, :]).then_inc(st_hi, 1)
                if not last:
                    split_hi(None, U_GLA % 2, i + (U_GLA + 4) // 2, i * 4 + (DONE[U_GLA] + 6))
                for t in range(TT):
                    if t % 2 == 0:
                        act.wait_ge(go_mm, i * 2 + (t // 2 + 1))
                    if t >= 1:
                        own.sync()
                    r = A(gsq, ps[:, 6 + t // 2, (t % 2) * 256:(t % 2) * 256 + 256], ACT.Square, accum_out=gss[:, t:t + 1])
                    if t < TT - 1:
                        own.do(r)
                    else:
                        r.then_inc(gss_done, 1)
                if not last:
                    gla_decays(i + 1)
                    gla_in_hi(i + 1)

            def gate_evac(n):
                for b in range(4):
                    for k in range(2):
                        act.wait_ge(block_done, DONE[n + b] + k + 1)
                        A(gr[:, 2 * b + k, :], ps[:, 2 * (b % 2) + k, :], ACT.Silu).then_inc(g_evac, 1)
                    if b < 3:
                        split_static(n + b + 2)

            def gated_hi_half(turn, chunks):
                for c in chunks:
                    act.wait_ge(prod_done, 8 * turn + c + 1)
                    copy(uhi[:, c, :], og[:, c, :]).then_inc(gated_hi, 1)

            def ple_split(layer):
                act.wait_ge(pe_sem, 16 * layer + 16)
                for k in range(2):
                    copy(pehi[:, k, :], pe_in[:, k, :]).then_inc(pe_hi, 1)

            def ple_norm(layer, n, j):
                def evac(m):
                    act.wait_ge(block_done, DONE[n] + m + 1)
                    copy(pp[:, m, :], ps[:, 4 + m % 3, :]).then_inc(pp_done, 1)

                for m in range(7):
                    evac(m)
                for c in range(DC):
                    act.wait_ge(un_done, 8 * j + c + 1)
                    copy(uhi[:, c, :], un[:, c % 2, :]).then_inc(u_hi, 1)
                    if c == 0:
                        evac(7)
                    if c == DC // 2:
                        split_static(n + 2)

            def ple_gate(layer, n):
                for b in range(4):
                    for k in range(2):
                        m = 2 * b + k
                        act.wait_ge(block_done, DONE[n + b] + k + 1)
                        if m >= 2:
                            act.wait_ge(h_added, 80 + 16 * layer + m - 1)
                        A(sg[:, m % 2, :], ps[:, 2 * (b % 2) + k, :], ACT.Sigmoid).then_inc(sg_done, 1)
                    if b < 3:
                        split_static(n + b + 2)
                    for k in range(2):
                        square(4 + 2 * layer, 2 * b + k)
                split_static(n + 5)

            tf = flat[:, 5 * 512:5 * 512 + NZ]

            def fox_prepare():
                act.wait_ge(block_done, DONE[U_F + 1])
                own.do(A(fl[:, 0, :], ps[0:16, 2, :], ACT.Identity, bias=vecs[0:16, VEC["fox_b_f"]:VEC["fox_b_f"] + 1]))
                own.sync()
                A(fl[:, 1, :], fl[:, 0, :], ACT.Abs).then_inc(f_evac, 1)
                split_static(U_F + 2)
                act.wait_ge(f_evac, 1)
                A(fl[:, 1, :], fl[:, 1, :], ACT.Exp, scale=-1.0).then_inc(f_evac, 1)

            def fox_log():
                act.wait_ge(f_evac, 2)
                A(fl[:, 1, :], fl[:, 1, :], ACT.Ln, bias=biases[0:16, 1:2]).then_inc(f_ln_done, 1)

            def fox_bias_hi():
                act.wait_ge(c_ready, 1)
                copy(nchi[:, :], fl[:, 2, :]).then_inc(f_exp, 1)

            def fox_evac(i, k):
                act.wait_ge(block_done, i * 4 + (DONE[U_FOX] + 1 + k))
                copy(qk[:, k, :], ps[:, k, :]).then_inc(qk_copy, 1)

            def fox_squares(i):
                act.wait_ge(qk_copy, i * 2 + 2)
                A(qksq[:, :, :], qk[:, :, :], ACT.Square).then_inc(qk_sq, 1)

            def fox_qk_norm(i):
                act.wait_ge(qk_ss, i + 1)
                A(f_t[:, :, :], ps[:, Z0:Z0 + 2, :], ACT.Ln, bias=eps_b, scale=1.0 / 64).then_inc(fln_done, 1)
                act.wait_ge(fln_done, i + 1)
                A(f_y[:, :, :], f_t[:, :, :], ACT.Exp, scale=-0.5).then_inc(fy_done, 1)

            def fox_qk_hi(i):
                act.wait_ge(qk_n, i + 1)
                copy(fqhi[:, :, :], qk[:, :, :]).then_inc(fq_hi, 1)

            def fox_v_evac(i):
                act.wait_ge(block_done, i * 4 + (DONE[U_FOX] + 3))
                copy(fvT[:, :], ps[:, 0, :]).then_inc(fvT_ready, 1)

            def fox_values_hi(i):
                act.wait_ge(fv_tr, i + 1)
                copy(fvhi[:, :, :], ps[:, 7, :].rearrange("p (t c) -> p t c", t=TT)).then_inc(fv_hi, 1)

            def fox_g_evac(i):
                act.wait_ge(block_done, i * 4 + (DONE[U_FOX] + 4))
                copy(gr[:, i, :], ps[:, 1, :]).then_inc(g_copy, 1)

            def fox(i, last=False):
                def exps(hh):
                    for g, group in enumerate(QB_GROUPS):
                        act.wait_ge(max_done, i * 6 + (hh * 3 + g + 1))
                        for qb in group:
                            at, col = slice(QB_AT[qb], QB_AT[qb] + (qb + 1) * P), slice(QB_COL[qb], QB_COL[qb] + 1)
                            e = A(pr[:, at], zf[:, at], ACT.Exp, bias=nmax[:, col], accum_out=rsum[:, col])
                            if qb == group[-1]:
                                e.then_inc(exp_done, 1)
                            else:
                                own.do(e)

                def probs_hi(hh):
                    act.wait_ge(pt_done, i * 2 + (hh + 1))
                    copy(pthi[:, :], tf).then_inc(pt_hi, 1)

                def store(hh):
                    act.wait_ge(fpv_done, i * 2 + (hh + 1))
                    rows = slice(64 * hh, 64 * hh + 64)
                    copy(og[rows, i, :], ps[rows, 5, :]).then_inc(fo_done, 1)

                exps(0)
                if not last:
                    fox_evac(i + 1, 0)
                else:
                    act.wait_ge(g_copy, FOX_PAIRS)
                    for c in range(DC):
                        A(gr[:, c, :], gr[:, c, :], ACT.Silu).then_inc(fox_silu, 1)
                probs_hi(0)
                exps(1)
                if not last:
                    fox_evac(i + 1, 1)
                    fox_squares(i + 1)
                store(0)
                probs_hi(1)
                if not last:
                    fox_qk_norm(i + 1)
                    split_hi(None, U_FOX % 2, i + (U_FOX + 4) // 2, i * 4 + (DONE[U_FOX] + 6))
                    fox_v_evac(i + 1)
                else:
                    gated_hi_half(1, range(DC - 1))
                store(1)
                if not last:
                    fox_qk_hi(i + 1)
                    fox_values_hi(i + 1)
                    fox_g_evac(i + 1)
                    split_hi(None, (U_FOX + 1) % 2, i + (U_FOX + 5) // 2, i * 4 + (DONE[U_FOX] + 8))

            act.wait_ge(bias_ready, 1)
            s5_prepare()
            for c in range(DC):
                square(0, c)
            norm(0)
            s5_turn()
            split_static(1)
            evac_qk(0)
            split_static(2)
            evac_v(0)
            s5_stage()
            table(0, 0)
            evac_u(0)
            values_hi(0)
            table(0, 1)
            with nc.scalar.Fori(0, HC - 1) as i:
                own.enter(i, 15)
                mixer(i)
                own.leave(HC - 1)
            mixer(HC - 1, True)
            merge()
            norm(1)
            with nc.scalar.Fori(0, FFB // 2 - 1) as i:
                ff(i)
            ff(FFB // 2 - 1, True)
            norm(BOTH)
            gla_prepare()
            gla_decays(0)
            act.wait_ge(block_done, DONE[U_GLA + 1])
            split_static(U_GLA + 2)
            gla_in_hi(0)
            with nc.scalar.Fori(0, GLA_H - 1) as i:
                own.enter(i, 5)
                gla_head(i)
                own.leave(GLA_H - 1)
            gla_head(GLA_H - 1, True)
            gate_evac(U_GLAG)
            gated_hi_half(0, range(DC))
            split_static(U_GLAG + 5)
            ple_split(0)
            split_squares(U_GLAO, 3)
            ple_norm(0, U_PLE0, 3)
            ple_gate(0, U_PLE0 + 1)
            norm(4)
            fox_prepare()
            fox_evac(0, 0)
            fox_evac(0, 1)
            fox_squares(0)
            fox_log()
            fox_qk_norm(0)
            fox_bias_hi()
            split_static(U_FOX + 2)
            fox_qk_hi(0)
            fox_v_evac(0)
            fox_values_hi(0)
            fox_g_evac(0)
            split_static(U_FOX + 3)
            with nc.scalar.Fori(0, FOX_PAIRS - 1) as i:
                own.enter(i, 2)
                fox(i)
                own.leave(FOX_PAIRS - 1)
            fox(FOX_PAIRS - 1, True)
            gated_hi_half(1, range(DC - 1, DC))
            split_squares(U_FOXO, 5, lambda: ple_split(1))
            ple_norm(1, U_PLE1, 5)
            ple_gate(1, U_PLE1 + 1)

        @block.vector
        def _(dve):
            own = Chain(dve, dve_own)
            V = nc.vector

            def split_lo(n, slot):
                dve.wait_ge(hi_done, n + 1)
                V.tensor_tensor(wlo[:, slot, :], wraw[:, slot, :], whi[:, slot, :], ALU.subtract).then_inc(lo_done, 1)

            def split_static(n):
                if n < NU:
                    split_lo(n, n % 2)

            def newton(y, half, tmp, out, done=None):
                step(V.tensor_tensor(tmp, y, y, ALU.mult))
                step(V.scalar_tensor_tensor(tmp, tmp, -1.0, half, ALU.mult, ALU.mult))
                r = V.scalar_tensor_tensor(out, tmp, 1.5, y, ALU.add, ALU.mult)
                if done is None:
                    step(r)
                else:
                    r.then_inc(done, 1)

            def rsqrt(half, y, tmp, out, done=None):
                step(V.tensor_scalar(tmp.bitcast(I32), half.bitcast(I32), 1, None, ALU.arith_shift_right))
                step(V.tensor_scalar(y.bitcast(I32), tmp.bitcast(I32), -1.0, float(0x5f3759df - (1 << 22)), ALU.mult, ALU.add))
                newton(y, half, tmp, y)
                newton(y, half, tmp, y)
                newton(y, half, tmp, out, done)

            def norm_scale(j, between=()):
                if j not in (0, BOTH):
                    norm_chunk_sum(dve, V, j, DC - 1)
                dve.wait_ge(ss_done, j + 1)
                step(V.tensor_scalar(rs_half[:, 0, :], ps[:, SS_BANK[j], 0:TT], 0.5 / D, 0.5 * EPS, ALU.mult, ALU.add))
                n = 1
                if j == BOTH:
                    n = 2
                    step(V.tensor_scalar(rs_half[:, 1, :], rs_half[:, 0, :], EPS, None, ALU.mult))
                    step(V.scalar_tensor_tensor(rs_half[:, 1, :], ps[:, SS_BANK[j], TT:2 * TT], 0.5 / D, rs_half[:, 1, :],
                                                ALU.mult, ALU.add))
                rsqrt(*(t[:, 0:n, :] for t in (rs_half, rs_y, rs_t, rstd)), rs_done)
                for n in between:
                    split_static(n)
                dve.wait_ge(bc_done, j + 1 + (j > BOTH))
                return ps[:, SS_BANK[j], :]

            def norm(j, gain, between=()):
                scale = norm_scale(j, between)

                def lo(c):
                    dve.wait_ge(u_hi, 8 * j + c + 1)
                    V.tensor_tensor(ulo[:, c, :], un[:, c % 2, :], uhi[:, c, :], ALU.subtract).then_inc(u_ready, 1)

                for c in range(DC):
                    if c >= 2:
                        lo(c - 2)
                        dve.wait_ge(u_ready, 8 * j + c - 1)
                    g = g12[:, c:c + 1] if j == BOTH else vec(gain, c)
                    V.scalar_tensor_tensor(un[:, c % 2, :], h[:, c, :], g, scale, ALU.mult, ALU.mult).then_inc(un_done, 1)
                lo(DC - 2)
                lo(DC - 1)

            def norm_out(j, gain, scale, dst, done):
                for c in range(DC):
                    V.scalar_tensor_tensor(dst[:, c, :], h[:, c, :], vec(gain, c), scale, ALU.mult,
                                           ALU.mult).then_inc(done, 1)

            def step(ins):
                own.do(ins)
                own.sync()

            c_all = 1 / (2 * np.pi)
            c_hi = float(np.float32(np.round(c_all * 2 ** 14) / 2 ** 14))
            c_lo = float(np.float32(c_all - c_hi))

            def s5_prepare():
                r = [s5p[:, k, :] for k in range(24)]
                TTp, TS, STT = V.tensor_tensor, V.tensor_scalar, V.scalar_tensor_tensor
                dve.wait_ge(par_in, 16)
                dve.wait_ge(s5_exp, 1)
                own.do(TTp(r[5], r[1], r[3], ALU.mult))
                TTp(r[4], r[0], r[3], ALU.mult).then_inc(s5_arg, 1)
                dve.wait_ge(s5_arg, 1)
                step(V.tensor_copy(s5r[:, 0, :], r[5]))
                step(TTp(r[16], r[5], s5r[:, 0, :], ALU.subtract))
                step(TS(r[9], r[5], c_all, None, ALU.mult))
                step(V.tensor_copy(s5r[:, 1, :], r[9]))
                own.do(V.tensor_copy(r[7], s5r[:, 1, :]))
                own.sync()
                step(STT(r[17], s5r[:, 0, :], c_hi, r[7], ALU.mult, ALU.subtract))
                step(STT(r[17], r[16], c_hi, r[17], ALU.mult, ALU.add))
                step(STT(r[8], r[5], c_lo, r[17], ALU.mult, ALU.add))
                step(TS(r[18], r[7], ROUND, ROUND, ALU.add, ALU.subtract))
                step(TTp(r[18], r[7], r[18], ALU.subtract))
                step(TTp(r[18], r[18], r[8], ALU.add))
                step(TS(r[19], r[18], ROUND, ROUND, ALU.add, ALU.subtract))
                TTp(r[12], r[18], r[19], ALU.subtract).then_inc(s5_arg, 1)

            def s5_factor():
                r = [s5p[:, k, :] for k in range(24)]
                TTp, TS = V.tensor_tensor, V.tensor_scalar
                dve.wait_ge(s5_exp, 2)
                dve.wait_ge(s5_trig, 2)
                own.do(TTp(r[16], r[6], r[15], ALU.mult))
                own.do(TTp(r[17], r[6], r[14], ALU.mult))
                own.do(TTp(r[18], r[0], r[0], ALU.mult))
                own.do(TTp(r[19], r[1], r[1], ALU.mult))
                own.sync()
                own.do(TS(r[16], r[16], 1.0, None, ALU.subtract))
                own.do(TTp(r[18], r[18], r[19], ALU.add))
                own.sync()
                own.do(V.reciprocal(r[19], r[18]))
                own.do(TTp(r[20], r[16], r[0], ALU.mult))
                own.do(TTp(r[21], r[17], r[1], ALU.mult))
                own.do(TTp(r[22], r[17], r[0], ALU.mult))
                own.do(TTp(r[23], r[16], r[1], ALU.mult))
                own.sync()
                own.do(TTp(r[20], r[20], r[21], ALU.add))
                own.do(TTp(r[22], r[22], r[23], ALU.subtract))
                own.sync()
                own.do(TTp(r[20], r[20], r[19], ALU.mult))
                own.do(TTp(r[22], r[22], r[19], ALU.mult))
                own.sync()

            def s5_scale_B():
                TTp = V.tensor_tensor
                dve.wait_ge(B_in, 16)

                def b(k):
                    return s5b[:, k, :].rearrange("p (a c) -> p a c", a=S5_PAIRS)

                def coef(k):
                    return s5p[:, k, :].unsqueeze(2).to_broadcast([P, S5_PAIRS, 32])

                own.do(TTp(b(2), b(0), coef(20), ALU.mult))
                own.do(TTp(b(4), b(1), coef(22), ALU.mult))
                own.do(TTp(b(3), b(1), coef(20), ALU.mult))
                own.do(TTp(b(5), b(0), coef(22), ALU.mult))
                own.sync()
                TTp(b(2), b(2), b(4), ALU.subtract).then_inc(B_ready, 1)
                TTp(b(3), b(3), b(5), ALU.add).then_inc(B_ready, 1)

            def phase(i, p):
                hi_s, lo_s = s5p[:, 7, bass.ds(i * 4 + p, 1)], s5p[:, 8, bass.ds(i * 4 + p, 1)]
                a, b = ph[:, 0, :], ph[:, 1, :]
                if not (isinstance(i, int) and i == 0 and p == 0):
                    dve.wait_ge(phase_ready, i * 4 + p)
                step(V.tensor_scalar(a, tvec[:, :], hi_s, None, ALU.mult))
                step(V.tensor_scalar(b, a, ROUND, ROUND, ALU.add, ALU.subtract))
                step(V.tensor_tensor(a, a, b, ALU.subtract))
                step(V.scalar_tensor_tensor(a, tvec[:, :], lo_s, a, ALU.mult, ALU.add))
                step(V.tensor_scalar(b, a, ROUND, ROUND, ALU.add, ALU.subtract))
                V.tensor_tensor(cosT[:, p, :], a, b, ALU.subtract).then_inc(phase_ready, 1)

            Z0, S0 = 2, 5
            zf = flat[:, Z0 * 512:Z0 * 512 + NZ]

            def evac_qk(i):
                dve.wait_ge(q_hi, i * 2 + 1)
                V.scalar_tensor_tensor(qklo[:, 0, :], ps[:, 0, :], 0.125, qkhi[:, 0, :], ALU.mult,
                                       ALU.subtract).then_inc(qk_ready, 1)
                dve.wait_ge(q_hi, i * 2 + 2)
                V.tensor_tensor(qklo[:, 1, :], ps[:, 1, :], qkhi[:, 1, :], ALU.subtract).then_inc(qk_ready, 1)

            def values_lo(i):
                dve.wait_ge(v_hi, i + 1)
                V.tensor_tensor(vlo[:, :, :], ps[:, 0, :].rearrange("p (t c) -> p t c", t=TT), vhi[:, :, :],
                                ALU.subtract).then_inc(v_ready, 1)

            def mixer(i, last=False):
                def pair(p):
                    cos2 = cosT[:, p, :].unsqueeze(1).to_broadcast([P, 2, T])
                    sin2 = sinT[:, p, :].unsqueeze(1).to_broadcast([P, 2, T])
                    dve.wait_ge(bu_done, i * 4 + (p + 1))
                    dve.wait_ge(table_ready, i * 4 + (p + 1))
                    own.do(V.tensor_tensor(rin[:, :, :], ps[:, S0:S0 + 2, :], cos2, ALU.mult))
                    V.tensor_tensor(rin2[:, :, :], ps[:, S0:S0 + 2, :], sin2, ALU.mult).then_inc(bu_used, 1)
                    dve.wait_ge(bu_used, i * 4 + (p + 1))
                    own.do(V.tensor_tensor(rin[:, 0, :], rin[:, 0, :], rin2[:, 1, :], ALU.subtract))
                    own.do(V.tensor_tensor(rin[:, 1, :], rin[:, 1, :], rin2[:, 0, :], ALU.add))
                    own.sync()
                    if p >= 1:
                        dve.wait_ge(z5_used, i * 4 + p)
                    decay = s5p[:, 6, bass.ds(i * 4 + p, 1)].to_broadcast([P, T])
                    own.do(V.tensor_tensor_scan(zst[:, 0, :], decay, rin[:, 0, :], 0.0, ALU.mult, ALU.add))
                    V.tensor_tensor_scan(zst[:, 1, :], decay, rin[:, 1, :], 0.0, ALU.mult, ALU.add).then_inc(z5_done, 1)

                def softplus(hh):
                    dve.wait_ge(l_done, i * 2 + (hh + 1))
                    V.scalar_tensor_tensor(att[:, :], zf, 0.0, att[:, :], ALU.max, ALU.add).then_inc(sp_done, 1)

                def fail_lo(hh):
                    dve.wait_ge(l_hi, i * 2 + (hh + 1))
                    V.tensor_tensor(atlo[:, :], att[:, :], athi[:, :], ALU.subtract).then_inc(l_ready, 1)

                def w_lo(hh):
                    dve.wait_ge(w_hi, i * 2 + (hh + 1))
                    V.tensor_tensor(atlo[:, :], att[:, :], athi[:, :], ALU.subtract).then_inc(w_ready, 1)

                pair(0)
                softplus(0)
                fail_lo(0)
                pair(1)
                w_lo(0)
                phase(i, 3)
                pair(2)
                if not last:
                    phase(i + 1, 0)
                softplus(1)
                if not last:
                    evac_qk(i + 1)
                fail_lo(1)
                pair(3)
                if not last:
                    phase(i + 1, 1)
                w_lo(1)
                if not last:
                    values_lo(i + 1)
                dve.wait_ge(y5_done, i * 4 + 4)
                V.scalar_tensor_tensor(ys[:, i, :], uch[:, :], vecs[:, bass.ds(i + VEC["D_skip"], 1)],
                                       ps[:, 7, :], ALU.mult, ALU.add).then_inc(ys_done, 1)
                if not last:
                    phase(i + 1, 2)

            def merge():
                n = U_MERGE
                for c in range(2 * HC):
                    dve.wait_ge(ye_hi, c + 1)
                    dst, src, hi = ((ylo, ys, yhi), (alo, ya, ahi))[c // HC]
                    V.tensor_tensor(dst[:, c % HC, :], src[:, c % HC, :], hi[:, c % HC, :], ALU.subtract).then_inc(y_ready, 1)
                split_static(n + 3)
                for m in range(HC):
                    dve.wait_ge(sig_evac, 4 + m + 1)
                    V.tensor_tensor(ys[:, m, :], ys[:, m, :], glu[:, m % 2, :], ALU.mult).then_inc(y2_mult, 1)
                split_static(n + 4)
                for m in range(HC):
                    dve.wait_ge(ye_hi, 2 * HC + m + 1)
                    V.tensor_tensor(ylo[:, m, :], ys[:, m, :], yhi[:, m, :], ALU.subtract).then_inc(y_ready, 1)
                split_static(n + 5)
                split_static(n + 6)

                def up(unit, m0, bank):
                    for m in range(m0, m0 + 2):
                        b = bank + 2 * (m - m0)
                        for br in range(2):
                            dve.wait_ge(block_done, DONE[unit] + 2 * (m - m0) + br + 1)
                            g = gate[:, br, m % 4, :]
                            V.tensor_tensor(g, ps[:, b + br, :], g, ALU.mult).then_inc(up_evac, 1)
                        dve.wait_ge(up_evac, 2 * m + 2)
                        if m >= 2:
                            dve.wait_ge(mg_ready, m - 1)
                        V.tensor_tensor(mg[:, m % 2, :], gate[:, 0, m % 4, :], gate[:, 1, m % 4, :],
                                        ALU.add).then_inc(mg_done, 1)
                        if m > m0:
                            for mm in (m - 1, m):
                                dve.wait_ge(mg_hi, mm + 1)
                                V.tensor_tensor(mlo[:, mm, :], mg[:, mm % 2, :], mhi[:, mm, :],
                                                ALU.subtract).then_inc(mg_ready, 1)
                    split_static(unit + 2)

                up(n + 5, 0, 0)
                up(n + 6, 2, 4)
                for k in range(4):
                    split_static(n + 9 + k)
                up(n + 11, 4, 4)
                up(n + 12, 6, 0)
                residual(U_OUT, (4, 6, 0, 2))

            def residual(n, banks, between=None):
                for b in range(4):
                    for k in range(2):
                        dve.wait_ge(block_done, DONE[n + b] + k + 1)
                        m = 2 * b + k
                        V.tensor_tensor(h[:, m, :], ps[:, banks[b] + k, :], h[:, m, :], ALU.add).then_inc(h_added, 1)
                    if b < 3:
                        split_static(n + b + 2)
                    if b == 1 and between is not None:
                        between()

            def ff(i, last=False):
                for q in range(2):
                    n = i * 8 + (U_FF + 4 * q)
                    s = (U_FF + 4 * q) % 2
                    base = i * 24 + (DONE[U_FF] + 12 * q)
                    a, b = (0, 4) if q == 0 else (4, 0)
                    hid = i * 8 + 4 * q

                    def square(m):
                        dve.wait_ge(rl_done, hid + (m + 1))
                        if m >= 2:
                            dve.wait_ge(hd_ready, hid + (m - 1))
                        V.tensor_tensor(hd[:, m % 2, :], rl[:, m % 2, :], rl[:, m % 2, :], ALU.mult).then_inc(hd_done, 1)

                    def lo(m):
                        dve.wait_ge(hd_hi, hid + (m + 1))
                        V.tensor_tensor(hdlo[:, m, :], hd[:, m % 2, :], hdhi[:, m, :], ALU.subtract).then_inc(hd_ready, 1)

                    def add(m, bank):
                        dve.wait_ge(block_done, base + (5 + m))
                        V.tensor_tensor(h[:, m, :], ps[:, bank, :], h[:, m, :], ALU.add).then_inc(h_added, 1)

                    square(0)
                    square(1)
                    lo(0)
                    lo(1)
                    split_lo(n + 2, s)
                    square(2)
                    square(3)
                    lo(2)
                    lo(3)
                    dve.wait_ge(hd_ready, hid + 4)
                    split_lo(n + 3, 1 - s)
                    for m in range(4):
                        add(m, b + m)
                    if last and q == 1:
                        for c in range(1, 4):
                            norm_chunk_sum(dve, V, BOTH, c)
                    split_lo(n + 4, s)
                    for m in range(4):
                        add(4 + m, a + m)
                        if last and q == 1 and m:
                            norm_chunk_sum(dve, V, BOTH, 3 + m)
                    if last and q == 1:
                        norm_chunk_sum(dve, V, BOTH, DC - 1)
                    if not (last and q == 1):
                        split_lo(n + 5, 1 - s)

            def gla_prepare():
                for hh in range(GLA_H):
                    dve.wait_ge(la_abs, hh + 1)
                    own.do(V.tensor_scalar(gr[:, hh, :], ps[:, 4 + hh, :], vec("gla_b_a", hh), 0.0, ALU.add, ALU.min))
                own.sync()
                split_static(U_ALR + 2)
                for hh in range(GLA_H):
                    dve.wait_ge(la_ln, min(hh + 1, 2))
                    step(V.tensor_tensor(gr[:, hh, :], gr[:, hh, :], cum[:, hh, :], ALU.subtract))
                    V.tensor_tensor_scan(cum[:, hh, :], reset[:, :], gr[:, hh, :], 0.0, ALU.mult, ALU.add).then_inc(cum_done, 1)
                    if hh == 0:
                        dve.wait_ge(cum_done, 1)
                        gla_decay_in(0)
                    if hh == 2:
                        gla_scale(0)
                        split_static(U_GLA + 2)

            def gla_decay_in(i):
                c3 = cum[:, i, :].rearrange("p (n c) -> p n c", c=GLA_C)
                V.tensor_tensor(kd[:, :].rearrange("p (n c) -> p n c", c=GLA_C),
                                c3[:, :, GLA_C - 1:GLA_C].to_broadcast([P, GLA_N, GLA_C]), c3,
                                ALU.subtract).then_inc(dec_in, 1)

            def gla_scale(i):
                dve.wait_ge(dec_done, i + 1)
                dve.wait_ge(block_done, i * 4 + (DONE[U_GLA] + 2))
                V.scalar_tensor_tensor(qin[:, :], ps[:, 0, :], float(P) ** -0.5, eq[:, :], ALU.mult,
                                       ALU.mult).then_inc(in_done, 1)
                V.tensor_tensor(kin[:, :], ps[:, 1, :], ek[:, :], ALU.mult).then_inc(in_done, 1)
                V.tensor_tensor(kdec[:, :], ps[:, 1, :], kd[:, :], ALU.mult).then_inc(in_done, 1)
                dve.wait_ge(in_hi, i * 2 + 1)
                V.tensor_tensor(qzlo[:, :, 0:4:3, :], qin[:, :].rearrange("p (t a b) -> p t a b", t=TT, a=2),
                                qzhi[:, :, 0:4:3, :], ALU.subtract).then_inc(in_ready, 1)
                dve.wait_ge(in_hi, i * 2 + 2)
                V.tensor_tensor(kilo[:, :], kin[:, :], kihi[:, :], ALU.subtract).then_inc(in_ready, 1)

            def gla_head(i, last=False):
                dve.wait_ge(kd_hi, i + 1)
                V.tensor_tensor(kdlo[:, :], ps[:, 4, :], kdhi[:, :], ALU.subtract).then_inc(kd_ready, 1)
                dve.wait_ge(gv_hi, i + 1)
                V.tensor_tensor(gvlo[:, :, :], flat[:, 1024:2048].rearrange("p (t c) -> p t c", t=TT), gvhi[:, :, :],
                                ALU.subtract).then_inc(gv_ready, 1)
                dve.wait_ge(ai_mm, i + 1)
                V.tensor_copy(biases[:, 5:6], ones[:, 0:1])
                V.copy_predicated(ai[:, :, :], samechunk[:, :].bitcast(U32).unsqueeze(1).to_broadcast([P, TT, P]),
                                  ps[:, 5, :].rearrange("p (t c) -> p t c", t=TT)).then_inc(ai_done, 1)
                dve.wait_ge(ai_hi, i + 1)
                V.tensor_tensor(ailo[:, :, :], ai[:, :, :], aihi[:, :, :], ALU.subtract).then_inc(ai_ready, 1)
                NS = GLA_N - 1
                for c in range(NS):
                    dve.wait_ge(kv_mm, i * NS + min(c + 3 if c in KV_FIRST else c + 1, NS))
                    kv = kv_sums(c)
                    if c == 0:
                        V.tensor_copy(st[:, 0, :], kv).then_inc(st_done, 1)
                    else:
                        at = c * GLA_C + GLA_C - 1
                        V.scalar_tensor_tensor(st[:, c % 2, :], st[:, (c - 1) % 2, :], eq[:, at:at + 1], kv, ALU.mult,
                                               ALU.add).then_inc(st_done, 1)
                    dve.wait_ge(st_hi, i * NS + (c + 1))
                    V.tensor_tensor(stlo[:, c + 1, :], st[:, c % 2, :], sthi[:, c + 1, :], ALU.subtract).then_inc(st_ready, 1)
                    dve.wait_ge(st_ready, i * NS + (c + 1))
                split_lo(i * 2 + (U_GLA + 3), (U_GLA + 3) % 2)
                if not last:
                    split_lo(i * 2 + (U_GLA + 4), U_GLA % 2)
                    gla_decay_in(i + 1)
                dve.wait_ge(gss_done, i + 1)
                step(V.tensor_scalar(g_half[:, :], gss[:, :], 0.5 / 256, 0.5 * EPS, ALU.mult, ALU.add))
                rsqrt(g_half[:, :], g_y[:, :], g_t[:, :], g_y[:, :])
                for t in range(TT):
                    r = V.tensor_scalar(otm[:, t, :], ps[:, 6 + t // 2, (t % 2) * 256:(t % 2) * 256 + 256], g_y[:, t:t + 1],
                                        None, ALU.mult)
                    if t == TT - 1:
                        r.then_inc(otm_done, 1)
                    else:
                        own.do(r)
                if not last:
                    gla_scale(i + 1)
                else:
                    split_static(U_GLAG + 2)
                dve.wait_ge(ot_done, i + 1)
                for dv in range(2):
                    V.tensor_scalar(og[:, i * 2 + dv, :], ps[:, 6 + dv, :], vec("gla_o_norm", dv), None,
                                    ALU.mult).then_inc(go_done, 1)

            def gate_products(turn, chunks, ready):
                for c in chunks:
                    dve.wait_ge(ready, c + 1)
                    V.tensor_tensor(og[:, c, :], og[:, c, :], gr[:, c, :], ALU.mult).then_inc(prod_done, 1)

            def gated_lo_half(turn, chunks):
                for c in chunks:
                    dve.wait_ge(gated_hi, 8 * turn + c + 1)
                    V.tensor_tensor(ulo[:, c, :], og[:, c, :], uhi[:, c, :], ALU.subtract).then_inc(gated, 1)

            def ple_split(layer):
                for k in range(2):
                    dve.wait_ge(pe_hi, 2 * layer + k + 1)
                    V.tensor_tensor(pelo[:, k, :], pe_in[:, k, :], pehi[:, k, :], ALU.subtract).then_inc(pe_ready, 1)

            def ple_gate(layer, n):
                for b in range(4):
                    for k in range(2):
                        m = 2 * b + k
                        dve.wait_ge(sg_done, 8 * layer + m + 1)
                        V.tensor_tensor(sg[:, m % 2, :], sg[:, m % 2, :], pp[:, m, :], ALU.mult).then_inc(sgp, 1)
                        dve.wait_ge(sgp, 8 * layer + m + 1)
                        V.tensor_tensor(h[:, m, :], h[:, m, :], sg[:, m % 2, :], ALU.add).then_inc(h_added, 1)
                    if b < 3:
                        split_static(n + b + 2)

            tf = flat[:, 5 * 512:5 * 512 + NZ]

            def fox_prepare():
                own.do(V.tensor_scalar(gq8[:, :], vec("fox_q_norm"), 0.125, None, ALU.mult))
                dve.wait_ge(f_evac, 1)
                step(V.tensor_scalar(fl[:, 2, :], fl[:, 0, :], 0.0, None, ALU.min))
                split_static(U_F + 2)
                dve.wait_ge(f_ln_done, 1)
                step(V.tensor_tensor(fl[:, 0, :], fl[:, 1, :], fl[:, 2, :], ALU.subtract))
                V.tensor_tensor_scan(fl[:, 2, :], biases[0:16, 1:2].to_broadcast([16, T]), fl[:, 0, :], 0.0, ALU.mult,
                                     ALU.add).then_inc(c_ready, 1)

            def fox_bias_lo():
                dve.wait_ge(f_exp, 1)
                step(V.tensor_tensor(nclo[:, :], fl[:, 2, :], nchi[:, :], ALU.subtract))

            def fox_qk_norm(i):
                dve.wait_ge(fln_done, i + 1)
                own.do(V.tensor_scalar(f_half[:, :, :], ps[:, Z0:Z0 + 2, :], 0.5 / 64, 0.5 * EPS, ALU.mult, ALU.add))
                dve.wait_ge(fy_done, i + 1)
                newton(f_y[:, :, :], f_half[:, :, :], f_t[:, :, :], f_y[:, :, :])
                own.do(V.scalar_tensor_tensor(qk[:, 0, :], qk[:, 0, :], gq8[:, :], f_y[:, 0, :], ALU.mult, ALU.mult))
                V.scalar_tensor_tensor(qk[:, 1, :], qk[:, 1, :], vec("fox_k_norm"), f_y[:, 1, :], ALU.mult,
                                       ALU.mult).then_inc(qk_n, 1)

            def fox_qk_lo(i):
                dve.wait_ge(fq_hi, i + 1)
                V.tensor_tensor(fqlo[:, :, :], qk[:, :, :], fqhi[:, :, :], ALU.subtract).then_inc(fq_ready, 1)

            def fox_bias(i, hh):
                row = ident[0:16, bass.ds(i * 2 + hh, 1)]
                own.do(V.tensor_scalar(cmhi[:, :], nchi[:, :], row, None, ALU.mult))
                V.tensor_scalar(cmlo[:, :], nclo[:, :], row, None, ALU.mult).then_inc(cm_ready, 1)

            def fox_values_lo(i):
                dve.wait_ge(fv_hi, i + 1)
                V.tensor_tensor(fvlo[:, :, :], ps[:, 7, :].rearrange("p (t c) -> p t c", t=TT), fvhi[:, :, :],
                                ALU.subtract).then_inc(fv_ready, 1)

            def fox(i, last=False):
                def row_max(hh):
                    dve.wait_ge(fz_done, i * 2 + (hh + 1))
                    for group in QB_GROUPS:
                        for qb in group:
                            r = V.tensor_reduce(nmax[:, QB_COL[qb]:QB_COL[qb] + 1], zf[:, QB_AT[qb]:QB_AT[qb] + (qb + 1) * P],
                                                AX.X, ALU.max, negate=True)
                            if qb == group[-1]:
                                r.then_inc(max_done, 1)
                            else:
                                own.do(r)

                def normalise(hh):
                    for g, group in enumerate(QB_GROUPS):
                        dve.wait_ge(exp_done, i * 6 + (hh * 3 + g + 1))
                        cols = slice(QB_COL[group[0]], QB_COL[group[-1]] + 1)
                        step(V.reciprocal(rinv[:, cols], rsum[:, cols]))
                        for qb in group:
                            at = slice(QB_AT[qb], QB_AT[qb] + (qb + 1) * P)
                            r = V.tensor_scalar(pr[:, at], pr[:, at], rinv[:, QB_COL[qb]:QB_COL[qb] + 1], None, ALU.mult)
                            if qb == group[-1]:
                                r.then_inc(p_done, 1)
                            else:
                                own.do(r)

                def probs_lo(hh):
                    dve.wait_ge(pt_hi, i * 2 + (hh + 1))
                    V.tensor_tensor(ptlo[:, :], tf, pthi[:, :], ALU.subtract).then_inc(pt_ready, 1)

                row_max(0)
                fox_bias(i, 1)
                normalise(0)
                probs_lo(0)
                row_max(1)
                normalise(1)
                if last:
                    gate_products(1, range(3), fox_silu)
                probs_lo(1)
                if last:
                    gate_products(1, range(3, DC - 1), fox_silu)
                    gated_lo_half(1, range(DC - 1))
                if not last:
                    fox_bias(i + 1, 0)
                    fox_qk_norm(i + 1)
                    split_lo(i * 2 + (U_FOX + 4), U_FOX % 2)
                    fox_qk_lo(i + 1)
                    fox_values_lo(i + 1)
                    split_lo(i * 2 + (U_FOX + 5), (U_FOX + 1) % 2)

            s5_prepare()
            for c in range(1, DC):
                norm_chunk_sum(dve, V, 0, c)
            dve.wait_ge(first_in, 48)
            norm(0, "norm_mix", [0])
            split_static(1)
            own.do(V.tensor_tensor(g12[:, :], vecs[:, VEC["norm_final"]:VEC["norm_final"] + DC],
                                   vecs[:, VEC["norm_mixer0"]:VEC["norm_mixer0"] + DC], ALU.mult))
            evac_qk(0)
            s5_factor()
            s5_scale_B()
            split_static(2)
            dve.wait_ge(cst_sem, 16 * N_CST)
            for k, dst in enumerate((onesr, keymaskr, querymaskr, trir, negonesr)):
                V.tensor_copy(dst[:, :], cst_in[:, k, :]).then_inc(consts_ready, 1)
            V.tensor_copy(identr[:, :], ident[:, :]).then_inc(consts_ready, 1)
            dve.wait_ge(BT_done, 1)
            for p in range(3):
                phase(0, p)
            values_lo(0)
            with nc.vector.Fori(0, HC - 1) as i:
                own.enter(i, 36)
                mixer(i)
                own.leave(HC - 1)
            mixer(HC - 1, True)
            merge()
            norm(1, "norm_mlp", [U_OUT + 5])
            with nc.vector.Fori(0, FFB // 2 - 1) as i:
                ff(i)
            ff(FFB // 2 - 1, True)
            norm(BOTH, None, [U_GLA])
            dve.wait_ge(bc_done, BOTH + 2)
            norm_out(BOTH, "norm_final", ps[:, RMS_BANK2, :], h, h_normed)
            step(V.memset(ai[:, :, :], 0.0))
            for q in (qzhi, qzlo):
                for k in range(2):
                    own.do(V.tensor_copy(q[:, 2 * k:2 * k + 2, :, :].rearrange("p t a b -> p (t a b)"),
                                         ai[:, :, :].rearrange("p t c -> p (t c)")))
            own.sync()
            gla_prepare()
            with nc.vector.Fori(0, GLA_H - 1) as i:
                own.enter(i, 15)
                gla_head(i)
                own.leave(GLA_H - 1)
            gla_head(GLA_H - 1, True)
            for k in range(4):
                gate_products(0, range(2 * k, 2 * k + 2), g_evac)
                if 0 < k < 3:
                    split_static(U_GLAG + 2 + k)
            gated_lo_half(0, range(DC))
            split_static(U_GLAG + 5)
            ple_split(0)
            residual(U_GLAO, (0, 2, 0, 2))
            norm(3, "ple_norm0", [U_GLAO + 5])
            split_static(U_PLE0 + 2)
            ple_gate(0, U_PLE0 + 1)
            norm(4, "norm_mixer1", [U_PLE0 + 6])
            fox_prepare()
            fox_qk_norm(0)
            fox_bias_lo()
            fox_bias(0, 0)
            fox_qk_lo(0)
            split_static(U_FOX + 2)
            fox_values_lo(0)
            split_static(U_FOX + 3)
            with nc.vector.Fori(0, FOX_PAIRS - 1) as i:
                own.enter(i, 17)
                fox(i)
                own.leave(FOX_PAIRS - 1)
            fox(FOX_PAIRS - 1, True)
            dve.wait_ge(fo_done, 2 * FOX_PAIRS)
            gate_products(1, range(DC - 1, DC), fox_silu)
            gated_lo_half(1, range(DC - 1, DC))
            residual(U_FOXO, (0, 2, 0, 2), lambda: ple_split(1))
            norm(5, "ple_norm1", [U_FOXO + 5])
            split_static(U_PLE1 + 2)
            ple_gate(1, U_PLE1 + 1)
            norm_out(6, "final_norm", norm_scale(6), pp, out_ready)


def pack_unit(w):
    k = w.shape[0] // P
    return w.reshape(k, P, w.shape[1]).transpose(1, 0, 2).reshape(P, UW)


def weight_units(a):
    def cols(w, c, n=256):
        return pack_unit(w[:, c:c + n])

    def pairs(w, *starts):
        return pack_unit(np.concatenate([w[:, c:c + P] for c in starts], axis=1))

    def padded(w):
        return pack_unit(np.concatenate([w, np.zeros((D, 256 - w.shape[1]), w.dtype)], axis=1))

    w_in, w_gate = a["w_in"][0], a["w_gate"][0]
    up = np.concatenate([a["w_up_ssm"][0], a["w_up_attn"][0]], axis=0)
    ff1, ff2 = a["w_ff1"][0], a["w_ff2"][0]
    gla, fox = a["gla_w_in_2"][0], a["fox_w_in_2"][0]
    for c in range(HC):
        yield pairs(w_in, DH + c * P, 2 * DH + c * P)
        yield pairs(w_in, 3 * DH + c * P, c * P)
    for half in range(2):
        for c in (512 * half, 512 * half + 256):
            yield cols(w_gate, c)
            yield cols(w_gate, D + c)
            if c == 0:
                yield pack_unit(a["w_glu"][0])
        for c in (512 * half, 512 * half + 256):
            yield cols(up, c)
    for c in range(4):
        yield cols(a["w_out"][0], 256 * c)
    for b in range(FFB):
        yield cols(ff1, 512 * b)
        yield cols(ff1, 512 * b + 256)
        yield cols(ff2[512 * b:512 * b + 512], 0, 512)
        yield cols(ff2[512 * b:512 * b + 512], 512, 512)
    yield padded(gla[:, 3072:3088])
    for hh in range(GLA_H):
        yield pairs(gla, hh * P, 512 + hh * P)
        yield cols(gla, 1024 + 256 * hh)
    for c in range(4):
        yield cols(gla, 2048 + 256 * c)
    for c in range(4):
        yield cols(a["gla_w_out_2"][0], 256 * c)
    for layer in range(2):
        if layer == 1:
            yield padded(fox[:, 4096:4112])
            for c in range(FOX_PAIRS):
                yield pairs(fox, c * P, D + c * P)
                yield pairs(fox, 2 * D + c * P, 3 * D + c * P)
            for c in range(4):
                yield cols(a["fox_w_out_2"][0], 256 * c)
        yield pack_unit(a["ple_proj_2"][layer])
        for c in range(4):
            yield cols(a["ple_gate_2"][layer], 256 * c)


def constants():
    p, f = np.arange(P)[:, None], np.arange(P)[None, :]
    t = np.arange(T)[None, :].repeat(P, 0)
    parts = {
        "ident": p == f, "ones": np.ones((P, P)), "keymask": np.where(p >= f, NEG, 0.0),
        "querymask": np.where(f > p, NEG, 0.0), "tri": np.where(p >= f, -1.0, 0.0), "negones": -np.ones((P, P)),
        "headones": p // 64 == f // 64, "samechunk": (p // GLA_C == f // GLA_C) & (f >= p),
        "reset": t % GLA_C != 0, "tvec": t,
    }
    return np.concatenate([np.asarray(parts[n], np.float32) for n in CST], axis=1)


def fm(x):
    return np.ascontiguousarray(x.T.reshape(-1, P, x.shape[0]).transpose(1, 0, 2))


def packed_vectors(a):
    out = np.zeros((P, NVEC), np.float32)

    def put(name, v):
        v = v.reshape(-1, P).T
        out[:, VEC[name]:VEC[name] + v.shape[1]] = v

    put("norm_mix", a["norm_mix"][0])
    put("norm_mlp", a["norm_mlp"][0])
    put("norm_final", a["norm_final"])
    put("norm_mixer0", a["norm_mixer_2"][0])
    put("norm_mixer1", a["norm_mixer_2"][1])
    put("ple_norm0", a["ple_norm_2"][0])
    put("ple_norm1", a["ple_norm_2"][1])
    put("final_norm", a["final_norm_2"])
    put("D_skip", a["D_skip"][0])
    put("b_glu", a["b_glu"][0])
    put("b_gate", a["b_gate"][0])
    put("gla_b_a", a["gla_b_a_2"][0])
    put("gla_o_norm", a["gla_o_norm_2"][0])
    put("fox_q_norm", np.concatenate([a["fox_q_norm_2"][0]] * 2))
    put("fox_k_norm", np.concatenate([a["fox_k_norm_2"][0]] * 2))
    out[0:16, VEC["fox_b_f"]] = a["fox_b_f_2"][0]
    return out


def s5_layout(a):
    def states(x):
        return x.reshape(S5_PAIRS, P).T

    params = [states(a["A_re"][0]), states(a["A_im"][0]), states(np.repeat(a["log_dt"][0], 64))]
    for b in (a["B_re"][0], a["B_im"][0]):
        tile = np.zeros((P, S5_PAIRS, 32), np.float32)
        for g in range(2):
            tile[64 * g:64 * g + 64, :, 16 * g:16 * g + 16] = b[g::2].transpose(1, 0, 2)
        params.append(tile.reshape(P, -1))
    c_tiles = np.zeros((HC, P, 4, 2, P), np.float32)
    for r, c in enumerate((a["C_re"][0], a["C_im"][0])):
        for g in range(32):
            chunk, pair, half = g // 8, (g // 2) % 4, g % 2
            at = 32 * pair + 16 * half
            c_tiles[chunk, 64 * half:64 * half + 64, pair, r, at:at + 16] = c[g].T
    return np.concatenate(params, axis=1), c_tiles.reshape(HC, P, -1)


def kernel(**inputs):
    import concourse.bacc as bacc
    from concourse.bass_utils import run_bass_kernel_spmd

    a = {k: np.asarray(v) for k, v in inputs.items()}
    s5p, cpad = s5_layout(a)
    arrays = {
        "wstream": np.stack(list(weight_units(a))), "xT": fm(a["x"][0]),
        "pT": np.stack([fm(a["p_2"][layer, 0]) for layer in range(2)]), "vecs_d": packed_vectors(a), "cst_d": constants(),
        "s5p_d": s5p, "cpad_d": cpad, "wa2_d": np.ascontiguousarray(a["gla_w_a2_2"][0]),
    }
    nc = bacc.Bacc("TRN2", target_bir_lowering=False, num_devices=1)
    args = [nc.dram_tensor(n, v.shape, mybir.dt.from_np(v.dtype), kind="ExternalInput").ap() for n, v in arrays.items()]
    args.append(nc.dram_tensor("outT", (P, DC, T), F32, kind="ExternalOutput").ap())
    build(nc, *args)
    r = run_bass_kernel_spmd(nc, [arrays], core_ids=[0])
    out = np.asarray(r.results[0]["outT"])
    return np.ascontiguousarray(out.transpose(2, 1, 0).reshape(1, T, D))
```
